# Optimizing a Trainium2 kernel written in Bass

```python
import jax, jax.numpy as jnp
from jax import lax
import numpy as np

D_MODEL = 1024
BATCH = 1
SEQ = 512
DEPTH = 1

N_META = 16
CHUNK = 128
PAD = CHUNK - N_META
RET_HEADS = 4
RET_DK = D_MODEL // RET_HEADS
RET_DV = 2 * RET_DK
SB_HEADS = D_MODEL // 64
SB_DH = 64
D_FF = -(-8 * D_MODEL // (3 * 256)) * 256
ROPE_BASE = 10000.0
NORM_EPS = 1e-6
GN_EPS = 1e-5
PROJ_SPLIT = (
    RET_HEADS * RET_DK,
    RET_HEADS * RET_DK,
    RET_HEADS * RET_DV,
    RET_HEADS * RET_DV,
    SB_HEADS * SB_DH,
    SB_HEADS * SB_DH,
    SB_HEADS * SB_DH,
    D_MODEL,
    D_MODEL,
)
PROJ_WIDTH = sum(PROJ_SPLIT)


def rmsnorm(x, g):
    xf = x.astype(jnp.float32)
    y = xf * lax.rsqrt(jnp.mean(xf * xf, axis=-1, keepdims=True) + NORM_EPS)
    return (y * g.astype(jnp.float32)).astype(x.dtype)

def rotary(x, pos):
    half = x.shape[-1] // 2
    inv = ROPE_BASE ** (-jnp.arange(half, dtype=jnp.float32) / half)
    ang = pos[:, None] * inv[None, :]
    cos, sin = jnp.cos(ang), jnp.sin(ang)
    x1, x2 = x[..., :half], x[..., half:]
    return jnp.concatenate([x1 * cos - x2 * sin, x1 * sin + x2 * cos], axis=-1)

def retention_chunkwise(q, k, v):
    B, H, Lp, dk = q.shape
    dv = v.shape[-1]
    n = Lp // CHUNK
    log_g = jnp.log1p(-(2.0 ** (-5.0 - jnp.arange(H, dtype=jnp.float32))))
    idx = jnp.arange(CHUNK, dtype=jnp.float32)
    diff = idx[:, None] - idx[None, :]
    decay = jnp.where(diff >= 0, jnp.exp(log_g[:, None, None] * jnp.maximum(diff, 0.0)), 0.0)
    zeta = jnp.exp(log_g[:, None] * (CHUNK - 1.0 - idx))[:, :, None]
    xi = jnp.exp(log_g[:, None] * (idx + 1.0))[:, :, None]
    g_chunk = jnp.exp(log_g * CHUNK)[:, None, None]

    qc = q.reshape(B, H, n, CHUNK, dk)
    kc = k.reshape(B, H, n, CHUNK, dk)
    vc = v.reshape(B, H, n, CHUNK, dv)
    scores = jnp.einsum('bhncd,bhnsd->bhncs', qc, kc) * decay[:, None]
    inner = jnp.einsum('bhncs,bhnse->bhnce', scores, vc)

    def step(state, inp):
        q_i, k_i, v_i = inp
        cross = jnp.einsum('bhcd,bhde->bhce', q_i, state) * xi
        state = g_chunk * state + jnp.einsum('bhsd,bhse->bhde', k_i, v_i * zeta)
        return state, cross

    s0 = jnp.zeros((B, H, dk, dv), jnp.float32)
    _, cross = lax.scan(step, s0, (qc.transpose(2, 0, 1, 3, 4), kc.transpose(2, 0, 1, 3, 4), vc.transpose(2, 0, 1, 3, 4)))
    out = inner + cross.transpose(1, 2, 0, 3, 4)
    return out.reshape(B, H, Lp, dv)

def head_groupnorm(y):
    mu = jnp.mean(y, axis=-1, keepdims=True)
    var = jnp.mean(jnp.square(y - mu), axis=-1, keepdims=True)
    return (y - mu) * lax.rsqrt(var + GN_EPS)

def stick_breaking(q, k, v):
    Lp, d = q.shape[2], q.shape[3]
    scale = d ** -0.5
    outs = []
    for i in range(Lp // CHUNK):
        lk = (i + 1) * CHUNK
        q_blk = q[:, :, i * CHUNK:lk]
        k_pre, v_pre = k[:, :, :lk], v[:, :, :lk]
        z = jnp.einsum('bhtd,bhsd->bhts', q_blk, k_pre) * scale
        t_pos = i * CHUNK + jnp.arange(CHUNK)
        s_pos = jnp.arange(lk)
        valid = (s_pos[None, :] < t_pos[:, None]) & (s_pos[None, :] >= PAD)
        log_not = jnp.where(valid, jax.nn.log_sigmoid(-z), 0.0)
        after = lax.cumsum(log_not, axis=3, reverse=True) - log_not
        a = jnp.where(valid, jnp.exp(jax.nn.log_sigmoid(z) + after), 0.0)
        outs.append(jnp.einsum('bhts,bhse->bhte', a, v_pre))
    return jnp.concatenate(outs, axis=2)

def hybrid_mixer(hn, w_in, w_ret_out, w_sb_out, w_out):
    B, L, _ = hn.shape
    dtype = hn.dtype
    proj = hn @ w_in
    rq, rk, rv, rg, sq, sk, sv, ga, gb = jnp.split(proj, list(np.cumsum(PROJ_SPLIT)[:-1]), axis=-1)

    def heads(t, h):
        t = t.reshape(B, L, h, -1).transpose(0, 2, 1, 3).astype(jnp.float32)
        return jnp.pad(t, ((0, 0), (0, 0), (PAD, 0), (0, 0)))

    def merge_heads(t):
        t = t[:, :, PAD:]
        return t.transpose(0, 2, 1, 3).reshape(B, L, -1)

    pos = jnp.arange(L + PAD, dtype=jnp.float32) - PAD
    q_r = rotary(heads(rq, RET_HEADS), pos) * (RET_DK ** -0.5)
    k_r = rotary(heads(rk, RET_HEADS), pos)
    y_ret = head_groupnorm(retention_chunkwise(q_r, k_r, heads(rv, RET_HEADS)))
    y_ret = (jax.nn.silu(rg.astype(jnp.float32)) * merge_heads(y_ret)).astype(dtype) @ w_ret_out
    y_sb = merge_heads(stick_breaking(heads(sq, SB_HEADS), heads(sk, SB_HEADS), heads(sv, SB_HEADS)))
    y_sb = y_sb.astype(dtype) @ w_sb_out
    merged = jax.nn.sigmoid(ga) * y_ret + jax.nn.sigmoid(gb) * y_sb
    return merged @ w_out

def swiglu(hn, w_ffn_in, w_ffn_out):
    a, b = jnp.split(hn @ w_ffn_in, 2, axis=-1)
    return (jax.nn.silu(a) * b) @ w_ffn_out

def first_inputs(seed: int = 0) -> dict:
    key = jax.random.key(seed)
    ks = jax.random.split(key, 12)
    f32 = jnp.float32
    nrm = lambda k, shape, fan: jax.random.normal(k, shape, f32) * (fan ** -0.5)
    gain = lambda k: 1.0 + 0.02 * jax.random.normal(k, (DEPTH, D_MODEL), f32)
    return {
        "x": jax.random.normal(ks[0], (BATCH, SEQ, D_MODEL), f32),
        "meta_tokens": jax.random.normal(ks[1], (N_META, D_MODEL), f32),
        "w_in": nrm(ks[2], (DEPTH, D_MODEL, PROJ_WIDTH), D_MODEL),
        "w_ret_out": nrm(ks[3], (DEPTH, RET_HEADS * RET_DV, D_MODEL), RET_HEADS * RET_DV),
        "w_sb_out": nrm(ks[4], (DEPTH, SB_HEADS * SB_DH, D_MODEL), SB_HEADS * SB_DH),
        "w_out": nrm(ks[5], (DEPTH, D_MODEL, D_MODEL), D_MODEL),
        "w_ffn_in": nrm(ks[6], (DEPTH, D_MODEL, 2 * D_FF), D_MODEL),
        "w_ffn_out": nrm(ks[7], (DEPTH, D_FF, D_MODEL), D_FF),
        "norm_mix_pre": gain(ks[8]),
        "norm_mix_post": gain(ks[9]),
        "norm_ffn_pre": gain(ks[10]),
        "norm_ffn_post": gain(ks[11]),
    }

def first_block(x, meta_tokens, w_in, w_ret_out, w_sb_out, w_out, w_ffn_in, w_ffn_out,
              norm_mix_pre, norm_mix_post, norm_ffn_pre, norm_ffn_post):
    B = x.shape[0]
    meta = jnp.broadcast_to(meta_tokens.astype(x.dtype)[None], (B, N_META, x.shape[-1]))
    h = jnp.concatenate([meta, x], axis=1)
    for l in range(DEPTH):
        mix = hybrid_mixer(rmsnorm(h, norm_mix_pre[l]), w_in[l], w_ret_out[l], w_sb_out[l], w_out[l])
        h = h + rmsnorm(mix, norm_mix_post[l])
        ff = swiglu(rmsnorm(h, norm_ffn_pre[l]), w_ffn_in[l], w_ffn_out[l])
        h = h + rmsnorm(ff, norm_ffn_post[l])
    return h[:, N_META:]


HEAD_DIM = 64
MIX_WIDTH = D_MODEL
W_A = MIX_WIDTH // 2
W_B = MIX_WIDTH - W_A
N_HEADS_A = W_A // HEAD_DIM
N_HEADS_B = W_B // HEAD_DIM
CONV_A_WIDTH = 3
CONV_B_WIDTH = 31
IN_PROJ_WIDTH = 3 * W_A + 2 * W_B
D_FF_2 = ((8 * D_MODEL // 3 + 255) // 256) * 256
RMS_EPS = 1e-6
LN_EPS = 1e-5


def rms_norm(x, g):
    xf = x.astype(jnp.float32)
    y = xf * lax.rsqrt(jnp.mean(xf * xf, axis=-1, keepdims=True) + RMS_EPS)
    return (y * g.astype(jnp.float32)).astype(x.dtype)

def layer_norm(x, g, b):
    xf = x.astype(jnp.float32)
    mu = jnp.mean(xf, axis=-1, keepdims=True)
    var = jnp.mean(jnp.square(xf - mu), axis=-1, keepdims=True)
    y = (xf - mu) * lax.rsqrt(var + LN_EPS)
    return (y * g.astype(jnp.float32) + b.astype(jnp.float32)).astype(x.dtype)

def causal_depthwise_conv(u, w):
    k = w.shape[0]
    return lax.conv_general_dilated(
        u, w[:, None, :].astype(u.dtype),
        window_strides=(1,), padding=[(k - 1, 0)],
        dimension_numbers=("NWC", "WIO", "NWC"),
        feature_group_count=u.shape[-1])

def mixer(xn, w_in, conv_a_w, conv_b_w, conv_b_bias, ln_b_gain, ln_b_bias, w_out):
    h = jnp.einsum("btd,de->bte", xn, w_in)
    b_gate, c_gate, h_a, glu_val, glu_gate = jnp.split(
        h, [W_A, 2 * W_A, 3 * W_A, 3 * W_A + W_B], axis=-1)
    y_a = b_gate * causal_depthwise_conv(c_gate * h_a, conv_a_w)
    g = glu_val * jax.nn.sigmoid(glu_gate)
    z = causal_depthwise_conv(g, conv_b_w) + conv_b_bias.astype(g.dtype)
    y_b = jax.nn.silu(layer_norm(z, ln_b_gain, ln_b_bias))
    y = jnp.concatenate([y_a, y_b], axis=-1)
    return jnp.einsum("bte,ed->btd", y, w_out)

def swiglu_2(xn, w_gate, w_up, w_down):
    a = jnp.einsum("btd,df->btf", xn, w_gate)
    u = jnp.einsum("btd,df->btf", xn, w_up)
    return jnp.einsum("btf,fd->btd", jax.nn.silu(a) * u, w_down)

def second_inputs(seed: int = 0) -> dict:
    key = jax.random.key(seed)
    ks = jax.random.split(key, 20)
    f32 = jnp.float32

    def nrm(k, shape, scale):
        return jax.random.normal(k, shape, f32) * scale

    def gain(k, n):
        return jnp.ones((DEPTH, n), f32) + 0.05 * jax.random.normal(k, (DEPTH, n), f32)

    return {
        "x": jax.random.normal(ks[0], (BATCH, SEQ, D_MODEL), f32),
        "meta_tokens": nrm(ks[1], (N_META, D_MODEL), 1.0),
        "pre_mix_norm": gain(ks[2], D_MODEL),
        "w_in": nrm(ks[3], (DEPTH, D_MODEL, IN_PROJ_WIDTH), D_MODEL ** -0.5),
        "conv_a_w": nrm(ks[4], (DEPTH, CONV_A_WIDTH, W_A), CONV_A_WIDTH ** -0.5),
        "conv_b_w": nrm(ks[5], (DEPTH, CONV_B_WIDTH, W_B), CONV_B_WIDTH ** -0.5),
        "conv_b_bias": nrm(ks[6], (DEPTH, W_B), 0.02),
        "ln_b_gain": gain(ks[7], W_B),
        "ln_b_bias": nrm(ks[8], (DEPTH, W_B), 0.02),
        "w_out": nrm(ks[9], (DEPTH, MIX_WIDTH, D_MODEL), MIX_WIDTH ** -0.5),
        "post_mix_norm": gain(ks[10], D_MODEL),
        "pre_ffn_norm": gain(ks[11], D_MODEL),
        "w_gate": nrm(ks[12], (DEPTH, D_MODEL, D_FF_2), D_MODEL ** -0.5),
        "w_up": nrm(ks[13], (DEPTH, D_MODEL, D_FF_2), D_MODEL ** -0.5),
        "w_down": nrm(ks[14], (DEPTH, D_FF_2, D_MODEL), D_FF_2 ** -0.5),
        "post_ffn_norm": gain(ks[15], D_MODEL),
    }

def second_block(x, meta_tokens, pre_mix_norm, w_in, conv_a_w, conv_b_w, conv_b_bias,
              ln_b_gain, ln_b_bias, w_out, post_mix_norm, pre_ffn_norm,
              w_gate, w_up, w_down, post_ffn_norm):
    b = x.shape[0]
    meta = jnp.broadcast_to(meta_tokens[None].astype(x.dtype), (b, N_META, x.shape[-1]))
    h = jnp.concatenate([meta, x], axis=1)
    for l in range(DEPTH):
        mix = mixer(rms_norm(h, pre_mix_norm[l]), w_in[l], conv_a_w[l], conv_b_w[l],
                    conv_b_bias[l], ln_b_gain[l], ln_b_bias[l], w_out[l])
        h = h + rms_norm(mix, post_mix_norm[l])
        ff = swiglu_2(rms_norm(h, pre_ffn_norm[l]), w_gate[l], w_up[l], w_down[l])
        h = h + rms_norm(ff, post_ffn_norm[l])
    return h[:, N_META:, :]


def setup_inputs(seed=0):
    out = dict(first_inputs(seed))
    for name, value in second_inputs(seed + 1).items():
        if name != "x":
            out[name + "_2"] = value
    return out


def reference(
    x, meta_tokens, w_in, w_ret_out, w_sb_out, w_out, w_ffn_in, w_ffn_out, norm_mix_pre,
    norm_mix_post, norm_ffn_pre, norm_ffn_post, meta_tokens_2, pre_mix_norm_2, w_in_2,
    conv_a_w_2, conv_b_w_2, conv_b_bias_2, ln_b_gain_2, ln_b_bias_2, w_out_2, post_mix_norm_2,
    pre_ffn_norm_2, w_gate_2, w_up_2, w_down_2, post_ffn_norm_2,
):
    x = first_block(
        x, meta_tokens, w_in, w_ret_out, w_sb_out, w_out, w_ffn_in, w_ffn_out, norm_mix_pre,
        norm_mix_post, norm_ffn_pre, norm_ffn_post,
    )
    return second_block(
        x, meta_tokens_2, pre_mix_norm_2, w_in_2, conv_a_w_2, conv_b_w_2, conv_b_bias_2,
        ln_b_gain_2, ln_b_bias_2, w_out_2, post_mix_norm_2, pre_ffn_norm_2, w_gate_2, w_up_2,
        w_down_2, post_ffn_norm_2,
    )


_drawn_inputs = setup_inputs


def setup_inputs(seed=0):
    import zlib

    import numpy as np

    out = dict(_drawn_inputs(seed))
    spreads = {}
    factors = {'norm_mix_post': 2.669,
     'norm_ffn_pre': 2.716,
     'norm_ffn_post': 12.965,
     'conv_b_bias_2': 43.416,
     'ln_b_gain_2': 155.24,
     'ln_b_bias_2': 200.0,
     'pre_mix_norm_2': 4.566,
     'post_mix_norm_2': 15.38,
     'pre_ffn_norm_2': 3.675,
     'post_ffn_norm_2': 17.784,
     'meta_tokens_2': 2.678}
    for name, (base, spread) in spreads.items():
        noise = np.random.default_rng([zlib.crc32(name.encode()), seed]).standard_normal(out[name].shape)
        drawn = base * np.exp(spread * noise) if base else spread * noise
        out[name] = __import__('jax').numpy.asarray(drawn.astype(out[name].dtype))
    for name, factor in factors.items():
        out[name] = (out[name] * factor).astype(out[name].dtype)
    return out
```

```python
from contextlib import ExitStack

import numpy as np

import concourse.bass as bass
from concourse import mybir

F32 = mybir.dt.float32
F32R = mybir.dt.float32r
ACT = mybir.ActivationFunctionType
ALU = mybir.AluOpType

P = 128
D = 1024
DT = D // P
SEQ = 512
META = 16
FULL = META + SEQ
HALF = FULL // 2
UNIT = 2048
RET_HEADS, RET_DK, RET_DV = 4, 256, 512
QUADS = 4
SB_DH = 64
D_FF = 2816
FF_PAIRS = D_FF // 256
WA = WB = 512
CT = WA // P
TAPS_A, TAPS_B = 3, 31
NORM_EPS, GN_EPS, LN_EPS = 1e-6, 1e-5, 1e-5
BLOCKS = SEQ // P
KEY_OFF = [0, 512, 896, 1152]
KEY_LEN = [SEQ - P * b for b in range(BLOCKS)]
PACKED = sum(KEY_LEN)
KEY_BANK = [0, 1, 2, 2]
KEY_COL = [0, 0, 0, 256]
PARTS = [(0, 0, 512), (1, 512, 384), (2, 896, 384)]
BLOCKED = -(2.0 ** 100)

STRIPS = {"P": 2, "R": 4, "D": 8}


def plan():
    phases = [
        ("gate_b", "P" * 4),
        ("quads", "PPPD" * QUADS),
        ("gate_a", "P" * 4),
        ("head0", "PPPPPP"),
        ("heads", "PPRRPPPP" * 3),
        ("head_out", "RR"),
        ("w_out", "P" * 4),
        ("ffn0", "PP"),
        ("ffn", "PPDPPD" * 5),
        ("ffn_end", "D"),
        ("conv_b", "PPPP"),
        ("conv_a", "PPPPPP"),
        ("w_out2", "P" * 4),
        ("ffn0_2", "PP"),
        ("ffn_2", "PPDPPD" * 4),
        ("ffn_last_2", "PPDPPD"),
        ("ffn_end_2", "D"),
    ]
    start, u, s = {}, 0, 0
    for name, kinds in phases:
        start[name] = (u, s)
        u += len(kinds)
        s += sum(STRIPS[k] for k in kinds)
    return start, u, s


START, N_UNITS, N_STRIPS = plan()


class Place:

    def __init__(self, phase, i=0, per_u=0, per_s=0):
        assert per_u % 2 == 0 and per_s % 2 == 0
        self.u0, self.s0 = START[phase]
        self.i, self.per_u, self.per_s = i, per_u, per_s

    def unit(self, j):
        return self.u0 + j + self.per_u * self.i

    def ring(self, j):
        return (self.u0 + j) % 2

    def loads(self, j):
        return (self.u0 + j) // 2 + 1 + (self.per_u // 2) * self.i

    def strip(self, j):
        return self.s0 + j + self.per_s * self.i

    def slot(self, j):
        return (self.s0 + j) % 2


class Steps:

    def __init__(self, sem, names):
        self.sem, self.names, self.n = sem, list(names), 0
        self.index = {x: k for k, x in enumerate(self.names)}
        assert len(self.index) == len(self.names)

    def at(self, name, i=0):
        return self.index[name] + 1 + len(self.names) * i

    def step(self, name):
        want = self.names[self.n % len(self.names)]
        assert name == want, (name, want)
        self.n += 1
        return self.sem, 1


def heads_of(names):
    return [f"{x}{j}" for j in range(4) for x in names]


def build(nc, units, xfm, meta2, consts, dec, vecs, out):
    ctx = ExitStack()

    def sb(name, shape, dt=F32, where=ctx):
        return where.enter_context(nc.sbuf_tensor(name, shape, dt))

    def sem(name):
        return ctx.enter_context(nc.semaphore(name))

    X_hi = sb("X_hi", [P, DT, FULL], F32R)
    X_lo = sb("X_lo", [P, DT, FULL], F32R)
    acc = sb("acc", [P, DT, SEQ])
    w_raw = [sb(f"w_raw{n}", [P, UNIT]) for n in range(2)]
    w_hi = [sb(f"w_hi{n}", [P, UNIT], F32R) for n in range(2)]
    w_lo = [sb(f"w_lo{n}", [P, UNIT], F32R) for n in range(2)]
    ones = sb("ones", [P, P])
    vec = sb("vec", [P, VEC_COLS])
    psum = ctx.enter_context(nc.psum_tensor("psum", [P, 8, 512], F32))

    cmat = sb("cmat", [P, N_CMAT, P], F32R)
    ident = sb("ident", [P, P])
    mask_k = sb("mask_k", [P, 2, 4, 32])
    mask_v = sb("mask_v", [P, 2, P])
    rot = sb("rot", [P, 2, FULL])
    mixer = ExitStack()
    gate = sb("gate", [P, DT, SEQ], where=mixer)

    quad = ExitStack()
    Q_hi = sb("Q_hi", [P, 2, SEQ], F32R, quad)
    Q_lo = sb("Q_lo", [P, 2, SEQ], F32R, quad)
    K_hi = sb("K_hi", [P, 2, FULL], F32R, quad)
    K_lo = sb("K_lo", [P, 2, FULL], F32R, quad)
    VY = sb("VY", [P, 2, FULL], F32, quad)
    v_pad = sb("v_pad", [P, 2, 4, 32], F32, quad)
    V_hi = sb("V_hi", [P, BLOCKS, 256], F32R, quad)
    V_lo = sb("V_lo", [P, BLOCKS, 256], F32R, quad)
    KM_hi = sb("KM_hi", [P, 2, P], F32R, quad)
    KM_lo = sb("KM_lo", [P, 2, P], F32R, quad)
    VM = sb("VM", [P, 2, P], F32, quad)
    VM_hi = sb("VM_hi", [P, 2, P], F32R, quad)
    VM_lo = sb("VM_lo", [P, 2, P], F32R, quad)
    sp = sb("sp", [P, PACKED], F32, quad)
    sp_hi = sb("sp_hi", [P, PACKED], F32R, quad)
    sp_lo = sb("sp_lo", [P, PACKED], F32R, quad)
    a_f = sb("a_f", [P, PACKED], F32, quad)
    a_hi = sb("a_hi", [P, PACKED], F32R, quad)
    a_lo = sb("a_lo", [P, PACKED], F32R, quad)
    m_f = sb("m_f", [P, SEQ], F32, quad)
    m_hi = sb("m_hi", [P, SEQ], F32R, quad)
    m_lo = sb("m_lo", [P, SEQ], F32R, quad)
    Y_hi = sb("Y_hi", [P, 2, SEQ], F32R, quad)
    Y_lo = sb("Y_lo", [P, 2, SEQ], F32R, quad)
    gated = sb("gated", [P, SEQ], F32, quad)
    quad.close()

    head = ExitStack()
    RQ_hi = sb("RQ_hi", [P, 2, SEQ], F32R, head)
    RQ_lo = sb("RQ_lo", [P, 2, SEQ], F32R, head)
    RK_hi = sb("RK_hi", [P, 2, FULL], F32R, head)
    RK_lo = sb("RK_lo", [P, 2, FULL], F32R, head)
    RY = sb("RY", [P, 4, FULL], F32, head)
    VZ_hi = sb("VZ_hi", [P, 4, SEQ], F32R, head)
    VZ_lo = sb("VZ_lo", [P, 4, SEQ], F32R, head)
    RVM_hi = sb("RVM_hi", [META, SEQ], F32R, head)
    RVM_lo = sb("RVM_lo", [META, SEQ], F32R, head)
    S_f = sb("S_f", [P, PACKED], F32, head)
    S_hi = sb("S_hi", [P, PACKED], F32R, head)
    S_lo = sb("S_lo", [P, PACKED], F32R, head)
    SM_f = sb("SM_f", [META, SEQ], F32, head)
    SM_hi = sb("SM_hi", [META, SEQ], F32R, head)
    SM_lo = sb("SM_lo", [META, SEQ], F32R, head)
    decay = sb("decay", [P, 2, SEQ], F32, head)
    r_std = sb("r_std", [P, SEQ], F32, head)
    silu_g = sb("silu_g", [P, 4, SEQ], F32, head)
    gated_r = sb("gated_r", [P, SEQ], F32, head)
    head.close()
    mixer.close()

    h = sb("h", [P, DT, FULL])
    std = sb("std", [P, FULL])
    sq = sb("sq", [P, 2, FULL])
    sq_sum = sb("sq_sum", [P, FULL])
    normed = sb("normed", [P, 2, FULL])
    meta2_f = sb("meta2_f", [P, DT, META])
    ffns = ExitStack()
    M_hi = sb("M_hi", [P, 2, 2, SEQ], F32R, ffns)
    M_lo = sb("M_lo", [P, 2, 2, SEQ], F32R, ffns)
    silu_a = sb("silu_a", [P, 2, SEQ], F32, ffns)
    ffns.close()
    conv_sig = sb("conv_sig", [P, 2, FULL])
    glu = sb("glu", [P, CT, TAPS_B - 1 - META + FULL])
    c_in = sb("c_in", [P, 2, FULL])
    u_in = sb("u_in", [P, 2, FULL])
    z = sb("z", [P, CT, SEQ])
    y2_hi = sb("y2_hi", [P, DT, SEQ], F32R)
    y2_lo = sb("y2_lo", [P, DT, SEQ], F32R)

    consts_in = sem("consts_in")
    cmat_ready = sem("cmat_ready")
    w_loaded = [sem("w_loaded0"), sem("w_loaded1")]
    w_hi_ready = sem("w_hi_ready")
    w_lo_ready = sem("w_lo_ready")
    strip_done = sem("strip_done")
    strip_free = sem("strip_free")
    x_loaded = sem("x_loaded")
    decay_loaded = sem("decay_loaded")
    memset_done = sem("memset_done")
    stored = sem("stored")

    sq_done = sem("sq_done")
    sq_added = sem("sq_added")
    sum_done = sem("sum_done")
    std_ready = sem("std_ready")
    norm_scaled = sem("norm_scaled")
    x_hi_ready = sem("x_hi_ready")
    x_lo_ready = sem("x_lo_ready")
    post_done = sem("post_done")

    q_act = Steps(sem("q_act"), ["Q_hi0", "Q_hi1", "K_hi0", "K_hi1", "V_hi0", "V_hi1", "VM_hi",
                                 "m_abs", "m_exp", "m_ln", "m_hi"]
                  + heads_of(["abs0_", "abs1_", "abs2_", "exp", "ln", "sp_hi", "a_part0_", "a_part1_", "a_part2_", "a_hi"])
                  + ["am_exp", "am_hi", "Y_hi"])
    q_dve = Steps(sem("q_dve"), ["KM_hi", "KM_lo", "v_pad0", "v_pad1", "V_lo0", "V_lo1", "VM", "VM_lo",
                                 "m_sp", "m_lo"]
                  + heads_of(["sp0_", "sp1_", "sp2_", "sp_lo", "a_lo", "y"])
                  + ["am_lo", "y_meta0", "y_meta1", "Y_lo"] + [f"merge{m}" for m in range(8)])
    q_pe = Steps(sem("q_pe"), ["V_turned0", "V_turned1", "VM_turned", "m_scores", "m_tri"]
                 + heads_of(["scores", "logs", "y"]) + ["y_meta"])
    r_act = Steps(sem("r_act"), ["RQ_hi0", "RQ_hi1", "RK_hi0", "RK_hi1", "V_hi0", "V_hi1", "V_hi2", "V_hi3",
                                 "VM_hi", "S_hi", "SM_hi", "g_sig0", "g_sig1", "g_sig2", "g_sig3",
                                 "y_sq0", "y_sq1", "y_sq2", "y_sq3", "ln", "std", "z_hi"])
    r_dve = Steps(sem("r_dve"), ["q_cos", "q_sin", "q_r1", "q_r2", "q_lo",
                                 "k_cos", "k_sin", "k_r1", "k_r2", "k_lo",
                                 "V_lo0", "V_lo1", "V_lo2", "V_lo3", "VM_lo",
                                 "S0", "S1", "S2", "S3", "SM", "S_lo", "SM_lo",
                                 "y0", "y1", "y2", "y3", "ys1", "ys2", "ys3",
                                 "yc0", "yc1", "yc2", "yc3", "sqs1", "sqs2", "sqs3",
                                 "zs", "zg", "z_lo"])
    r_pe = Steps(sem("r_pe"), ["V_turned0", "V_turned1", "V_turned2", "V_turned3", "VM_turned", "scores",
                               "y", "mean", "var"])
    r_merge = sem("r_merge")
    m_split_hi = sem("m_split_hi")
    m_split_lo = sem("m_split_lo")
    mix_out = sem("mix_out")
    f_act = Steps(sem("f_act"), ["sig0", "sig1", "M_hi"])
    f_dve = Steps(sem("f_dve"), ["prod", "M_lo"])
    acc_zero = sem("acc_zero")
    f_added = sem("f_added")
    c_act = sem("c_act")
    c_dve = sem("c_dve")
    c_pe = sem("c_pe")
    conv_step = sem("conv_step")

    def ring3(u_hi_or_lo, kind):
        k, c = {"P": (8, 256), "R": (4, 512), "D": (2, 1024)}[kind]
        return u_hi_or_lo[:, :].rearrange("p (k c) -> p k c", k=k, c=c)

    def strip_view(slot, width):
        if width == FULL:
            return psum[:, 2 * slot:2 * slot + 2, 0:HALF]
        return psum[:, 2 * slot, 0:SEQ]

    def wide(ap):
        return ap.rearrange("p (a b) -> p a b", a=2)

    def as_f32(ap):
        return ap.bitcast(F32)

    def g_col(name, k):
        o = VEC[name] + k
        return vec[:, o:o + 1]

    def loop(eng, n, body, peel=0):
        for i in range(peel):
            body(i)
        if peel == n:
            return
        with eng.Fori(peel, n) as i:
            body(i)

    block = ctx.enter_context(nc.Block())

    @block.sync
    def _(sync):
        for dst, src in ((vec[:, :], vecs), (ones[:, :], consts[:, 0:P]),
                         (ident[:, :], consts[:, P:2 * P]),
                         (mask_k[:, :, :, :].rearrange("p a b c -> p (a b c)"), consts[:, 2 * P:4 * P]),
                         (mask_v[:, :, :].rearrange("p a b -> p (a b)"), consts[:, 4 * P:6 * P]),
                         (rot[:, :, :].rearrange("p a b -> p (a b)"), consts[:, 6 * P:6 * P + 2 * FULL]),
                         (w_raw[0][:, 0:N_CMAT * P], consts[:, 6 * P + 2 * FULL:])):
            sync.dma_start(dst, src).then_inc(consts_in, 16)
        sync.dma_start(h[:, :, :].rearrange("p a b -> p (a b)"), xfm).then_inc(x_loaded, 16)
        sync.wait_ge(cmat_ready, 1)
        for u in range(2):
            sync.dma_start(w_raw[u][:, :], units[u, :, :]).then_inc(w_loaded[u], 16)

        def load(u, slot):
            sync.wait_ge(w_hi_ready, u - 1)
            sync.wait_ge(w_lo_ready, u - 1)
            sync.dma_start(w_raw[slot][:, :], units[bass.ds(u, 1), :, :].rearrange("a p c -> (a p) c"))\
                .then_inc(w_loaded[slot], 16)

        def load_decay(n):
            if n > 0:
                sync.wait_ge(r_dve.sem, r_dve.at("SM", n - 1))
            sync.dma_start(decay[:, :, :].rearrange("p a b -> p (a b)"), dec[n, :, :]).then_inc(decay_loaded, 16)

        def loads(first, last):
            n = (last - first) // 2
            if last <= first:
                return

            def body(i):
                for slot in range(2):
                    load(first + 2 * i + slot, (first + slot) % 2)
            loop(sync, n, body)
            if (last - first) % 2:
                load(last - 1, (last - 1) % 2)

        loads(2, START["gate_a"][0] + 2)
        sync.wait_ge(q_dve.sem, q_dve.at("merge7", QUADS - 1))
        load_decay(0)
        loads(START["gate_a"][0] + 2, START["heads"][0] + 2)
        for n in range(1, RET_HEADS):
            load_decay(n)
            loads(START["heads"][0] + 8 * (n - 1) + 2, START["heads"][0] + 8 * n + 2)
        loads(START["head_out"][0] + 2, START["ffn0"][0] - 2)
        sync.wait_ge(m_split_lo, DT)
        sync.dma_start(h[:, :, :].rearrange("p a b -> p (a b)"), xfm).then_inc(x_loaded, 16)
        sync.dma_start(meta2_f[:, :, :].rearrange("p a b -> p (a b)"), meta2).then_inc(x_loaded, 16)
        loads(START["ffn0"][0] - 2, N_UNITS)
        sync.wait_ge(post_done, 4 * DT)
        sync.dma_start(out.rearrange("p (a b) -> p a b", a=DT), h[:, :, META:FULL]).then_inc(stored, 16)
        sync.wait_ge(stored, 16)

    @block.tensor
    def _(pe):
        def mm3(dst, w2, x2, first, last, sig=None):
            nc.tensor.matmul(dst, w2[0], x2[0], start=first, stop=False, skip_group_check=True)
            nc.tensor.matmul(dst, w2[0], x2[1], start=False, stop=False, skip_group_check=True)
            m = nc.tensor.matmul(dst, w2[1], x2[0], start=False, stop=last, skip_group_check=True)
            if sig:
                m.then_inc(*sig)

        def unit(at, j, s, kind, width, x):
            pe.wait_ge(w_lo_ready, at.unit(j) + 1)
            w = [ring3(r[at.ring(j)], kind) for r in (w_hi, w_lo)]
            tiles = {"P": 8, "R": 4, "D": 2}[kind]
            for c in range(STRIPS[kind]):
                slot = at.slot(s + c)
                if not (type(at.strip(s + c)) is int and at.strip(s + c) < 2):
                    pe.wait_ge(strip_free, at.strip(s + c) - 1)
                halves = [(0, HALF), (HALF, FULL)] if width == FULL else [(META, FULL)]
                for k in range(tiles):
                    for n, (a, b) in enumerate(halves):
                        end = k == tiles - 1 and n == len(halves) - 1
                        mm3(psum[:, 2 * slot + n, 0:b - a], [y[:, k, c * P:(c + 1) * P] for y in w], x(k, a, b),
                            k == 0, k == tiles - 1, (strip_done, 1) if end else None)

        def from_x(k, a, b):
            return X_hi[:, k, a:b], X_lo[:, k, a:b]

        def seq_of(hi, lo):
            return lambda k, a, b: (hi[:, k, a - META:b - META], lo[:, k, a - META:b - META])

        def sums(n, width):
            pe.wait_ge(sq_added, DT * (n + 1))
            for hf in range(2):
                w = width // 2
                m = nc.tensor.matmul(psum[:, 6 + hf, 0:w], ones[:, :], sq_sum[:, hf * w:(hf + 1) * w],
                                     start=True, stop=True)
            m.then_inc(sum_done, 1)

        pe.wait_ge(consts_in, 16 * 7)
        sums(0, FULL)
        pe.wait_ge(x_lo_ready, DT)
        def gates(phase):
            def body(i):
                at = Place(phase, i, 2, 4)
                for j in range(2):
                    unit(at, j, 2 * j, "P", SEQ, from_x)
            loop(pe, 2, body, 2 if phase == "gate_b" else 0)

        gates("gate_b")

        def split(hi, lo, *ix):
            return hi[ix], lo[ix]

        def quad_body(i):
            at = Place("quads", i, 4, 14)
            unit(at, 0, 0, "P", SEQ, from_x)
            unit(at, 1, 2, "P", FULL, from_x)
            unit(at, 2, 4, "P", FULL, from_x)
            pe.wait_ge(q_dve.sem, q_dve.at("v_pad1", i))
            pe.wait_ge(strip_free, at.strip(5) + 1)
            if True:
                for n in range(2):
                    for b in (2 * n, 2 * n + 1):
                        for t in range(2):
                            m = nc.tensor.transpose(psum[:, 4 + n, (b % 2) * 256 + t * P:(b % 2) * 256 + (t + 1) * P],
                                                    VY[:, t, META + b * P:META + (b + 1) * P], ident[:, :])
                    m.then_inc(*q_pe.step(f"V_turned{n}"))
                for t in range(2):
                    m = nc.tensor.transpose(psum[:, 6, t * P:(t + 1) * P],
                                            v_pad[:, t, :, :].rearrange("p a b -> p (a b)"), ident[:, :])
                m.then_inc(*q_pe.step("VM_turned"))
            pe.wait_ge(q_act.sem, q_act.at("Q_hi1", i))
            pe.wait_ge(q_dve.sem, q_dve.at("KM_lo", i))
            for t in range(2):
                mm3(psum[:, 7, :], split(KM_hi, KM_lo, slice(None), t, slice(None)),
                    split(Q_hi, Q_lo, slice(None), t, slice(None)), t == 0, False,
                    q_pe.step("m_scores") if t == 1 else None)
            pe.wait_ge(q_dve.sem, q_dve.at("m_lo", i))
            nc.tensor.matmul(psum[:, 7, :], cmat[:, C_TRI_META, :], m_hi[:, :], start=False, stop=False,
                             skip_group_check=True)
            nc.tensor.matmul(psum[:, 7, :], cmat[:, C_TRI_META, :], m_lo[:, :], start=False, stop=False,
                             skip_group_check=True).then_inc(*q_pe.step("m_tri"))
            pe.wait_ge(q_act.sem, q_act.at("VM_hi", i))
            pe.wait_ge(q_dve.sem, q_dve.at("VM_lo", i))
            for j in range(4):
                t, r = j // 2, SB_DH * (j % 2)
                rows = slice(r, r + SB_DH)
                for b in range(BLOCKS):
                    dst = psum[:, 4 + KEY_BANK[b], KEY_COL[b]:KEY_COL[b] + KEY_LEN[b]]
                    mm3(dst, split(K_hi, K_lo, rows, t, slice(META + b * P, META + (b + 1) * P)),
                        split(Q_hi, Q_lo, rows, t, slice(b * P, SEQ)), b < 3, False)
                    m = nc.tensor.matmul(psum[:, 4 + KEY_BANK[b], KEY_COL[b]:KEY_COL[b] + P],
                                         cmat[:, C_IDENT, :], cmat[:, C_BLOCKED, :], start=False, stop=False,
                                         skip_group_check=True)
                m.then_inc(*q_pe.step(f"scores{j}"))
                pe.wait_ge(q_dve.sem, q_dve.at(f"sp_lo{j}", i))
                for b in range(BLOCKS):
                    for b2 in range(b, BLOCKS):
                        c0 = KEY_COL[b] + P * (b2 - b)
                        for x in (sp_hi, sp_lo):
                            m = nc.tensor.matmul(psum[:, 4 + KEY_BANK[b], c0:c0 + KEY_LEN[b2]],
                                                 cmat[:, C_TRI if b2 == b else C_ALL, :],
                                                 x[:, KEY_OFF[b2]:KEY_OFF[b2] + KEY_LEN[b2]],
                                                 start=False, stop=False, skip_group_check=True)
                m.then_inc(*q_pe.step(f"logs{j}"))
                for b in range(BLOCKS):
                    for x in (sp_hi, sp_lo):
                        nc.tensor.matmul(psum[:, 7, b * P:SEQ], cmat[:, C_ROWS + j, :],
                                         x[:, KEY_OFF[b]:KEY_OFF[b] + KEY_LEN[b]],
                                         start=False, stop=False, skip_group_check=True)
                pe.wait_ge(q_dve.sem, q_dve.at(f"a_lo{j}", i))
                if j >= 2:
                    pe.wait_ge(q_dve.sem, q_dve.at(f"y{j - 2}", i))
                for b in range(BLOCKS):
                    mm3(psum[:, 2 + j % 2, b * P:SEQ],
                        split(V_hi, V_lo, slice(None), b, slice(t * P, (t + 1) * P)),
                        split(a_hi, a_lo, slice(None), slice(KEY_OFF[b], KEY_OFF[b] + KEY_LEN[b])),
                        b == 0, b == BLOCKS - 1, q_pe.step(f"y{j}") if b == BLOCKS - 1 else None)
            pe.wait_ge(q_dve.sem, q_dve.at("am_lo", i))
            for t in range(2):
                mm3(psum[:, 4 + t, :], split(VM_hi, VM_lo, slice(None), t, slice(None)),
                    (m_hi[:, :], m_lo[:, :]), True, True, q_pe.step("y_meta") if t else None)
            pe.wait_ge(q_dve.sem, q_dve.at("Y_lo", i))
            unit(at, 3, 6, "D", SEQ, seq_of(Y_hi, Y_lo))

        pe.wait_ge(cmat_ready, 1)
        pe.wait_ge(memset_done, 2)
        loop(pe, QUADS, quad_body)
        gates("gate_a")

        def head_units(at, i, off_u, off_s, first):
            unit(at, 0, 0, "P", SEQ, from_x)
            unit(at, 1, 2, "P", FULL, from_x)
            if not first:
                out_units(at, 2, 4, i - 1)
            u, s = (2, 4) if first else (4, 12)
            unit(at, u, s, "P", FULL, from_x)
            unit(at, u + 1, s + 2, "P", FULL, from_x)
            pe.wait_ge(strip_free, at.strip(s + 3) + 1)
            for b in range(BLOCKS):
                for e in range(4):
                    m = nc.tensor.transpose(psum[:, 4 + b, e * P:(e + 1) * P],
                                            RY[:, e, META + b * P:META + (b + 1) * P], ident[:, :])
                m.then_inc(*r_pe.step(f"V_turned{b}"))
            pe.wait_ge(r_dve.sem, r_dve.at("V_lo0", i))
            for e in range(4):
                m = nc.tensor.transpose(psum[0:META, 4, e * P:(e + 1) * P], RY[:, e, 0:META], ident[:, :])
            m.then_inc(*r_pe.step("VM_turned"))
            pe.wait_ge(r_dve.sem, r_dve.at("VM_lo", i))
            for b in range(BLOCKS):
                for t in range(2):
                    mm3(psum[:, 4 + KEY_BANK[b], KEY_COL[b]:KEY_COL[b] + KEY_LEN[b]],
                        split(RK_hi, RK_lo, slice(None), t, slice(META + b * P, META + (b + 1) * P)),
                        split(RQ_hi, RQ_lo, slice(None), t, slice(b * P, SEQ)), t == 0 and b < 3, t == 1)
            for t in range(2):
                mm3(psum[:, 7, :], split(RK_hi, RK_lo, slice(None), t, slice(0, P)),
                    split(RQ_hi, RQ_lo, slice(None), t, slice(None)), t == 0, t == 1,
                    r_pe.step("scores") if t else None)
            unit(at, u + 2, s + 4, "P", SEQ, from_x)
            unit(at, u + 3, s + 6, "P", SEQ, from_x)
            pe.wait_ge(r_dve.sem, r_dve.at("SM_lo", i))
            for e in range(4):
                for b in range(BLOCKS):
                    mm3(psum[:, 4 + e, b * P:SEQ],
                        split(VZ_hi, VZ_lo, slice(None), b, slice(e * P, (e + 1) * P)),
                        split(S_hi, S_lo, slice(None), slice(KEY_OFF[b], KEY_OFF[b] + KEY_LEN[b])),
                        b == 0, False)
                mm3(psum[:, 4 + e, :], split(RVM_hi, RVM_lo, slice(None), slice(e * P, (e + 1) * P)),
                    (SM_hi[:, :], SM_lo[:, :]), False, True, r_pe.step("y") if e == 3 else None)
            pe.wait_ge(r_dve.sem, r_dve.at("ys3", i))
            nc.tensor.matmul(psum[:, 4, :], ones[:, :], S_f[:, 0:SEQ], start=True, stop=True)\
                .then_inc(*r_pe.step("mean"))
            pe.wait_ge(r_dve.sem, r_dve.at("sqs3", i))
            nc.tensor.matmul(psum[:, 5, :], ones[:, :], S_f[:, 0:SEQ], start=True, stop=True)\
                .then_inc(*r_pe.step("var"))

        def out_units(at, j, s, i):
            pe.wait_ge(r_dve.sem, r_dve.at("z_lo", i))
            for n in range(2):
                unit(at, j + n, s + 4 * n, "R", SEQ, seq_of(VZ_hi, VZ_lo))

        head_units(Place("head0"), 0, 0, 0, True)
        loop(pe, RET_HEADS - 1, lambda i: head_units(Place("heads", i, 8, 20), i + 1, 0, 0, False))
        out_units(Place("head_out"), 0, 0, RET_HEADS - 1)

        def out_product(phase, x):
            def body(i):
                at = Place(phase, i, 2, 4)
                for j in range(2):
                    unit(at, j, 2 * j, "P", SEQ, x)
            loop(pe, 2, body)

        pe.wait_ge(m_split_lo, DT)
        out_product("w_out", from_x)
        sums(1, SEQ)
        sums(2, SEQ)

        def ffn(tag, n):
            def up(at, j, s):
                unit(at, j, s, "P", SEQ, from_x)
                unit(at, j + 1, s + 2, "P", SEQ, from_x)

            def down(at, j, s, i, slot):
                pe.wait_ge(f_dve.sem, f_dve.at("M_lo", i))
                unit(at, j, s, "D", SEQ, lambda k, a, b: (M_hi[:, slot, k, :], M_lo[:, slot, k, :]))

            def two(at, i0):
                for m in range(2):
                    up(at, 3 * m, 12 * m)
                    down(at, 3 * m + 2, 12 * m + 4, i0 + m, m)
            base = FF_PAIRS * n
            pe.wait_ge(acc_zero, n + 1)
            up(Place("ffn0" + tag), 0, 0)
            rounds = 5 if n == 0 else 4
            loop(pe, rounds, lambda i: two(Place("ffn" + tag, i, 6, 24), base + 2 * i))
            if n:
                two(Place("ffn_last" + tag), base + 2 * rounds)
            down(Place("ffn_end" + tag), 0, 0, base + FF_PAIRS - 1, 0)

        pe.wait_ge(x_lo_ready, 2 * DT)
        ffn("", 0)
        sums(3, SEQ)
        sums(4, FULL)
        pe.wait_ge(x_lo_ready, 3 * DT)
        at = Place("conv_b")
        for j in range(4):
            unit(at, j, 2 * j, "P", FULL, from_x)
        at = Place("conv_a")
        for j in range(6):
            unit(at, j, 2 * j, "P", FULL if j % 3 < 2 else SEQ, from_x)
        pe.wait_ge(c_dve, C2["z_sum"])
        nc.tensor.matmul(psum[:, 4, :], ones[:, :], sq_sum[:, 0:SEQ], start=True, stop=True).then_inc(c_pe, 1)
        pe.wait_ge(c_dve, C2["z_sq_sum"])
        nc.tensor.matmul(psum[:, 5, :], ones[:, :], sq_sum[:, 0:SEQ], start=True, stop=True).then_inc(c_pe, 1)
        pe.wait_ge(c_dve, C2["y_lo"])
        out_product("w_out2", seq_of(y2_hi, y2_lo))
        sums(5, SEQ)
        sums(6, SEQ)
        pe.wait_ge(x_lo_ready, 4 * DT)
        ffn("_2", 1)
        sums(7, SEQ)

    @block.scalar
    def _(act):
        def a(out_, in_, f, **kw):
            return nc.scalar.activation(out_, in_, f, **kw)

        def split_hi(at, j):
            act.wait_ge(w_loaded[at.ring(j)], 16 * (at.loads(j) + 1))
            a(w_hi[at.ring(j)][:, :], w_raw[at.ring(j)][:, :], ACT.Copy).then_inc(w_hi_ready, 1)

        def strips(at, s, n=1):
            act.wait_ge(strip_done, at.strip(s) + n)

        def norm(n, src, width, k_split=None):
            use("ln, exp")
            for k in range(DT):
                if DT * n + k >= 2:
                    act.wait_ge(sq_added, DT * n + k - 1)
                src(k)
            act.wait_ge(sum_done, n + 1)
            if width == FULL:
                dst, ps = wide(std[:, :]), psum[:, 6:8, 0:HALF]
            else:
                dst, ps = std[:, 0:SEQ].rearrange("p (a b) -> p a b", a=2), psum[:, 6:8, 0:SEQ // 2]
            if n:
                act.wait_ge(norm_scaled, DT * n)
            a(dst, ps, ACT.Ln, scale=1.0 / D, bias=g_col("norm_eps", 0)).then_inc(std_ready, 1)
            act.wait_ge(std_ready, 2 * n + 1)
            a(dst, dst, ACT.Exp, scale=-0.5).then_inc(std_ready, 1)
            if k_split is not None:
                for k in range(DT):
                    act.wait_ge(norm_scaled, DT * n + k + 1)
                    a(X_hi[:, k, 0:width] if width == FULL else X_hi[:, k, META:FULL],
                      normed[:, k % 2, 0:width], ACT.Copy).then_inc(x_hi_ready, 1)

        def squares(n, tile, width, ready):
            def src(k):
                ready(k)
                a(sq[:, k % 2, 0:width], tile(k), ACT.Square).then_inc(sq_done, 1)
            return src

        def use(functions):
            act.preload_act_table_set({"ln, exp": "natural_log_exp_and_others",
                                       "sigmoid": "sigmoid_and_others"}[functions])

        act.wait_ge(consts_in, 16 * 7)
        a(cmat[:, :, :].rearrange("p a b -> p (a b)"), w_raw[0][:, 0:N_CMAT * P], ACT.Copy).then_inc(cmat_ready, 1)
        act.wait_ge(x_loaded, 16)
        norm(0, squares(0, lambda k: h[:, k, :], FULL, lambda k: None), FULL, 0)
        for u in range(2):
            act.wait_ge(w_loaded[u], 16)
            a(w_hi[u][:, :], w_raw[u][:, :], ACT.Copy).then_inc(w_hi_ready, 1)

        def gates(phase):
            use("sigmoid")

            def body(i):
                at = Place(phase, i, 2, 4)
                for j in range(2):
                    for c in range(2):
                        strips(at, 2 * j + c)
                        a(gate[:, 4 * i + 2 * j + c, :], strip_view(at.slot(2 * j + c), SEQ), ACT.Sigmoid)\
                            .then_inc(strip_free, 1)
                    split_hi(at, j)
            loop(act, 2, body, 2 if phase == "gate_b" else 0)

        gates("gate_b")

        def quad_body(i):
            at = Place("quads", i, 4, 14)
            for t in range(2):
                strips(at, t)
                a(Q_hi[:, t, :], strip_view(at.slot(t), SEQ), ACT.Copy, scale=SB_DH ** -0.5)\
                    .then_inc(*q_act.step(f"Q_hi{t}"))
            split_hi(at, 0)
            for t in range(2):
                strips(at, 2 + t)
                a(wide(K_hi[:, t, :]), strip_view(at.slot(2 + t), FULL), ACT.Copy)\
                    .then_inc(*q_act.step(f"K_hi{t}"))
            split_hi(at, 1)
            strips(at, 5)
            split_hi(at, 2)
            for n in range(2):
                act.wait_ge(q_pe.sem, q_pe.at(f"V_turned{n}", i))
                a(V_hi[:, 2 * n:2 * n + 2, :].rearrange("p a b -> p (a b)"), psum[:, 4 + n, :], ACT.Copy)\
                    .then_inc(*q_act.step(f"V_hi{n}"))
            act.wait_ge(q_dve.sem, q_dve.at("VM", i))
            a(VM_hi[:, :, :], VM[:, :, :], ACT.Copy).then_inc(*q_act.step("VM_hi"))
            act.wait_ge(q_pe.sem, q_pe.at("m_scores", i))
            a(m_f[:, :], psum[:, 7, :], ACT.Abs).then_inc(*q_act.step("m_abs"))
            act.wait_ge(q_act.sem, q_act.at("m_abs", i))
            a(m_f[:, :], m_f[:, :], ACT.Exp, scale=-1.0).then_inc(*q_act.step("m_exp"))
            act.wait_ge(q_act.sem, q_act.at("m_exp", i))
            a(m_f[:, :], m_f[:, :], ACT.Ln, bias=g_col("one", 0)).then_inc(*q_act.step("m_ln"))
            act.wait_ge(q_dve.sem, q_dve.at("m_sp", i))
            a(m_hi[:, :], m_f[:, :], ACT.Copy).then_inc(*q_act.step("m_hi"))
            for j in range(4):
                act.wait_ge(q_pe.sem, q_pe.at(f"scores{j}", i))
                if j:
                    act.wait_ge(q_dve.sem, q_dve.at(f"sp_lo{j - 1}", i))
                for n, (bank, off, w) in enumerate(PARTS):
                    a(sp[:, off:off + w], psum[:, 4 + bank, 0:w], ACT.Abs).then_inc(*q_act.step(f"abs{n}_{j}"))
                act.wait_ge(q_act.sem, q_act.at(f"abs2_{j}", i))
                a(sp[:, :], sp[:, :], ACT.Exp, scale=-1.0).then_inc(*q_act.step(f"exp{j}"))
                act.wait_ge(q_act.sem, q_act.at(f"exp{j}", i))
                a(sp[:, :], sp[:, :], ACT.Ln, bias=g_col("one", 0)).then_inc(*q_act.step(f"ln{j}"))
                act.wait_ge(q_dve.sem, q_dve.at(f"sp2_{j}", i))
                a(sp_hi[:, :], sp[:, :], ACT.Copy).then_inc(*q_act.step(f"sp_hi{j}"))
                act.wait_ge(q_pe.sem, q_pe.at(f"logs{j}", i))
                for n, (bank, off, w) in enumerate(PARTS):
                    a(a_f[:, off:off + w], psum[:, 4 + bank, 0:w], ACT.Exp).then_inc(*q_act.step(f"a_part{n}_{j}"))
                act.wait_ge(q_act.sem, q_act.at(f"a_part2_{j}", i))
                if j:
                    act.wait_ge(q_pe.sem, q_pe.at(f"y{j - 1}", i))
                a(a_hi[:, :], a_f[:, :], ACT.Copy).then_inc(*q_act.step(f"a_hi{j}"))
            act.wait_ge(q_pe.sem, q_pe.at("y3", i))
            a(m_f[:, :], psum[:, 7, :], ACT.Exp).then_inc(*q_act.step("am_exp"))
            act.wait_ge(q_act.sem, q_act.at("am_exp", i))
            a(m_hi[:, :], m_f[:, :], ACT.Copy).then_inc(*q_act.step("am_hi"))
            act.wait_ge(q_dve.sem, q_dve.at("y_meta1", i))
            a(Y_hi[:, :, :], VY[:, :, META:FULL], ACT.Copy).then_inc(*q_act.step("Y_hi"))
            strips(at, 13)
            split_hi(at, 3)

        use("ln, exp")
        loop(act, QUADS, quad_body)

        act.wait_ge(q_dve.sem, q_dve.at("merge7", QUADS - 1))
        gates("gate_a")

        def head_units(at, i, first):
            for t in range(2):
                act.wait_ge(r_dve.sem, r_dve.at(f"q_r{t + 1}", i))
                a(RQ_hi[:, t, :], RY[:, t, 0:SEQ], ACT.Copy).then_inc(*r_act.step(f"RQ_hi{t}"))
            strips(at, 1)
            split_hi(at, 0)
            for t in range(2):
                act.wait_ge(r_dve.sem, r_dve.at(f"k_r{t + 1}", i))
                a(RK_hi[:, t, :], RY[:, t, :], ACT.Copy).then_inc(*r_act.step(f"RK_hi{t}"))
            strips(at, 3)
            split_hi(at, 1)
            if not first:
                for n in range(2):
                    strips(at, 4 + 4 * n + 3)
                    split_hi(at, 2 + n)
            u, s = (2, 4) if first else (4, 12)
            for n in range(2):
                strips(at, s + 2 * n + 1)
                split_hi(at, u + n)
            for b in range(BLOCKS):
                act.wait_ge(r_pe.sem, r_pe.at(f"V_turned{b}", i))
                a(VZ_hi[:, b, :], psum[:, 4 + b, :], ACT.Copy).then_inc(*r_act.step(f"V_hi{b}"))
            act.wait_ge(r_pe.sem, r_pe.at("VM_turned", i))
            a(RVM_hi[:, :], psum[0:META, 4, :], ACT.Copy).then_inc(*r_act.step("VM_hi"))
            act.wait_ge(r_dve.sem, r_dve.at("S3", i))
            a(S_hi[:, :], S_f[:, :], ACT.Copy).then_inc(*r_act.step("S_hi"))
            act.wait_ge(r_dve.sem, r_dve.at("SM", i))
            a(SM_hi[:, :], SM_f[:, :], ACT.Copy).then_inc(*r_act.step("SM_hi"))
            use("sigmoid")
            for n in range(2):
                for c in range(2):
                    strips(at, s + 4 + 2 * n + c)
                    e = 2 * n + c
                    a(silu_g[:, e, :], strip_view(at.slot(s + 4 + e), SEQ), ACT.Sigmoid)\
                        .then_inc(*r_act.step(f"g_sig{e}"))
                split_hi(at, u + 2 + n)
            use("ln, exp")
            for e in range(4):
                act.wait_ge(r_dve.sem, r_dve.at(f"yc{e}", i))
                if e == 0:
                    act.wait_ge(r_pe.sem, r_pe.at("mean", i))
                a(S_sq(e), RY[:, e, 0:SEQ], ACT.Square).then_inc(*r_act.step(f"y_sq{e}"))
            act.wait_ge(r_pe.sem, r_pe.at("var", i))
            a(r_std[:, :], psum[:, 5, :], ACT.Ln, scale=1.0 / RET_DV, bias=g_col("gn_eps", 0))\
                .then_inc(*r_act.step("ln"))
            act.wait_ge(r_act.sem, r_act.at("ln", i))
            a(r_std[:, :], r_std[:, :], ACT.Exp, scale=-0.5).then_inc(*r_act.step("std"))
            act.wait_ge(r_dve.sem, r_dve.at("zg", i))
            a(VZ_hi[:, :, :], RY[:, :, 0:SEQ], ACT.Copy).then_inc(*r_act.step("z_hi"))

        def S_sq(e):
            if e == 0:
                return S_f[:, 0:SEQ]
            if e == 1:
                return S_f[:, SEQ:2 * SEQ]
            return gated_r[:, :] if e == 2 else decay_sq

        decay_sq = r_std[:, :]

        head_units(Place("head0"), 0, True)
        loop(act, RET_HEADS - 1, lambda i: head_units(Place("heads", i, 8, 20), i + 1, False))
        at = Place("head_out")
        for n in range(2):
            strips(at, 4 * n + 3)
            split_hi(at, n)
        act.wait_ge(r_merge, DT * RET_HEADS)
        for k in range(DT):
            a(X_hi[:, k, META:FULL], acc[:, k, :], ACT.Copy).then_inc(m_split_hi, 1)

        def out_product(phase):
            def body(i):
                at = Place(phase, i, 2, 4)
                for j in range(2):
                    strips(at, 2 * j + 1)
                    split_hi(at, j)
            loop(act, 2, body)

        out_product("w_out")
        norm(1, squares(1, lambda k: acc[:, k, :], SEQ, lambda k: act.wait_ge(mix_out, k + 1)), SEQ)
        norm(2, squares(2, lambda k: h[:, k, META:FULL], SEQ, lambda k: act.wait_ge(post_done, k + 1)), SEQ, 1)

        def ffn(tag, n):
            def gate_up(at, j, s, i):
                for c in range(2):
                    strips(at, s + c)
                    if c == 0:
                        act.wait_ge(f_dve.sem, f_dve.at("M_lo", i - 1)) if not (type(i) is int and i == 0) else None
                    a(silu_a[:, c, :], strip_view(at.slot(s + c), SEQ), ACT.Sigmoid)\
                        .then_inc(*f_act.step(f"sig{c}"))
                split_hi(at, j)
                strips(at, s + 3)
                split_hi(at, j + 1)
                act.wait_ge(f_dve.sem, f_dve.at("prod", i))
            def hidden(i, slot):
                a(M_hi[:, slot, :, :], silu_a[:, :, :], ACT.Copy).then_inc(*f_act.step("M_hi"))

            def two(at, i0, final):
                for m in range(2):
                    gate_up(at, 3 * m, 12 * m, i0 + m + 1)
                    hidden(i0 + m + 1, (m + 1) % 2)
                    strips(at, 12 * m + 11)
                    if not (final and m == 1):
                        split_hi(at, 3 * m + 2)
            base = FF_PAIRS * n
            use("sigmoid")
            gate_up(Place("ffn0" + tag), 0, 0, base)
            hidden(base, 0)
            rounds = 5 if n == 0 else 4
            loop(act, rounds, lambda i: two(Place("ffn" + tag, i, 6, 24), base + 2 * i, False))
            if n:
                two(Place("ffn_last" + tag), base + 2 * rounds, True)
            at = Place("ffn_end" + tag)
            if n == 0:
                strips(at, 7)
                split_hi(at, 0)

        ffn("", 0)
        norm(3, squares(3, lambda k: acc[:, k, :], SEQ, lambda k: act.wait_ge(f_added, DT * FF_PAIRS) if k == 0 else None), SEQ)
        norm(4, squares(4, lambda k: h[:, k, :], FULL, lambda k: act.wait_ge(post_done, DT + k + 1)), FULL, 2)

        use("sigmoid")
        at = Place("conv_b")
        count = [0]

        def ca(ins):
            count[0] += 1
            ins.then_inc(c_act, 1)
            return count[0]

        for half in range(2):
            for c in range(2):
                strips(at, 4 * half + c)
                if half:
                    act.wait_ge(c_dve, C2[f"glu{c}"])
                a(wide(conv_sig[:, c, :]), strip_view(at.slot(c), FULL), ACT.Sigmoid).then_inc(strip_free, 1)
            split_hi(at, 2 * half)
            strips(at, 4 * half + 3)
            split_hi(at, 2 * half + 1)
        at = Place("conv_a")
        for j in range(6):
            strips(at, 2 * j + 1)
            split_hi(at, j)
        use("ln, exp")
        for t in range(CT):
            act.wait_ge(c_dve, C2[f"zc{t}"])
            if t >= 2:
                act.wait_ge(c_dve, C2[f"zsq{t - 2}"])
            ca(a(sq[:, t % 2, 0:SEQ], z[:, t, :], ACT.Square))
        act.wait_ge(c_pe, 2)
        n = ca(a(std[:, 0:SEQ], psum[:, 5, :], ACT.Ln, scale=1.0 / WB, bias=g_col("ln_eps", 0)))
        act.wait_ge(c_act, n)
        n = ca(a(std[:, 0:SEQ], std[:, 0:SEQ], ACT.Exp, scale=-0.5))
        assert n == A2["std"]
        use("sigmoid")
        for t in range(CT):
            act.wait_ge(c_dve, C2[f"zn{t}"])
            n = ca(a(z[:, t, :], z[:, t, :], ACT.Identity, scale=g_col("ln_gain", t), bias=g_col("ln_bias", t)))
            act.wait_ge(c_act, n)
            if t >= 2:
                act.wait_ge(c_dve, C2[f"yb{t - 2}"])
            n = ca(a(normed[:, t % 2, 0:SEQ], z[:, t, :], ACT.Sigmoid))
            assert n == A2[f"e{t}"]
        for t in range(CT):
            act.wait_ge(c_dve, C2[f"yb{t}"])
            n = ca(a(y2_hi[:, CT + t, :], z[:, t, :], ACT.Copy))
            assert n == A2[f"yh{t}"]
        out_product("w_out2")
        norm(5, squares(5, lambda k: acc[:, k, :], SEQ, lambda k: act.wait_ge(mix_out, DT + k + 1)), SEQ)
        norm(6, squares(6, lambda k: h[:, k, META:FULL], SEQ, lambda k: act.wait_ge(post_done, 2 * DT + k + 1)), SEQ, 3)
        ffn("_2", 1)
        norm(7, squares(7, lambda k: acc[:, k, :], SEQ, lambda k: act.wait_ge(f_added, 2 * DT * FF_PAIRS) if k == 0 else None), SEQ)

    @block.vector
    def _(dve):
        v = nc.vector

        def split_lo(at, j):
            dve.wait_ge(w_hi_ready, at.unit(j) + 3)
            v.tensor_tensor(w_lo[at.ring(j)][:, :], w_raw[at.ring(j)][:, :], as_f32(w_hi[at.ring(j)][:, :]),
                            ALU.subtract).then_inc(w_lo_ready, 1)

        def strips(at, s, n=1):
            dve.wait_ge(strip_done, at.strip(s) + n)

        def stt(out_, in0, scalar, in1, op0, op1):
            return v.scalar_tensor_tensor(out=out_, in0=in0, scalar=scalar, in1=in1, op0=op0, op1=op1)

        def norm(n, width):
            for k in range(DT):
                dve.wait_ge(sq_done, DT * n + k + 1)
                if k == 0:
                    if n:
                        dve.wait_ge(sum_done, n)
                    ins = v.tensor_copy(sq_sum[:, 0:width], sq[:, 0, 0:width])
                else:
                    dve.wait_ge(sq_added, DT * n + k)
                    ins = v.tensor_tensor(sq_sum[:, 0:width], sq_sum[:, 0:width], sq[:, k % 2, 0:width], ALU.add)
                ins.then_inc(sq_added, 1)

        def norm_split(n, s, width, gain):
            norm(n, width)
            dve.wait_ge(std_ready, 2 * n + 2)
            cols = slice(0, FULL) if width == FULL else slice(META, FULL)

            def lo(k):
                dve.wait_ge(x_hi_ready, DT * s + k + 1)
                v.tensor_tensor(X_lo[:, k, cols], normed[:, k % 2, 0:width], as_f32(X_hi[:, k, cols]),
                                ALU.subtract).then_inc(x_lo_ready, 1)
            for k in range(DT):
                if k >= 2:
                    dve.wait_ge(x_lo_ready, DT * s + k - 1)
                stt(normed[:, k % 2, 0:width], h[:, k, cols], g_col(gain, k), std[:, 0:width],
                    ALU.mult, ALU.mult).then_inc(norm_scaled, 1)
                if k:
                    lo(k - 1)
            lo(DT - 1)

        def norm_add(n, p, gain):
            norm(n, SEQ)
            dve.wait_ge(std_ready, 2 * n + 2)
            for k in range(DT):
                stt(normed[:, k % 2, 0:SEQ], acc[:, k, :], g_col(gain, k), std[:, 0:SEQ],
                    ALU.mult, ALU.mult).then_inc(norm_scaled, 1)
                dve.wait_ge(norm_scaled, DT * n + k + 1)
                v.tensor_tensor(h[:, k, META:FULL], h[:, k, META:FULL], normed[:, k % 2, 0:SEQ], ALU.add)\
                    .then_inc(post_done, 1)

        dve.wait_ge(consts_in, 16 * 7)
        dve.wait_ge(x_loaded, 16)
        norm_split(0, 0, FULL, "pre_mix")
        for u in range(2):
            dve.wait_ge(w_hi_ready, u + 1)
            v.tensor_tensor(w_lo[u][:, :], w_raw[u][:, :], as_f32(w_hi[u][:, :]), ALU.subtract)\
                .then_inc(w_lo_ready, 1)
        dve.wait_ge(x_lo_ready, DT)
        v.memset(acc[:, :, :], 0.0).then_inc(memset_done, 1)
        v.memset(v_pad[:, :, :, :], 0.0).then_inc(memset_done, 1)
        dve.wait_ge(memset_done, 2)

        def gates(phase):
            def body(i):
                at = Place(phase, i, 2, 4)
                for j in range(2):
                    split_lo(at, j)
            loop(dve, 2, body)

        gates("gate_b")

        def quad_body(i):
            at = Place("quads", i, 4, 14)

            def split_strip(t, s, hi, lo, width, scale, name):
                dve.wait_ge(q_act.sem, q_act.at(name, i))
                ps = strip_view(at.slot(s), width)
                hi_, lo_ = as_f32(hi[:, t, :]), lo[:, t, :]
                if width == FULL:
                    hi_, lo_ = wide(hi_), wide(lo_)
                stt(lo_, ps, scale, hi_, ALU.mult, ALU.subtract).then_inc(strip_free, 1)

            for t in range(2):
                split_strip(t, t, Q_hi, Q_lo, SEQ, SB_DH ** -0.5, f"Q_hi{t}")
            split_lo(at, 0)
            for t in range(2):
                split_strip(t, 2 + t, K_hi, K_lo, FULL, 1.0, f"K_hi{t}")
            split_lo(at, 1)
            dve.wait_ge(strip_free, at.strip(3) + 1)
            for name, src, dst in (("KM_hi", K_hi, KM_hi), ("KM_lo", K_lo, KM_lo)):
                v.tensor_tensor(dst[:, :, :].rearrange("p t (j m) -> p t j m", j=4),
                                as_f32(src[:, :, 0:32]).unsqueeze(2).broadcast_to([P, 2, 4, 32]),
                                mask_k[:, :, :, :], ALU.mult).then_inc(*q_dve.step(name))
            for t in range(2):
                strips(at, 4 + t)
                v.tensor_copy(wide(VY[:, t, :]), strip_view(at.slot(4 + t), FULL)).then_inc(strip_free, 1)
            split_lo(at, 2)
            dve.wait_ge(strip_free, at.strip(5) + 1)
            for t in range(2):
                v.tensor_copy(v_pad[:, t, 2 * t:2 * t + 2, 0:META],
                              VY[:, t, 0:META].unsqueeze(1).broadcast_to([P, 2, META]))\
                    .then_inc(*q_dve.step(f"v_pad{t}"))
            for n in range(2):
                dve.wait_ge(q_act.sem, q_act.at(f"V_hi{n}", i))
                v.tensor_tensor(V_lo[:, 2 * n:2 * n + 2, :].rearrange("p a b -> p (a b)"), psum[:, 4 + n, :],
                                as_f32(V_hi[:, 2 * n:2 * n + 2, :]).rearrange("p a b -> p (a b)"), ALU.subtract)\
                    .then_inc(*q_dve.step(f"V_lo{n}"))
            dve.wait_ge(q_pe.sem, q_pe.at("VM_turned", i))
            v.tensor_tensor(VM[:, :, :].rearrange("p a b -> p (a b)"), psum[:, 6, 0:2 * P],
                            mask_v[:, :, :].rearrange("p a b -> p (a b)"), ALU.mult).then_inc(*q_dve.step("VM"))
            dve.wait_ge(q_act.sem, q_act.at("VM_hi", i))
            v.tensor_tensor(VM_lo[:, :, :], VM[:, :, :], as_f32(VM_hi[:, :, :]), ALU.subtract)\
                .then_inc(*q_dve.step("VM_lo"))
            dve.wait_ge(q_act.sem, q_act.at("m_ln", i))
            stt(m_f[:, :], psum[:, 7, :], 0.0, m_f[:, :], ALU.max, ALU.add).then_inc(*q_dve.step("m_sp"))
            dve.wait_ge(q_act.sem, q_act.at("m_hi", i))
            v.tensor_tensor(m_lo[:, :], m_f[:, :], as_f32(m_hi[:, :]), ALU.subtract).then_inc(*q_dve.step("m_lo"))
            for j in range(4):
                t, r = j // 2, SB_DH * (j % 2)
                dve.wait_ge(q_act.sem, q_act.at(f"ln{j}", i))
                for n, (bank, off, w) in enumerate(PARTS):
                    stt(sp[:, off:off + w], psum[:, 4 + bank, 0:w], 0.0, sp[:, off:off + w], ALU.max, ALU.add)\
                        .then_inc(*q_dve.step(f"sp{n}_{j}"))
                dve.wait_ge(q_act.sem, q_act.at(f"sp_hi{j}", i))
                v.tensor_tensor(sp_lo[:, :], sp[:, :], as_f32(sp_hi[:, :]), ALU.subtract)\
                    .then_inc(*q_dve.step(f"sp_lo{j}"))
                dve.wait_ge(q_act.sem, q_act.at(f"a_hi{j}", i))
                v.tensor_tensor(a_lo[:, :], a_f[:, :], as_f32(a_hi[:, :]), ALU.subtract)\
                    .then_inc(*q_dve.step(f"a_lo{j}"))
                dve.wait_ge(q_pe.sem, q_pe.at(f"y{j}", i))
                v.tensor_copy(VY[r:r + SB_DH, t, META:FULL], psum[r:r + SB_DH, 2 + j % 2, :])\
                    .then_inc(*q_dve.step(f"y{j}"))
            dve.wait_ge(q_act.sem, q_act.at("am_hi", i))
            v.tensor_tensor(m_lo[:, :], m_f[:, :], as_f32(m_hi[:, :]), ALU.subtract).then_inc(*q_dve.step("am_lo"))
            dve.wait_ge(q_pe.sem, q_pe.at("y_meta", i))
            dve.wait_ge(q_dve.sem, q_dve.at("y3", i))
            for t in range(2):
                v.tensor_tensor(VY[:, t, META:FULL], VY[:, t, META:FULL], psum[:, 4 + t, :], ALU.add)\
                    .then_inc(*q_dve.step(f"y_meta{t}"))
            dve.wait_ge(q_act.sem, q_act.at("Y_hi", i))
            v.tensor_tensor(Y_lo[:, :, :], VY[:, :, META:FULL], as_f32(Y_hi[:, :, :]), ALU.subtract)\
                .then_inc(*q_dve.step("Y_lo"))
            for m in range(DT):
                strips(at, 6 + m)
                if m:
                    dve.wait_ge(q_dve.sem, q_dve.at(f"merge{m - 1}", i))
                v.tensor_tensor(gated[:, :], strip_view(at.slot(6 + m), SEQ), gate[:, m, :], ALU.mult)\
                    .then_inc(strip_free, 1)
                dve.wait_ge(strip_free, at.strip(6 + m) + 1)
                v.tensor_tensor(acc[:, m, :], acc[:, m, :], gated[:, :], ALU.add)\
                    .then_inc(*q_dve.step(f"merge{m}"))
            split_lo(at, 3)

        dve.wait_ge(strip_free, START["gate_b"][1] + DT)
        loop(dve, QUADS, quad_body)
        gates("gate_a")
        dve.wait_ge(strip_free, START["gate_a"][1] + DT)

        def merge(at, s, i):
            for n in range(4):
                m = n + (0 if s[1] == 0 else 4)
                strips(at, s[0] + n)
                v.tensor_tensor(gated_r[:, :], strip_view(at.slot(s[0] + n), SEQ), gate[:, m, :], ALU.mult)\
                    .then_inc(strip_free, 1)
                dve.wait_ge(strip_free, at.strip(s[0] + n) + 1)
                v.tensor_tensor(acc[:, m, :], acc[:, m, :], gated_r[:, :], ALU.add).then_inc(r_merge, 1)
                dve.wait_ge(r_merge, DT * i + m + 1)

        def head_units(at, i, first):
            def rotary(x, s, width, hi, lo):
                cols = slice(0, FULL) if width == FULL else slice(META, FULL)
                fold = wide if width == FULL else (lambda ap: ap)
                cos, sin = (fold(rot[:, n, cols]) for n in range(2))
                R = [fold(RY[:, n, 0:width]) for n in range(4)]
                strips(at, s)
                v.tensor_tensor(R[0], strip_view(at.slot(s), width), cos, ALU.mult)\
                    .then_inc(*r_dve.step(f"{x}_cos"))
                v.tensor_tensor(R[1], strip_view(at.slot(s), width), sin, ALU.mult).then_inc(strip_free, 1)
                strips(at, s + 1)
                v.tensor_tensor(R[2], strip_view(at.slot(s + 1), width), sin, ALU.mult)\
                    .then_inc(*r_dve.step(f"{x}_sin"))
                v.tensor_tensor(R[3], strip_view(at.slot(s + 1), width), cos, ALU.mult).then_inc(strip_free, 1)
                dve.wait_ge(strip_free, at.strip(s + 1) + 1)
                dve.wait_ge(r_dve.sem, r_dve.at(f"{x}_sin", i))
                v.tensor_tensor(RY[:, 0, 0:width], RY[:, 0, 0:width], RY[:, 2, 0:width], ALU.subtract)\
                    .then_inc(*r_dve.step(f"{x}_r1"))
                v.tensor_tensor(RY[:, 1, 0:width], RY[:, 1, 0:width], RY[:, 3, 0:width], ALU.add)\
                    .then_inc(*r_dve.step(f"{x}_r2"))
                dve.wait_ge(r_act.sem, r_act.at(f"R{x.upper()}_hi1", i))
                v.tensor_tensor(lo[:, :, :], RY[:, 0:2, 0:width], as_f32(hi[:, :, :]), ALU.subtract)\
                    .then_inc(*r_dve.step(f"{x}_lo"))
            if not first:
                dve.wait_ge(r_dve.sem, r_dve.at("z_lo", i - 1))
            rotary("q", 0, SEQ, RQ_hi, RQ_lo)
            split_lo(at, 0)
            dve.wait_ge(r_dve.sem, r_dve.at("q_lo", i))
            rotary("k", 2, FULL, RK_hi, RK_lo)
            split_lo(at, 1)
            if not first:
                for n in range(2):
                    merge(at, (4 + 4 * n, n), i - 1)
                    split_lo(at, 2 + n)
            u, s = (2, 4) if first else (4, 12)
            dve.wait_ge(r_dve.sem, r_dve.at("k_lo", i))
            for e in range(4):
                strips(at, s + e)
                v.tensor_copy(wide(RY[:, e, :]), strip_view(at.slot(s + e), FULL)).then_inc(strip_free, 1)
                if e % 2:
                    split_lo(at, u + e // 2)
            for b in range(BLOCKS):
                dve.wait_ge(r_act.sem, r_act.at(f"V_hi{b}", i))
                v.tensor_tensor(VZ_lo[:, b, :], psum[:, 4 + b, :], as_f32(VZ_hi[:, b, :]), ALU.subtract)\
                    .then_inc(*r_dve.step(f"V_lo{b}"))
            dve.wait_ge(r_act.sem, r_act.at("VM_hi", i))
            v.tensor_tensor(RVM_lo[:, :], psum[0:META, 4, :], as_f32(RVM_hi[:, :]), ALU.subtract)\
                .then_inc(*r_dve.step("VM_lo"))
            dve.wait_ge(r_pe.sem, r_pe.at("scores", i))
            dve.wait_ge(decay_loaded, 16 * (i + 1))
            for b in range(BLOCKS):
                v.tensor_tensor(S_f[:, KEY_OFF[b]:KEY_OFF[b] + KEY_LEN[b]],
                                psum[:, 4 + KEY_BANK[b], KEY_COL[b]:KEY_COL[b] + KEY_LEN[b]],
                                decay[:, 0, 0:KEY_LEN[b]], ALU.mult).then_inc(*r_dve.step(f"S{b}"))
            v.tensor_tensor(SM_f[:, :], psum[0:META, 7, :], decay[0:META, 1, :], ALU.mult)\
                .then_inc(*r_dve.step("SM"))
            dve.wait_ge(r_act.sem, r_act.at("S_hi", i))
            v.tensor_tensor(S_lo[:, :], S_f[:, :], as_f32(S_hi[:, :]), ALU.subtract).then_inc(*r_dve.step("S_lo"))
            dve.wait_ge(r_act.sem, r_act.at("SM_hi", i))
            v.tensor_tensor(SM_lo[:, :], SM_f[:, :], as_f32(SM_hi[:, :]), ALU.subtract)\
                .then_inc(*r_dve.step("SM_lo"))
            for e in range(4):
                dve.wait_ge(r_act.sem, r_act.at(f"g_sig{e}", i))
                v.tensor_tensor(silu_g[:, e, :], silu_g[:, e, :], strip_view(at.slot(s + 4 + e), SEQ), ALU.mult)\
                    .then_inc(strip_free, 1)
                if e % 2:
                    split_lo(at, u + 2 + e // 2)
            dve.wait_ge(r_pe.sem, r_pe.at("y", i))
            for e in range(4):
                v.tensor_copy(RY[:, e, 0:SEQ], psum[:, 4 + e, :]).then_inc(*r_dve.step(f"y{e}"))
            for e in range(1, 4):
                dve.wait_ge(r_dve.sem, r_dve.at(f"y{e}" if e == 1 else f"ys{e - 1}", i))
                v.tensor_tensor(S_f[:, 0:SEQ], RY[:, 0, 0:SEQ] if e == 1 else S_f[:, 0:SEQ], RY[:, e, 0:SEQ],
                                ALU.add).then_inc(*r_dve.step(f"ys{e}"))
            dve.wait_ge(r_pe.sem, r_pe.at("mean", i))
            for e in range(4):
                stt(RY[:, e, 0:SEQ], psum[:, 4, :], -1.0 / RET_DV, RY[:, e, 0:SEQ], ALU.mult, ALU.add)\
                    .then_inc(*r_dve.step(f"yc{e}"))
            squares = [S_f[:, 0:SEQ], S_f[:, SEQ:2 * SEQ], gated_r[:, :], r_std[:, :]]
            for e in range(1, 4):
                dve.wait_ge(r_act.sem, r_act.at(f"y_sq{e}", i))
                if e > 1:
                    dve.wait_ge(r_dve.sem, r_dve.at(f"sqs{e - 1}", i))
                v.tensor_tensor(squares[0], squares[0], squares[e], ALU.add).then_inc(*r_dve.step(f"sqs{e}"))
            dve.wait_ge(r_act.sem, r_act.at("std", i))
            v.tensor_tensor(RY[:, :, 0:SEQ], RY[:, :, 0:SEQ],
                            r_std[:, :].unsqueeze(1).broadcast_to([P, 4, SEQ]), ALU.mult)\
                .then_inc(*r_dve.step("zs"))
            dve.wait_ge(r_dve.sem, r_dve.at("zs", i))
            dve.wait_ge(strip_free, at.strip(s + 7) + 1)
            v.tensor_tensor(RY[:, :, 0:SEQ], RY[:, :, 0:SEQ], silu_g[:, :, :], ALU.mult)\
                .then_inc(*r_dve.step("zg"))
            dve.wait_ge(r_act.sem, r_act.at("z_hi", i))
            v.tensor_tensor(VZ_lo[:, :, :], RY[:, :, 0:SEQ], as_f32(VZ_hi[:, :, :]), ALU.subtract)\
                .then_inc(*r_dve.step("z_lo"))

        head_units(Place("head0"), 0, True)
        loop(dve, RET_HEADS - 1, lambda i: head_units(Place("heads", i, 8, 20), i + 1, False))
        at = Place("head_out")
        for n in range(2):
            merge(at, (4 * n, n), RET_HEADS - 1)
            split_lo(at, n)
        for k in range(DT):
            dve.wait_ge(m_split_hi, k + 1)
            v.tensor_tensor(X_lo[:, k, META:FULL], acc[:, k, :], as_f32(X_hi[:, k, META:FULL]), ALU.subtract)\
                .then_inc(m_split_lo, 1)

        def out_product(phase):
            def body(i):
                at = Place(phase, i, 2, 4)
                for j in range(2):
                    for c in range(2):
                        strips(at, 2 * j + c)
                        v.tensor_copy(acc[:, 4 * i + 2 * j + c, :], strip_view(at.slot(2 * j + c), SEQ))\
                            .then_inc(strip_free, 1)
                    split_lo(at, j)
            loop(dve, 2, body)
            dve.wait_ge(strip_free, START[phase][1] + DT)
            for k in range(DT):
                v.tensor_copy(acc[:, k, 0:1], acc[:, k, 0:1]).then_inc(mix_out, 1)

        out_product("w_out")
        dve.wait_ge(x_loaded, 48)
        norm_add(1, 0, "post_mix")
        norm_split(2, 1, SEQ, "pre_ffn")

        def ffn(tag, n):
            def gate_up(at, j, s, i, slot, final=False):
                for c in range(2):
                    dve.wait_ge(f_act.sem, f_act.at(f"sig{c}", i))
                    v.tensor_tensor(silu_a[:, c, :], silu_a[:, c, :], strip_view(at.slot(s + c), SEQ), ALU.mult)\
                        .then_inc(strip_free, 1)
                split_lo(at, j)
                dve.wait_ge(strip_free, at.strip(s + 1) + 1)
                for c in range(2):
                    strips(at, s + 2 + c)
                    v.tensor_tensor(silu_a[:, c, :], silu_a[:, c, :], strip_view(at.slot(s + 2 + c), SEQ), ALU.mult)\
                        .then_inc(strip_free, 1)
                dve.wait_ge(strip_free, at.strip(s + 3) + 1)
                v.tensor_copy(silu_a[:, 0, 0:1], silu_a[:, 0, 0:1]).then_inc(*f_dve.step("prod"))
                split_lo(at, j + 1)
                dve.wait_ge(f_act.sem, f_act.at("M_hi", i))
                v.tensor_tensor(M_lo[:, slot, :, :], silu_a[:, :, :], as_f32(M_hi[:, slot, :, :]), ALU.subtract)\
                    .then_inc(*f_dve.step("M_lo"))

            def add(at, s, i):
                for m in range(DT):
                    strips(at, s + m)
                    v.tensor_tensor(acc[:, m, :], acc[:, m, :], strip_view(at.slot(s + m), SEQ), ALU.add)\
                        .then_inc(strip_free, 1)

            def two(at, i0, final):
                for m in range(2):
                    gate_up(at, 3 * m, 12 * m, i0 + m + 1, (m + 1) % 2)
                    add(at, 12 * m + 4, i0 + m)
                    if not (final and m == 1):
                        split_lo(at, 3 * m + 2)
            base = FF_PAIRS * n
            dve.wait_ge(post_done, (2 * n + 1) * DT)
            v.memset(acc[:, :, :], 0.0).then_inc(acc_zero, 1)
            gate_up(Place("ffn0" + tag), 0, 0, base, 0)
            dve.wait_ge(acc_zero, n + 1)
            rounds = 5 if n == 0 else 4
            loop(dve, rounds, lambda i: two(Place("ffn" + tag, i, 6, 24), base + 2 * i, False))
            if n:
                two(Place("ffn_last" + tag), base + 2 * rounds, True)
            at = Place("ffn_end" + tag)
            add(at, 0, base + FF_PAIRS - 1)
            if n == 0:
                split_lo(at, 0)
            dve.wait_ge(strip_free, at.strip(7) + 1)
            v.tensor_copy(acc[:, 0, 0:1], acc[:, 0, 0:1]).then_inc(f_added, DT * FF_PAIRS)

        ffn("", 0)
        v.tensor_copy(h[:, :, 0:META], meta2_f[:, :, :]).then_inc(memset_done, 1)
        dve.wait_ge(memset_done, 3)
        norm_add(3, 1, "post_ffn")
        norm_split(4, 2, FULL, "pre_mix2")

        count = [0]

        def cd(ins, name=None):
            count[0] += 1
            ins.then_inc(c_dve, 1)
            if name:
                assert C2[name] == count[0], (name, count[0])
            return count[0]

        def last():
            dve.wait_ge(c_dve, count[0])

        LEFT = TAPS_B - 1
        pad = LEFT - META
        cd(v.memset(glu[:, :, 0:pad], 0.0))
        at = Place("conv_b")
        for half in range(2):
            for c in range(2):
                dve.wait_ge(strip_free, at.strip(4 * half + c) + 1)
            split_lo(at, 2 * half)
            for c in range(2):
                strips(at, 4 * half + 2 + c)
                v.tensor_tensor(wide(glu[:, 2 * half + c, pad:]), wide(conv_sig[:, c, :]),
                                strip_view(at.slot(4 * half + 2 + c), FULL), ALU.mult).then_inc(strip_free, 1)
            dve.wait_ge(strip_free, at.strip(4 * half + 3) + 1)
            for c in range(2):
                cd(v.tensor_copy(conv_sig[:, c, 0:1], conv_sig[:, c, 0:1]), f"glu{c}" if half == 0 else None)
            split_lo(at, 2 * half + 1)

        at = Place("conv_a")
        steps = [0]

        def taps(t, n0, n1):
            for k in range(n0, n1):
                shifted = glu[:, t, k:k + SEQ]
                w = g_col("conv_b_w", t * TAPS_B + k)
                if k == 0:
                    ins = v.tensor_scalar(z[:, t, :], shifted, w, g_col("conv_b_bias", t), ALU.mult, ALU.add)
                else:
                    dve.wait_ge(conv_step, steps[0])
                    ins = stt(z[:, t, :], shifted, w, z[:, t, :], ALU.mult, ALU.add)
                ins.then_inc(conv_step, 1)
                steps[0] += 1

        pieces = [(t, n, min(n + 11, TAPS_B)) for t in range(CT) for n in range(0, TAPS_B, 11)]
        per = 2
        for half in range(2):
            o = 6 * half
            for c in range(2):
                strips(at, o + c)
                v.tensor_copy(wide(c_in[:, c, :]), strip_view(at.slot(o + c), FULL)).then_inc(strip_free, 1)
            split_lo(at, 3 * half)
            for x in pieces[:per]:
                taps(*x)
            pieces = pieces[per:]
            dve.wait_ge(strip_free, at.strip(o + 1) + 1)
            for c in range(2):
                strips(at, o + 2 + c)
                v.tensor_tensor(wide(u_in[:, c, :]), wide(c_in[:, c, :]), strip_view(at.slot(o + 2 + c), FULL),
                                ALU.mult).then_inc(strip_free, 1)
            split_lo(at, 3 * half + 1)
            dve.wait_ge(strip_free, at.strip(o + 3) + 1)
            for c in range(2):
                for k in range(TAPS_A):
                    w = g_col("conv_a_w", (2 * half + c) * TAPS_A + k)
                    shifted = u_in[:, c, META - (TAPS_A - 1) + k:META - (TAPS_A - 1) + k + SEQ]
                    if k == 0:
                        cd(v.tensor_scalar(c_in[:, c, 0:SEQ], shifted, w, None, ALU.mult))
                    else:
                        last()
                        cd(stt(c_in[:, c, 0:SEQ], shifted, w, c_in[:, c, 0:SEQ], ALU.mult, ALU.add))
            last()
            for c in range(2):
                strips(at, o + 4 + c)
                v.tensor_tensor(c_in[:, c, 0:SEQ], c_in[:, c, 0:SEQ], strip_view(at.slot(o + 4 + c), SEQ),
                                ALU.mult).then_inc(strip_free, 1)
            dve.wait_ge(strip_free, at.strip(o + 5) + 1)
            for c in range(2):
                cd(v.tensor_copy(y2_hi[:, 2 * half + c, :], c_in[:, c, 0:SEQ]))
                last()
                cd(v.tensor_tensor(y2_lo[:, 2 * half + c, :], c_in[:, c, 0:SEQ],
                                   as_f32(y2_hi[:, 2 * half + c, :]), ALU.subtract))
            split_lo(at, 3 * half + 2)
            for x in pieces[:per]:
                taps(*x)
            pieces = pieces[per:]
        for x in pieces:
            taps(*x)
        dve.wait_ge(conv_step, steps[0])
        cd(v.tensor_tensor(sq_sum[:, 0:SEQ], z[:, 0, :], z[:, 1, :], ALU.add))
        for t in range(2, CT):
            last()
            cd(v.tensor_tensor(sq_sum[:, 0:SEQ], sq_sum[:, 0:SEQ], z[:, t, :], ALU.add),
               "z_sum" if t == CT - 1 else None)
        dve.wait_ge(c_pe, 1)
        for t in range(CT):
            cd(stt(z[:, t, :], psum[:, 4, :], -1.0 / WB, z[:, t, :], ALU.mult, ALU.add), f"zc{t}")
        for t in range(CT):
            dve.wait_ge(c_act, A2["sq"] + t)
            if t:
                last()
            cd(v.tensor_copy(sq_sum[:, 0:SEQ], sq[:, 0, 0:SEQ]) if t == 0 else
               v.tensor_tensor(sq_sum[:, 0:SEQ], sq_sum[:, 0:SEQ], sq[:, t % 2, 0:SEQ], ALU.add),
               f"zsq{t}")
        dve.wait_ge(c_act, A2["std"])
        for t in range(CT):
            cd(v.tensor_tensor(z[:, t, :], z[:, t, :], std[:, 0:SEQ], ALU.mult), f"zn{t}")
        for t in range(CT):
            dve.wait_ge(c_act, A2[f"e{t}"])
            cd(v.tensor_tensor(z[:, t, :], z[:, t, :], normed[:, t % 2, 0:SEQ], ALU.mult), f"yb{t}")
        for t in range(CT):
            dve.wait_ge(c_act, A2[f"yh{t}"])
            cd(v.tensor_tensor(y2_lo[:, CT + t, :], z[:, t, :], as_f32(y2_hi[:, CT + t, :]), ALU.subtract),
               "y_lo" if t == CT - 1 else None)
        out_product("w_out2")
        norm_add(5, 2, "post_mix2")
        norm_split(6, 3, SEQ, "pre_ffn2")
        ffn("_2", 1)
        norm_add(7, 3, "post_ffn2")

    ctx.close()


def second_mixer_steps():
    d, n = {}, 1
    n += 2
    d["glu0"], d["glu1"] = n - 1, n
    n += 2
    n += 2 * (2 * TAPS_A + 4)
    n += CT - 1
    d["z_sum"] = n
    for t in range(CT):
        n += 1
        d[f"zc{t}"] = n
    for t in range(CT):
        n += 1
        d[f"zsq{t}"] = n
    d["z_sq_sum"] = n
    for t in range(CT):
        n += 1
        d[f"zn{t}"] = n
    for t in range(CT):
        n += 1
        d[f"yb{t}"] = n
    d["y_lo"] = n + CT
    a, n = {}, 0
    a["sq"] = n + 1
    n += CT + 2
    a["std"] = n
    for t in range(CT):
        n += 2
        a[f"e{t}"] = n
    for t in range(CT):
        n += 1
        a[f"yh{t}"] = n
    return d, a


C2, A2 = second_mixer_steps()

C_IDENT, C_BLOCKED, C_TRI, C_ALL, C_TRI_META, C_ROWS = 0, 1, 2, 3, 4, 5
N_CMAT = 9

VEC, VEC_COLS = {}, 0
for _name, _n in (("norm_eps", 1), ("gn_eps", 1), ("ln_eps", 1), ("one", 1), ("pre_mix", 8), ("post_mix", 8),
                  ("pre_ffn", 8), ("post_ffn", 8), ("pre_mix2", 8), ("post_mix2", 8), ("pre_ffn2", 8),
                  ("post_ffn2", 8), ("conv_a_w", CT * TAPS_A), ("conv_b_w", CT * TAPS_B), ("conv_b_bias", CT),
                  ("ln_gain", CT), ("ln_bias", CT)):
    VEC[_name] = VEC_COLS
    VEC_COLS += _n


def constants():
    i = np.arange(P)
    ones = np.ones((P, P), np.float32)
    ident = np.eye(P, dtype=np.float32)
    mask_k = np.zeros((P, 2, 4, 32), np.float32)
    mask_v = np.zeros((P, 2, P), np.float32)
    for t in range(2):
        for r in range(2):
            j = 2 * t + r
            mask_k[64 * r:64 * r + 64, t, j, 0:META] = 1
            mask_v[32 * j:32 * j + META, t, 64 * r:64 * r + 64] = 1
    half = RET_DK // 2
    inv = np.float32(10000.0) ** (-np.arange(half, dtype=np.float32) / np.float32(half))
    ang = (np.arange(FULL, dtype=np.float32)[None, :] * inv[:, None]).astype(np.float32)
    cos, sin = np.cos(ang), np.sin(ang)
    cm = np.zeros((P, N_CMAT, P), np.float32)
    cm[:, C_IDENT] = ident
    cm[:, C_BLOCKED] = np.where(i[:, None] < i[None, :], 0.0, BLOCKED)
    cm[:, C_TRI] = np.where(i[:, None] >= i[None, :], -1.0, 0.0)
    cm[:, C_ALL] = -1.0
    same = (i[:, None] // 32 == i[None, :] // 32) & (i[:, None] % 32 < META)
    cm[:, C_TRI_META] = np.where(same & (i[:, None] >= i[None, :]), -1.0, 0.0)
    for j in range(4):
        cm[:, C_ROWS + j] = np.where(i[None, :] // 32 == j, -1.0, 0.0)
    consts = np.concatenate([ones, ident, mask_k.reshape(P, -1), mask_v.reshape(P, -1), cos, sin,
                             cm.reshape(P, -1)], axis=1).astype(np.float32)
    log_g = np.log1p(-(2.0 ** (-5.0 - np.arange(RET_HEADS))))
    scale = RET_DK ** -0.5
    dec = np.zeros((RET_HEADS, P, 2, SEQ))
    u = np.arange(SEQ)
    for n in range(RET_HEADS):
        diff = u[None, :] - i[:, None]
        dec[n, :, 0] = np.where(diff >= 0, np.exp(log_g[n] * np.maximum(diff, 0)), 0.0) * scale
        dec[n, :META, 1] = np.exp(log_g[n] * (u[None, :] + META - i[:META, None])) * scale
    return consts, dec.reshape(RET_HEADS, P, 2 * SEQ).astype(np.float32)


def lay_out(inp):
    def P_unit(w, c):
        return w[:, c:c + 256].reshape(8, P, 256).transpose(1, 0, 2).reshape(P, UNIT)

    def R_unit(w, r, c):
        return w[r:r + 512, c:c + 512].reshape(4, P, 512).transpose(1, 0, 2).reshape(P, UNIT)

    def D_unit(w, r):
        return w[r:r + 256, :].reshape(2, P, 1024).transpose(1, 0, 2).reshape(P, UNIT)

    w_in, w_ret, w_sb, w_out = (inp[n][0] for n in ("w_in", "w_ret_out", "w_sb_out", "w_out"))
    w_fi, w_fo, w_in2, w_out2 = (inp[n][0] for n in ("w_ffn_in", "w_ffn_out", "w_in_2", "w_out_2"))
    w_g, w_u, w_d = (inp[n][0] for n in ("w_gate_2", "w_up_2", "w_down_2"))
    rq, rk, rv, rg, sq, sk, sv, ga, gb = np.cumsum([0, 1024, 1024, 2048, 2048, 1024, 1024, 1024, 1024])
    L = []
    L += [P_unit(w_in, gb + 256 * k) for k in range(4)]
    for q in range(QUADS):
        L += [P_unit(w_in, o + 256 * q) for o in (sq, sk, sv)] + [D_unit(w_sb, 256 * q)]
    L += [P_unit(w_in, ga + 256 * k) for k in range(4)]
    for n in range(RET_HEADS):
        L += [P_unit(w_in, o + 256 * n) for o in (rq, rk)]
        if n:
            L += [R_unit(w_ret, 512 * (n - 1), c) for c in (0, 512)]
        L += [P_unit(w_in, o + 512 * n + c) for o in (rv, rg) for c in (0, 256)]
    L += [R_unit(w_ret, 512 * (RET_HEADS - 1), c) for c in (0, 512)]
    L += [P_unit(w_out, 256 * k) for k in range(4)]

    def ffn(g, go, u, uo, d):
        r = []
        for k in range(FF_PAIRS):
            r += [P_unit(g, go + 256 * k), P_unit(u, uo + 256 * k)]
            if k:
                r.append(D_unit(d, 256 * (k - 1)))
        return r + [D_unit(d, 256 * (FF_PAIRS - 1))]
    L += ffn(w_fi, 0, w_fi, D_FF, w_fo)
    for c in range(2):
        L += [P_unit(w_in2, 3 * WA + WB + 256 * c), P_unit(w_in2, 3 * WA + 256 * c)]
    for c in range(2):
        L += [P_unit(w_in2, o + 256 * c) for o in (WA, 2 * WA, 0)]
    L += [P_unit(w_out2, 256 * k) for k in range(4)]
    L += ffn(w_g, 0, w_u, 0, w_d)
    assert len(L) == N_UNITS
    units = np.stack(L)

    def tiles(a):
        n = a.shape[0]
        return a.T.reshape(-1, P, n).transpose(1, 0, 2).reshape(P, -1)
    xfm = tiles(np.concatenate([inp["meta_tokens"], inp["x"][0]], axis=0))
    meta2 = tiles(inp["meta_tokens_2"])
    col = lambda a: a.reshape(-1, P).T
    const = lambda x: np.full((P, 1), x, np.float32)
    taps = lambda w: w.T.reshape(CT, P, -1).transpose(1, 0, 2).reshape(P, -1)
    vecs = np.concatenate(
        [const(NORM_EPS), const(GN_EPS), const(LN_EPS), const(1.0)]
        + [col(inp[n][0]) for n in ("norm_mix_pre", "norm_mix_post", "norm_ffn_pre", "norm_ffn_post",
                                    "pre_mix_norm_2", "post_mix_norm_2", "pre_ffn_norm_2", "post_ffn_norm_2")]
        + [taps(inp["conv_a_w_2"][0]), taps(inp["conv_b_w_2"][0])]
        + [col(inp[n][0]) for n in ("conv_b_bias_2", "ln_b_gain_2", "ln_b_bias_2")], axis=1)
    consts, dec = constants()
    return dict(units=units, xfm=xfm, meta2=meta2, consts=consts, dec=dec, vecs=vecs)


def kernel(**inputs):
    import concourse.bacc as _bacc
    from concourse.bass_utils import run_bass_kernel_spmd as _run

    laid = lay_out({k: np.asarray(x) for k, x in inputs.items()})
    nc = _bacc.Bacc("TRN2", target_bir_lowering=False, num_devices=1)
    arrays, args = {}, []
    for name, a in laid.items():
        a = np.ascontiguousarray(a)
        arrays[f"in_{name}"] = a
        args.append(nc.dram_tensor(f"in_{name}", a.shape, mybir.dt.from_np(a.dtype), kind="ExternalInput").ap())
    args.append(nc.dram_tensor("out_0", (P, DT * SEQ), F32, kind="ExternalOutput").ap())
    build(nc, *args)
    r = _run(nc, [arrays], core_ids=[0])
    o = np.asarray(r.results[0]["out_0"])
    return o.reshape(P, DT, SEQ).transpose(2, 1, 0).reshape(1, SEQ, D)
```

```python
from contextlib import ExitStack

import numpy as np

import concourse.bass as bass
from concourse import mybir

F32 = mybir.dt.float32
F32R = mybir.dt.float32r
ACT = mybir.ActivationFunctionType
ALU = mybir.AluOpType

P = 128
D = 1024
DT = D // P
SEQ = 512
META = 16
FULL = META + SEQ
HALF = FULL // 2
UNIT = 2048
RET_HEADS, RET_DK, RET_DV = 4, 256, 512
QUADS = 4
SB_DH = 64
D_FF = 2816
FF_PAIRS = D_FF // 256
WA = WB = 512
CT = WA // P
TAPS_A, TAPS_B = 3, 31
NORM_EPS, GN_EPS, LN_EPS = 1e-6, 1e-5, 1e-5
BLOCKS = SEQ // P
KEY_OFF = [0, 512, 896, 1152]
KEY_LEN = [SEQ - P * b for b in range(BLOCKS)]
PACKED = sum(KEY_LEN)
KEY_BANK = [0, 1, 2, 2]
KEY_COL = [0, 0, 0, 256]
PARTS = [(0, 0, 512), (1, 512, 384), (2, 896, 384)]
BLOCKED = -(2.0 ** 100)

STRIPS = {"P": 2, "R": 4, "D": 8}


def plan():
    phases = [
        ("quad_start", "P"),
        ("quad_first", "PPP"),
        ("quads", "PPDP" * (QUADS - 2)),
        ("quad_last", "PPD"),
        ("quad_end", "D"),
        ("gate_b", "P" * 4),
        ("head0", "PP"),
        ("heads", "PPPPPPRR" * 3),
        ("head_last", "PPPP"),
        ("head_out", "RR"),
        ("gate_a", "P" * 4),
        ("w_out", "P" * 4),
        ("ffn0", "PP"),
        ("ffn", "PPDPPD" * 5),
        ("ffn_end", "D"),
        ("conv_b", "PPPP"),
        ("conv_a", "PPPPPP"),
        ("w_out2", "P" * 4),
        ("ffn0_2", "PP"),
        ("ffn_2", "PPDPPD" * 4),
        ("ffn_last_2", "PPDPPD"),
        ("ffn_end_2", "D"),
    ]
    start, u, s = {}, 0, 0
    for name, kinds in phases:
        start[name] = (u, s)
        u += len(kinds)
        s += sum(STRIPS[k] for k in kinds)
    return start, u, s


START, N_UNITS, N_STRIPS = plan()


class Place:

    def __init__(self, phase, i=0, per_u=0, per_s=0, depth=2, first=0):
        assert per_u % 2 == 0 and per_s % depth == 0
        self.depth = depth
        self.first = first
        self.u0, self.s0 = START[phase]
        self.i, self.per_u, self.per_s = i, per_u, per_s

    def unit(self, j):
        return self.u0 + j - self.per_u * self.first + self.per_u * self.i

    def ring(self, j):
        return (self.u0 + j) % 2

    def loads(self, j):
        return (self.u0 + j) // 2 + 1 - (self.per_u // 2) * self.first + (self.per_u // 2) * self.i

    def strip(self, j):
        return self.s0 + j - self.per_s * self.first + self.per_s * self.i

    def bank(self, j):
        return (self.s0 + j) % self.depth * (4 // self.depth)


class Steps:

    def __init__(self, sem, names):
        self.sem, self.names, self.n = sem, list(names), 0
        self.index = {x: k for k, x in enumerate(self.names)}
        assert len(self.index) == len(self.names)

    def at(self, name, i=0):
        return self.index[name] + 1 + len(self.names) * i

    def step(self, name):
        want = self.names[self.n % len(self.names)]
        assert name == want, (name, want)
        self.n += 1
        return self.sem, 1


def heads_of(names):
    return [f"{x}{j}" for j in range(4) for x in names]


def build(nc, units, xfm, meta2, consts, dec, vecs, out):
    ctx = ExitStack()

    def sb(name, shape, dt=F32, where=ctx):
        return where.enter_context(nc.sbuf_tensor(name, shape, dt))

    def sem(name):
        return ctx.enter_context(nc.semaphore(name))

    X_hi = sb("X_hi", [P, DT, FULL], F32R)
    X_lo = sb("X_lo", [P, DT, FULL], F32R)
    acc = sb("acc", [P, DT, SEQ])
    w_raw = [sb(f"w_raw{n}", [P, UNIT]) for n in range(2)]
    w_hi = [sb(f"w_hi{n}", [P, UNIT], F32R) for n in range(2)]
    w_lo = [sb(f"w_lo{n}", [P, UNIT], F32R) for n in range(2)]
    ones = sb("ones", [P, P])
    vec = sb("vec", [P, VEC_COLS])
    psum = ctx.enter_context(nc.psum_tensor("psum", [P, 8, 512], F32))

    rot = sb("rot", [P, 2, FULL])
    mixer = ExitStack()
    sig = sb("sig", [P, 2, FULL], where=mixer)

    quad = ExitStack()
    Q_hi = sb("Q_hi", [P, 2, SEQ], F32R, quad)
    Q_lo = sb("Q_lo", [P, 2, SEQ], F32R, quad)
    K_hi = sb("K_hi", [P, 2, SEQ], F32R, quad)
    K_lo = sb("K_lo", [P, 2, SEQ], F32R, quad)
    V_hi = sb("V_hi", [P, 2 * BLOCKS, 3, SB_DH], F32R, quad)
    V_lo = sb("V_lo", [P, 2 * BLOCKS, 3, SB_DH], F32R, quad)
    XM_hi = sb("XM_hi", [P, DT, P], F32R, quad)
    XM_lo = sb("XM_lo", [P, DT, P], F32R, quad)
    KM = sb("KM", [P, P], F32, quad)
    KM_hi = sb("KM_hi", [P, P], F32R, quad)
    KM_lo = sb("KM_lo", [P, P], F32R, quad)
    VM = sb("VM", [P, 2, P], F32, quad)
    VM_hi = sb("VM_hi", [P, 2, P], F32R, quad)
    VM_lo = sb("VM_lo", [P, 2, P], F32R, quad)
    sp = sb("sp", [P, PACKED], F32, quad)
    sp_hi = sb("sp_hi", [P, PACKED], F32R, quad)
    sp_lo = sb("sp_lo", [P, PACKED], F32R, quad)
    a_f = sb("a_f", [P, PACKED], F32, quad)
    a_hi = sb("a_hi", [P, PACKED], F32R, quad)
    a_lo = sb("a_lo", [P, PACKED], F32R, quad)
    m_f = sb("m_f", [P, SEQ], F32, quad)
    m_hi = sb("m_hi", [P, SEQ], F32R, quad)
    m_lo = sb("m_lo", [P, SEQ], F32R, quad)
    Y = sb("Y", [P, SEQ], F32, quad)
    Y_hi = sb("Y_hi", [P, 2, SEQ], F32R, quad)
    Y_lo = sb("Y_lo", [P, 2, SEQ], F32R, quad)
    cmat = sb("cmat", [P, N_CMAT, P], F32R, quad)
    mask_k = sb("mask_k", [P, 2, 4, 32], F32, quad)
    mask_v = sb("mask_v", [P, 2, P], F32, quad)
    quad.close()

    head = ExitStack()
    ret = sb("ret", [P, DT, SEQ], F32, head)
    RQ_hi = sb("RQ_hi", [P, 2, SEQ], F32R, head)
    RQ_lo = sb("RQ_lo", [P, 2, SEQ], F32R, head)
    RK_hi = sb("RK_hi", [P, 2, FULL], F32R, head)
    RK_lo = sb("RK_lo", [P, 2, FULL], F32R, head)
    turned = sb("turned", [P, 2, FULL], F32, head)
    RY = sb("RY", [P, 4, SEQ], F32, head)
    VZ_hi = sb("VZ_hi", [P, 4, SEQ], F32R, head)
    VZ_lo = sb("VZ_lo", [P, 4, SEQ], F32R, head)
    RVM_hi = sb("RVM_hi", [META, SEQ], F32R, head)
    RVM_lo = sb("RVM_lo", [META, SEQ], F32R, head)
    S_f = sb("S_f", [P, PACKED], F32, head)
    S_hi = sb("S_hi", [P, PACKED], F32R, head)
    S_lo = sb("S_lo", [P, PACKED], F32R, head)
    SM_f = sb("SM_f", [META, SEQ], F32, head)
    SM_hi = sb("SM_hi", [META, SEQ], F32R, head)
    SM_lo = sb("SM_lo", [META, SEQ], F32R, head)
    decay = sb("decay", [P, 2, SEQ], F32, head)
    r_std = sb("r_std", [P, SEQ], F32, head)
    silu_g = sb("silu_g", [P, 4, SEQ], F32, head)
    head.close()
    mixer.close()

    h = sb("h", [P, DT, FULL])
    std = sb("std", [P, FULL])
    sq = sb("sq", [P, 2, FULL])
    sq_sum = sb("sq_sum", [P, FULL])
    normed = sb("normed", [P, 2, FULL])
    meta2_f = sb("meta2_f", [P, DT, META])
    ffns = ExitStack()
    M_hi = sb("M_hi", [P, 2, 2, SEQ], F32R, ffns)
    M_lo = sb("M_lo", [P, 2, 2, SEQ], F32R, ffns)
    silu_a = sb("silu_a", [P, 2, SEQ], F32, ffns)
    ffns.close()
    conv_sig = sb("conv_sig", [P, 2, FULL])
    glu = sb("glu", [P, CT, TAPS_B - 1 - META + FULL])
    c_in = sb("c_in", [P, 2, FULL])
    u_in = sb("u_in", [P, 2, FULL])
    z = sb("z", [P, CT, SEQ])
    y2_hi = sb("y2_hi", [P, DT, SEQ], F32R)
    y2_lo = sb("y2_lo", [P, DT, SEQ], F32R)

    consts_in = sem("consts_in")
    cmat_ready = sem("cmat_ready")
    w_loaded = [sem("w_loaded0"), sem("w_loaded1")]
    w_hi_ready = sem("w_hi_ready")
    w_lo_ready = sem("w_lo_ready")
    strip_done = sem("strip_done")
    strip_free = sem("strip_free")
    x_loaded = sem("x_loaded")
    decay_loaded = sem("decay_loaded")
    memset_done = sem("memset_done")
    stored = sem("stored")

    sq_done = sem("sq_done")
    sq_added = sem("sq_added")
    sum_done = sem("sum_done")
    std_ready = sem("std_ready")
    norm_scaled = sem("norm_scaled")
    x_hi_ready = sem("x_hi_ready")
    x_lo_ready = sem("x_lo_ready")
    post_done = sem("post_done")

    qk_act = Steps(sem("qk_act"), ["K_hi", "KM_hi", "Q_hi"])
    qk_dve = Steps(sem("qk_dve"), ["K_lo", "KM_lo"])
    mk_act = Steps(sem("mk_act"), ["m_abs", "m_exp", "m_ln", "m_hi", "am_exp", "am_hi"])
    mk_dve = Steps(sem("mk_dve"), ["m_sp", "m_lo", "am_lo"])
    mk_pe = Steps(sem("mk_pe"), ["m_scores", "m_rows", "y_meta"])
    y_out = sem("y_out")
    y_hi_ready = sem("y_hi_ready")
    y_lo_ready = sem("y_lo_ready")
    v_act = Steps(sem("v_act"), ["V_hi0", "VM_hi", "V_hi1"])
    v_dve = Steps(sem("v_dve"), ["V_lo0", "VM_lo"])
    hd_act = Steps(sem("hd_act"), ["abs1", "abs2", "abs0", "exp1", "exp0", "ln1", "ln0", "hi1", "hi0",
                                   "a_part0", "a_part1", "a_part2", "a_hi"])
    hd_dve = Steps(sem("hd_dve"), ["sp1", "sp2", "sp0", "sp_lo1", "sp_lo0", "a_lo"])
    hd_pe = Steps(sem("hd_pe"), ["scores", "logs"])
    t_act = Steps(sem("t_act"), ["RQ_hi0", "RQ_hi1", "RK_hi0", "RK_hi1"])
    t_dve = Steps(sem("t_dve"), ["q_cos", "q_sin", "q_r1", "q_r2", "q_lo",
                                 "k_cos", "k_sin", "k_r1", "k_r2", "k_lo"])
    r_act = Steps(sem("r_act"), ["V_hi0", "VM_hi0", "V_hi1", "V_hi2", "VM_hi1", "V_hi3",
                                 "S_hi", "SM_hi", "g_sig0", "g_sig1", "g_sig2", "g_sig3",
                                 "y_sq0", "y_sq1", "y_sq2", "y_sq3", "ln", "std",
                                 "z_hi0", "z_hi1", "z_hi2", "z_hi3"])
    r_dve = Steps(sem("r_dve"), ["V_lo0", "V_lo2", "S0", "S1", "S2", "S3", "SM", "S_lo", "SM_lo",
                                 "y0", "y1", "y2", "y3", "ys1", "ys2", "ys3",
                                 "yc0", "yc1", "yc2", "yc3", "sqs1", "sqs2", "sqs3", "yg",
                                 "z0", "z1", "z_lo0", "z2", "z_lo1", "z3", "z_lo2", "z_lo3"])
    r_pe = Steps(sem("r_pe"), ["scores", "y", "mean", "var"])
    mixed = sem("mixed")
    quad_ready = sem("quad_ready")
    gate_used = sem("gate_used")
    m_split_hi = sem("m_split_hi")
    m_split_lo = sem("m_split_lo")
    mix_out = sem("mix_out")
    f_act = Steps(sem("f_act"), ["sig0", "sig1", "M_hi"])
    f_dve = Steps(sem("f_dve"), ["prod", "M_lo"])
    acc_zero = sem("acc_zero")
    f_added = sem("f_added")
    ret_zero = sem("ret_zero")
    c_act = sem("c_act")
    c_dve = sem("c_dve")
    c_pe = sem("c_pe")
    conv_step = sem("conv_step")

    def ring3(u_hi_or_lo, kind):
        k, c = {"P": (8, 256), "R": (4, 512), "D": (2, 1024)}[kind]
        return u_hi_or_lo[:, :].rearrange("p (k c) -> p k c", k=k, c=c)

    def strip_view(bank, width):
        if width == FULL:
            return psum[:, bank:bank + 2, 0:HALF]
        return psum[:, bank, 0:SEQ]

    def wide(ap):
        return ap.rearrange("p (a b) -> p a b", a=2)

    def as_f32(ap):
        return ap.bitcast(F32)

    def g_col(name, k):
        o = VEC[name] + k
        return vec[:, o:o + 1]

    def loop(eng, n, body, peel=0):
        for i in range(peel):
            body(i)
        if peel == n:
            return
        with eng.Fori(peel, n) as i:
            body(i)

    block = ctx.enter_context(nc.Block())

    @block.sync
    def _(sync):
        for dst, src in ((vec[:, :], vecs), (ones[:, :], consts[:, 0:P]),
                         (mask_k[:, :, :, :].rearrange("p a b c -> p (a b c)"), consts[:, 2 * P:4 * P]),
                         (mask_v[:, :, :].rearrange("p a b -> p (a b)"), consts[:, 4 * P:6 * P]),
                         (rot[:, :, :].rearrange("p a b -> p (a b)"), consts[:, 6 * P:6 * P + 2 * FULL]),
                         (w_raw[0][:, 0:N_CMAT * P], consts[:, 6 * P + 2 * FULL:])):
            sync.dma_start(dst, src).then_inc(consts_in, 16)
        sync.dma_start(h[:, :, :].rearrange("p a b -> p (a b)"), xfm).then_inc(x_loaded, 16)
        sync.wait_ge(cmat_ready, 1)
        for u in range(2):
            sync.dma_start(w_raw[u][:, :], units[u, :, :]).then_inc(w_loaded[u], 16)

        def load(u, slot):
            sync.wait_ge(w_hi_ready, u - 1)
            sync.wait_ge(w_lo_ready, u - 1)
            sync.dma_start(w_raw[slot][:, :], units[bass.ds(u, 1), :, :].rearrange("a p c -> (a p) c"))\
                .then_inc(w_loaded[slot], 16)

        def load_decay(n):
            if n > 0:
                sync.wait_ge(r_dve.sem, r_dve.at("SM", n - 1))
            sync.dma_start(decay[:, :, :].rearrange("p a b -> p (a b)"), dec[n, :, :]).then_inc(decay_loaded, 16)

        def loads(first, last):
            n = (last - first) // 2
            if last <= first:
                return

            def body(i):
                for slot in range(2):
                    load(first + 2 * i + slot, (first + slot) % 2)
            loop(sync, n, body)
            if (last - first) % 2:
                load(last - 1, (last - 1) % 2)

        loads(2, START["gate_b"][0] + 2)
        sync.wait_ge(strip_free, START["gate_b"][1])
        load_decay(0)
        loads(START["gate_b"][0] + 2, START["heads"][0] + 6)
        for n in range(1, RET_HEADS):
            load_decay(n)
            loads(START["heads"][0] + 8 * (n - 1) + 6, START["heads"][0] + 8 * n + (6 if n < RET_HEADS - 1 else 2))
        loads(START["head_last"][0] + 2, START["ffn0"][0] - 2)
        sync.wait_ge(m_split_lo, DT)
        sync.dma_start(h[:, :, :].rearrange("p a b -> p (a b)"), xfm).then_inc(x_loaded, 16)
        sync.dma_start(meta2_f[:, :, :].rearrange("p a b -> p (a b)"), meta2).then_inc(x_loaded, 16)
        loads(START["ffn0"][0] - 2, N_UNITS)
        sync.wait_ge(post_done, 4 * DT)
        sync.dma_start(out.rearrange("p (a b) -> p a b", a=DT), h[:, :, META:FULL]).then_inc(stored, 16)
        sync.wait_ge(stored, 16)

    @block.tensor
    def _(pe):
        def mm3(dst, w2, x2, first, last, sig=None):
            nc.tensor.matmul(dst, w2[0], x2[0], start=first, stop=False, skip_group_check=True)
            nc.tensor.matmul(dst, w2[0], x2[1], start=False, stop=False, skip_group_check=True)
            m = nc.tensor.matmul(dst, w2[1], x2[0], start=False, stop=last, skip_group_check=True)
            if sig:
                m.then_inc(*sig)

        def take(at, s):
            if not (type(at.strip(s)) is int and at.strip(s) < at.depth):
                pe.wait_ge(strip_free, at.strip(s) + 1 - at.depth)

        def unit(at, j, s, kind, width, x, cs=None):
            pe.wait_ge(w_lo_ready, at.unit(j) + 1)
            w = [ring3(r[at.ring(j)], kind) for r in (w_hi, w_lo)]
            tiles = {"P": 8, "R": 4, "D": 2}[kind]
            for c in range(STRIPS[kind]) if cs is None else cs:
                bank = at.bank(s + c)
                take(at, s + c)
                halves = [(0, HALF), (HALF, FULL)] if width == FULL else [(META, FULL)]
                for k in range(tiles):
                    for n, (a, b) in enumerate(halves):
                        end = k == tiles - 1 and n == len(halves) - 1
                        mm3(psum[:, bank + n, 0:b - a], [y[:, k, c * P:(c + 1) * P] for y in w], x(k, a, b),
                            k == 0, k == tiles - 1, (strip_done, 1) if end else None)

        def from_x(k, a, b):
            return X_hi[:, k, a:b], X_lo[:, k, a:b]

        def seq_of(hi, lo):
            return lambda k, a, b: (hi[:, k, a - META:b - META], lo[:, k, a - META:b - META])

        def sums(n, width):
            pe.wait_ge(sq_added, DT * (n + 1))
            for hf in range(2):
                w = width // 2
                m = nc.tensor.matmul(psum[:, 6 + hf, 0:w], ones[:, :], sq_sum[:, hf * w:(hf + 1) * w],
                                     start=True, stop=True)
            m.then_inc(sum_done, 1)

        pe.wait_ge(consts_in, 16 * 6)
        sums(0, FULL)
        pe.wait_ge(x_lo_ready, DT)

        def split(hi, lo, *ix):
            return hi[ix], lo[ix]

        ALL = slice(None)

        def value_strip(at, j, s, half, meta):
            pe.wait_ge(w_lo_ready, at.unit(j) + 1)
            take(at, s)
            w = [ring3(r[at.ring(j)], "P") for r in (w_hi, w_lo)]
            parts = [(0, n * 256, split(X_hi, X_lo, ALL, ALL, slice(META + b * P, META + (b + 1) * P)))
                     for n, b in enumerate((2 * half, 2 * half + 1))]
            if half == 0:
                parts.append((1, 0, meta))
            for nb, col, x in parts:
                for k in range(DT):
                    end = x is parts[-1][2] and k == DT - 1
                    mm3(psum[:, at.bank(s) + nb, col:col + 256], (x[0][:, k], x[1][:, k]),
                        (w[0][:, k, :], w[1][:, k, :]), k == 0 and col == 0, k == DT - 1,
                        (strip_done, 1) if end else None)

        def key_strip(at, j, s):
            pe.wait_ge(w_lo_ready, at.unit(j) + 1)
            take(at, s)
            w = [ring3(r[at.ring(j)], "P") for r in (w_hi, w_lo)]
            for k in range(DT):
                for nb, a, b in ((0, META, FULL), (1, 0, META)):
                    mm3(psum[:, at.bank(s) + nb, 0:b - a], [y[:, k, 0:P] for y in w], from_x(k, a, b),
                        k == 0, k == DT - 1, (strip_done, 1) if nb and k == DT - 1 else None)

        def scores(t, r, at, s, g):
            pe.wait_ge(strip_free, at.strip(s) + 1)
            if not (type(g) is int and g == 0):
                pe.wait_ge(hd_act.sem, hd_act.at("a_part2", g - 1))
            rows = slice(SB_DH * r, SB_DH * (r + 1))
            for b in range(BLOCKS):
                dst = psum[:, 4 + KEY_BANK[b], KEY_COL[b]:KEY_COL[b] + KEY_LEN[b]]
                mm3(dst, split(K_hi, K_lo, rows, t, slice(b * P, (b + 1) * P)),
                    split(Q_hi, Q_lo, rows, t, slice(b * P, SEQ)), b < 3, False)
                m = nc.tensor.matmul(psum[:, 4 + KEY_BANK[b], KEY_COL[b]:KEY_COL[b] + P],
                                     cmat[:, C_IDENT, :], cmat[:, C_BLOCKED, :], start=False, stop=False,
                                     skip_group_check=True)
            m.then_inc(*hd_pe.step("scores"))

        def logs(g):
            pe.wait_ge(hd_dve.sem, hd_dve.at("sp_lo0", g))
            for b in range(BLOCKS):
                for b2 in range(b, BLOCKS):
                    c0 = KEY_COL[b] + P * (b2 - b)
                    for x in (sp_hi, sp_lo):
                        m = nc.tensor.matmul(psum[:, 4 + KEY_BANK[b], c0:c0 + KEY_LEN[b2]],
                                             cmat[:, C_TRI if b2 == b else C_ALL, :],
                                             x[:, KEY_OFF[b2]:KEY_OFF[b2] + KEY_LEN[b2]],
                                             start=False, stop=False, skip_group_check=True)
            m.then_inc(*hd_pe.step("logs"))

        def meta_scores(t, p):
            pe.wait_ge(qk_dve.sem, qk_dve.at("KM_lo", p))
            mm3(psum[:, 7, :], (KM_hi[:, :], KM_lo[:, :]), split(Q_hi, Q_lo, ALL, t, ALL), True, False,
                mk_pe.step("m_scores"))

        def meta_logs(r, p):
            if r == 0:
                pe.wait_ge(mk_dve.sem, mk_dve.at("m_lo", p))
                for x in (m_hi, m_lo):
                    nc.tensor.matmul(psum[:, 7, :], cmat[:, C_TRI_META, :], x[:, :], start=False, stop=False,
                                     skip_group_check=True)
            for b in range(BLOCKS):
                for x in (sp_hi, sp_lo):
                    m = nc.tensor.matmul(psum[:, 7, b * P:SEQ], cmat[:, C_ROWS + r, :],
                                         x[:, KEY_OFF[b]:KEY_OFF[b] + KEY_LEN[b]],
                                         start=False, stop=False, skip_group_check=True)
            if r == 1:
                m.then_inc(*mk_pe.step("m_rows"))

        def outputs(t, r, g, p):
            pe.wait_ge(hd_dve.sem, hd_dve.at("a_lo", g))
            if r == 0 and not (type(p) is int and p == 0):
                pe.wait_ge(y_out, p)
            for b in range(BLOCKS):
                vw = [x[:, 2 * b + t, r:r + 2, :].rearrange("p a c -> p (a c)") for x in (V_hi, V_lo)]
                mm3(psum[:, 3, b * P:SEQ], vw,
                    split(a_hi, a_lo, ALL, slice(KEY_OFF[b], KEY_OFF[b] + KEY_LEN[b])),
                    r == 0 and b == 0, False)

        def meta_outputs(t, p):
            pe.wait_ge(mk_dve.sem, mk_dve.at("am_lo", p))
            mm3(psum[:, 3, :], split(VM_hi, VM_lo, ALL, t, ALL), (m_hi[:, :], m_lo[:, :]), False, True,
                mk_pe.step("y_meta"))

        def quad_body(at, i, has_d, has_next):
            g, p = 4 * i, 2 * i
            dj, ds = 2, 4
            nj, ns = (3, 12) if has_d else (2, 4)
            value_strip(at, 0, 0, 0, (XM_hi, XM_lo))
            logs(g)
            value_strip(at, 0, 1, 1, None)
            meta_logs(0, p)
            scores(0, 1, at, 1, g + 1)
            pe.wait_ge(v_dve.sem, v_dve.at("VM_lo", i))
            pe.wait_ge(strip_free, at.strip(1) + 1)
            outputs(0, 0, g, p)
            key_strip(at, 1, 2)
            logs(g + 1)
            unit(at, 1, 2, "P", SEQ, from_x, [1])
            meta_logs(1, p)
            outputs(0, 1, g + 1, p)
            scores(1, 0, at, 3, g + 2)
            meta_outputs(0, p)
            meta_scores(1, p + 1)
            y = seq_of(Y_hi, Y_lo)
            if has_d:
                pe.wait_ge(y_lo_ready, p)
                unit(at, dj, ds, "D", SEQ, y, range(4))
            logs(g + 2)
            if has_d:
                unit(at, dj, ds, "D", SEQ, y, range(4, 8))
            meta_logs(0, p + 1)
            scores(1, 1, at, 3, g + 3)
            outputs(1, 0, g + 2, p + 1)
            if has_next:
                key_strip(at, nj, ns)
            logs(g + 3)
            if has_next:
                unit(at, nj, ns, "P", SEQ, from_x, [1])
            meta_logs(1, p + 1)
            outputs(1, 1, g + 3, p + 1)
            if has_next:
                scores(0, 0, at, ns + 1, g + 4)
            meta_outputs(1, p + 1)
            if has_next:
                meta_scores(0, p + 2)

        pe.wait_ge(cmat_ready, 1)
        pe.wait_ge(quad_ready, 4)
        at = Place("quad_start")
        key_strip(at, 0, 0)
        unit(at, 0, 0, "P", SEQ, from_x, [1])
        scores(0, 0, at, 1, 0)
        meta_scores(0, 0)
        quad_body(Place("quad_first"), 0, False, True)
        with pe.Fori(1, QUADS - 1) as i:
            quad_body(Place("quads", i, 4, 14, first=1), i, True, True)
        quad_body(Place("quad_last"), QUADS - 1, True, False)
        pe.wait_ge(y_lo_ready, 2 * QUADS)
        unit(Place("quad_end"), 0, 0, "D", SEQ, seq_of(Y_hi, Y_lo))

        def gates(phase):
            def body(i):
                at = Place(phase, i, 2, 4)
                for j in range(2):
                    unit(at, j, 2 * j, "P", SEQ, from_x)
            loop(pe, 2, body)

        gates("gate_b")

        def ret_scores(i):
            pe.wait_ge(t_dve.sem, t_dve.at("k_lo", i))
            for b in range(BLOCKS):
                for t in range(2):
                    mm3(psum[:, 4 + KEY_BANK[b], KEY_COL[b]:KEY_COL[b] + KEY_LEN[b]],
                        split(RK_hi, RK_lo, ALL, t, slice(META + b * P, META + (b + 1) * P)),
                        split(RQ_hi, RQ_lo, ALL, t, slice(b * P, SEQ)), t == 0 and b < 3, t == 1)
            for t in range(2):
                mm3(psum[:, 7, :], split(RK_hi, RK_lo, ALL, t, slice(0, P)),
                    split(RQ_hi, RQ_lo, ALL, t, ALL), t == 0, t == 1,
                    r_pe.step("scores") if t else None)

        def mean():
            nc.tensor.matmul(psum[:, 4, :], ones[:, :], S_f[:, 0:SEQ], start=True, stop=True)\
                .then_inc(*r_pe.step("mean"))

        def var():
            nc.tensor.matmul(psum[:, 5, :], ones[:, :], S_f[:, 0:SEQ], start=True, stop=True)\
                .then_inc(*r_pe.step("var"))

        plain_meta = [x[:, :, 0:P] for x in (X_hi, X_lo)]

        def head_body(at, i, has_next):
            for n in range(2):
                for half in range(2):
                    value_strip(at, n, 2 * n + half, half, plain_meta)
            for n in range(2):
                unit(at, 2 + n, 4 + 2 * n, "P", SEQ, from_x)
            pe.wait_ge(r_dve.sem, r_dve.at("SM_lo", i))
            for e in range(4):
                for b in range(BLOCKS):
                    mm3(psum[:, 4 + e, b * P:SEQ],
                        split(VZ_hi, VZ_lo, ALL, b, slice(e * P, (e + 1) * P)),
                        split(S_hi, S_lo, ALL, slice(KEY_OFF[b], KEY_OFF[b] + KEY_LEN[b])),
                        b == 0, False)
                mm3(psum[:, 4 + e, :], split(RVM_hi, RVM_lo, ALL, slice(e * P, (e + 1) * P)),
                    (SM_hi[:, :], SM_lo[:, :]), False, True, r_pe.step("y") if e == 3 else None)
            if has_next:
                unit(at, 4, 8, "P", SEQ, from_x, [0])
            pe.wait_ge(r_dve.sem, r_dve.at("ys3", i))
            mean()
            if has_next:
                unit(at, 4, 8, "P", SEQ, from_x, [1])
                unit(at, 5, 10, "P", FULL, from_x, [0])
            pe.wait_ge(r_dve.sem, r_dve.at("sqs3", i))
            var()
            if has_next:
                unit(at, 5, 10, "P", FULL, from_x, [1])
                out_units(at, 6, 12, i)
                ret_scores(i + 1)

        def out_units(at, j, s, i):
            pe.wait_ge(r_dve.sem, r_dve.at("z_lo3", i))
            for n in range(2):
                unit(at, j + n, s + 4 * n, "R", SEQ, seq_of(VZ_hi, VZ_lo))

        at = Place("head0")
        unit(at, 0, 0, "P", SEQ, from_x)
        unit(at, 1, 2, "P", FULL, from_x)
        ret_scores(0)
        loop(pe, RET_HEADS - 1, lambda i: head_body(Place("heads", i, 8, 20), i, True))
        head_body(Place("head_last"), RET_HEADS - 1, False)
        out_units(Place("head_out"), 0, 0, RET_HEADS - 1)
        gates("gate_a")

        def out_product(phase, x):
            def body(i):
                at = Place(phase, i, 2, 4)
                for j in range(2):
                    unit(at, j, 2 * j, "P", SEQ, x)
            loop(pe, 2, body)

        pe.wait_ge(m_split_lo, DT)
        out_product("w_out", from_x)
        sums(1, SEQ)
        sums(2, SEQ)

        def ffn(tag, n):
            def up(at, j, s):
                unit(at, j, s, "P", SEQ, from_x)
                unit(at, j + 1, s + 2, "P", SEQ, from_x)

            def down(at, j, s, i, slot):
                pe.wait_ge(f_dve.sem, f_dve.at("M_lo", i))
                unit(at, j, s, "D", SEQ, lambda k, a, b: (M_hi[:, slot, k, :], M_lo[:, slot, k, :]))

            def two(at, i0):
                for m in range(2):
                    up(at, 3 * m, 12 * m)
                    down(at, 3 * m + 2, 12 * m + 4, i0 + m, m)
            base = FF_PAIRS * n
            pe.wait_ge(acc_zero, n + 1)
            up(Place("ffn0" + tag, depth=4), 0, 0)
            rounds = 5 if n == 0 else 4
            loop(pe, rounds, lambda i: two(Place("ffn" + tag, i, 6, 24, 4), base + 2 * i))
            if n:
                two(Place("ffn_last" + tag, depth=4), base + 2 * rounds)
            down(Place("ffn_end" + tag, depth=4), 0, 0, base + FF_PAIRS - 1, 0)

        pe.wait_ge(x_lo_ready, 2 * DT)
        ffn("", 0)
        sums(3, SEQ)
        sums(4, FULL)
        pe.wait_ge(x_lo_ready, 3 * DT)
        at = Place("conv_b")
        for j in range(4):
            unit(at, j, 2 * j, "P", FULL, from_x)
        at = Place("conv_a")
        for j in range(6):
            unit(at, j, 2 * j, "P", FULL if j % 3 < 2 else SEQ, from_x)
        pe.wait_ge(c_dve, C2["z_sum"])
        nc.tensor.matmul(psum[:, 4, :], ones[:, :], sq_sum[:, 0:SEQ], start=True, stop=True).then_inc(c_pe, 1)
        pe.wait_ge(c_dve, C2["z_sq_sum"])
        nc.tensor.matmul(psum[:, 5, :], ones[:, :], sq_sum[:, 0:SEQ], start=True, stop=True).then_inc(c_pe, 1)
        pe.wait_ge(c_dve, C2["y_lo"])
        out_product("w_out2", seq_of(y2_hi, y2_lo))
        sums(5, SEQ)
        sums(6, SEQ)
        pe.wait_ge(x_lo_ready, 4 * DT)
        ffn("_2", 1)
        sums(7, SEQ)

    @block.scalar
    def _(act):
        def a(out_, in_, f, **kw):
            return nc.scalar.activation(out_, in_, f, **kw)

        def split_hi(at, j):
            act.wait_ge(w_loaded[at.ring(j)], 16 * (at.loads(j) + 1))
            a(w_hi[at.ring(j)][:, :], w_raw[at.ring(j)][:, :], ACT.Copy).then_inc(w_hi_ready, 1)

        def strips(at, s, n=1):
            act.wait_ge(strip_done, at.strip(s) + n)

        def norm(n, src, width, k_split=None):
            use("ln, exp")
            for k in range(DT):
                if DT * n + k >= 2:
                    act.wait_ge(sq_added, DT * n + k - 1)
                src(k)
            act.wait_ge(sum_done, n + 1)
            if width == FULL:
                dst, ps = wide(std[:, :]), psum[:, 6:8, 0:HALF]
            else:
                dst, ps = std[:, 0:SEQ].rearrange("p (a b) -> p a b", a=2), psum[:, 6:8, 0:SEQ // 2]
            if n:
                act.wait_ge(norm_scaled, DT * n)
            a(dst, ps, ACT.Ln, scale=1.0 / D, bias=g_col("norm_eps", 0)).then_inc(std_ready, 1)
            act.wait_ge(std_ready, 2 * n + 1)
            a(dst, dst, ACT.Exp, scale=-0.5).then_inc(std_ready, 1)
            if k_split is not None:
                for k in range(DT):
                    act.wait_ge(norm_scaled, DT * n + k + 1)
                    a(X_hi[:, k, 0:width] if width == FULL else X_hi[:, k, META:FULL],
                      normed[:, k % 2, 0:width], ACT.Copy).then_inc(x_hi_ready, 1)

        def squares(n, tile, width, ready):
            def src(k):
                ready(k)
                a(sq[:, k % 2, 0:width], tile(k), ACT.Square).then_inc(sq_done, 1)
            return src

        def use(functions):
            act.preload_act_table_set({"ln, exp": "natural_log_exp_and_others",
                                       "sigmoid": "sigmoid_and_others"}[functions])

        act.wait_ge(consts_in, 16 * 6)
        a(cmat[:, :, :].rearrange("p a b -> p (a b)"), w_raw[0][:, 0:N_CMAT * P], ACT.Copy).then_inc(cmat_ready, 1)
        act.wait_ge(x_loaded, 16)
        norm(0, squares(0, lambda k: h[:, k, :], FULL, lambda k: None), FULL, 0)
        for u in range(2):
            act.wait_ge(w_loaded[u], 16)
            a(w_hi[u][:, :], w_raw[u][:, :], ACT.Copy).then_inc(w_hi_ready, 1)

        H1, H0 = slice(SEQ, PACKED), slice(0, SEQ)

        def softplus(g):
            act.wait_ge(hd_pe.sem, hd_pe.at("scores", g))
            for n in (1, 2, 0):
                bank, off, w = PARTS[n]
                a(sp[:, off:off + w], psum[:, 4 + bank, 0:w], ACT.Abs).then_inc(*hd_act.step(f"abs{n}"))
            for n, cols, ready in ((1, H1, "abs2"), (0, H0, "abs0")):
                act.wait_ge(hd_act.sem, hd_act.at(ready, g))
                a(sp[:, cols], sp[:, cols], ACT.Exp, scale=-1.0).then_inc(*hd_act.step(f"exp{n}"))
            for n, cols in ((1, H1), (0, H0)):
                act.wait_ge(hd_act.sem, hd_act.at(f"exp{n}", g))
                a(sp[:, cols], sp[:, cols], ACT.Ln, bias=g_col("one", 0)).then_inc(*hd_act.step(f"ln{n}"))
            for n, cols, ready in ((1, H1, "sp2"), (0, H0, "sp0")):
                act.wait_ge(hd_dve.sem, hd_dve.at(ready, g))
                a(sp_hi[:, cols], sp[:, cols], ACT.Copy).then_inc(*hd_act.step(f"hi{n}"))

        def weights(g):
            act.wait_ge(hd_pe.sem, hd_pe.at("logs", g))
            for n, (bank, off, w) in enumerate(PARTS):
                a(a_f[:, off:off + w], psum[:, 4 + bank, 0:w], ACT.Exp).then_inc(*hd_act.step(f"a_part{n}"))
            act.wait_ge(hd_act.sem, hd_act.at("a_part2", g))
            a(a_hi[:, :], a_f[:, :], ACT.Copy).then_inc(*hd_act.step("a_hi"))

        def meta_softplus(p):
            act.wait_ge(mk_pe.sem, mk_pe.at("m_scores", p))
            a(m_f[:, :], psum[:, 7, :], ACT.Abs).then_inc(*mk_act.step("m_abs"))
            act.wait_ge(mk_act.sem, mk_act.at("m_abs", p))
            a(m_f[:, :], m_f[:, :], ACT.Exp, scale=-1.0).then_inc(*mk_act.step("m_exp"))
            act.wait_ge(mk_act.sem, mk_act.at("m_exp", p))
            a(m_f[:, :], m_f[:, :], ACT.Ln, bias=g_col("one", 0)).then_inc(*mk_act.step("m_ln"))
            act.wait_ge(mk_dve.sem, mk_dve.at("m_sp", p))
            a(m_hi[:, :], m_f[:, :], ACT.Copy).then_inc(*mk_act.step("m_hi"))

        def meta_weights(p):
            act.wait_ge(mk_pe.sem, mk_pe.at("m_rows", p))
            a(m_f[:, :], psum[:, 7, :], ACT.Exp).then_inc(*mk_act.step("am_exp"))
            act.wait_ge(mk_act.sem, mk_act.at("am_exp", p))
            a(m_hi[:, :], m_f[:, :], ACT.Copy).then_inc(*mk_act.step("am_hi"))

        def key_hi(t, at, s):
            strips(at, s)
            a(K_hi[:, t, :], psum[:, at.bank(s), :], ACT.Copy).then_inc(*qk_act.step("K_hi"))
            act.wait_ge(strip_free, at.strip(s) + 1)
            a(KM_hi[:, :], KM[:, :], ACT.Copy).then_inc(*qk_act.step("KM_hi"))

        def query_hi(t, at, s):
            strips(at, s)
            a(Q_hi[:, t, :], psum[:, at.bank(s), :], ACT.Copy, scale=SB_DH ** -0.5).then_inc(*qk_act.step("Q_hi"))

        def value_hi(at, half):
            strips(at, half)
            a(V_hi[:, 4 * half:4 * half + 4, 0:3:2, :],
              psum[:, at.bank(half), :].rearrange("p (a r c) -> p a r c", r=2, c=SB_DH), ACT.Copy)\
                .then_inc(*v_act.step(f"V_hi{half}"))
            if half == 0:
                act.wait_ge(strip_free, at.strip(0) + 1)
                a(VM_hi[:, :, :], VM[:, :, :], ACT.Copy).then_inc(*v_act.step("VM_hi"))

        def y_hi(t, p):
            act.wait_ge(y_out, p + 1)
            a(Y_hi[:, t, :], Y[:, :], ACT.Copy).then_inc(y_hi_ready, 1)

        def quad_body(at, i, has_d, has_next):
            g, p = 4 * i, 2 * i
            nj, ns = (3, 12) if has_d else (2, 4)
            softplus(g)
            meta_softplus(p)
            if has_d:
                y_hi(1, p - 1)
            value_hi(at, 0)
            weights(g)
            value_hi(at, 1)
            split_hi(at, 0)
            softplus(g + 1)
            key_hi(1, at, 2)
            weights(g + 1)
            query_hi(1, at, 3)
            meta_weights(p)
            softplus(g + 2)
            split_hi(at, 1)
            meta_softplus(p + 1)
            weights(g + 2)
            if has_d:
                strips(at, 11)
                split_hi(at, 2)
            y_hi(0, p)
            softplus(g + 3)
            if has_next:
                key_hi(0, at, ns)
            weights(g + 3)
            if has_next:
                query_hi(0, at, ns + 1)
            meta_weights(p + 1)
            if has_next:
                split_hi(at, nj)

        at = Place("quad_start")
        use("ln, exp")
        act.wait_ge(memset_done, 2)
        for x in (V_hi, V_lo):
            a(x[:, :, 1, :], acc[:, 0, :].rearrange("p (a c) -> p a c", c=SB_DH), ACT.Copy).then_inc(quad_ready, 1)
        for x, y in ((XM_hi, X_hi), (XM_lo, X_lo)):
            a(x[:, :, :].rearrange("p k (j m) -> p k j m", j=4),
              as_f32(y[:, :, 0:32]).unsqueeze(2).broadcast_to([P, DT, 4, 32]), ACT.Copy).then_inc(quad_ready, 1)
        key_hi(0, at, 0)
        query_hi(0, at, 1)
        split_hi(at, 0)
        quad_body(Place("quad_first"), 0, False, True)
        with act.Fori(1, QUADS - 1) as i:
            quad_body(Place("quads", i, 4, 14, first=1), i, True, True)
        quad_body(Place("quad_last"), QUADS - 1, True, False)
        y_hi(1, 2 * QUADS - 1)
        at = Place("quad_end")
        strips(at, 7)
        split_hi(at, 0)

        def gates(phase, n):
            use("sigmoid")
            act.wait_ge(strip_free, START[phase][1])

            def body(i):
                at = Place(phase, i, 2, 4)
                for j in range(2):
                    for c in range(2):
                        strips(at, 2 * j + c)
                        if not (n == 0 and type(i) is int and i == 0 and j == 0):
                            act.wait_ge(gate_used, DT * n + 4 * i + 2 * j + c - 1)
                        a(sig[:, c, 0:SEQ], strip_view(at.bank(2 * j + c), SEQ), ACT.Sigmoid).then_inc(strip_free, 1)
                    split_hi(at, j)
            loop(act, 2, body, 2)

        gates("gate_b", 0)

        def turned_hi(x, hi, width, i):
            for t in range(2):
                act.wait_ge(t_dve.sem, t_dve.at(f"{x}_r{t + 1}", i))
                a(hi[:, t, :], turned[:, t, 0:width], ACT.Copy).then_inc(*t_act.step(f"R{x.upper()}_hi{t}"))

        def head_body(at, i, has_next):
            for n in range(2):
                for half in range(2):
                    s = 2 * n + half
                    strips(at, s)
                    a(VZ_hi[:, 2 * half:2 * half + 2, 256 * n:256 * (n + 1)],
                      psum[:, at.bank(s), :].rearrange("p (b c) -> p b c", b=2), ACT.Copy)\
                        .then_inc(*r_act.step(f"V_hi{s}"))
                    if half == 0:
                        a(RVM_hi[:, 256 * n:256 * (n + 1)], psum[0:META, at.bank(s) + 1, 0:256], ACT.Copy)\
                            .then_inc(*r_act.step(f"VM_hi{n}"))
                split_hi(at, n)
            act.wait_ge(r_dve.sem, r_dve.at("S3", i))
            a(S_hi[:, :], S_f[:, :], ACT.Copy).then_inc(*r_act.step("S_hi"))
            act.wait_ge(r_dve.sem, r_dve.at("SM", i))
            a(SM_hi[:, :], SM_f[:, :], ACT.Copy).then_inc(*r_act.step("SM_hi"))
            use("sigmoid")
            for n in range(2):
                for c in range(2):
                    e = 2 * n + c
                    strips(at, 4 + e)
                    a(silu_g[:, e, :], strip_view(at.bank(4 + e), SEQ), ACT.Sigmoid)\
                        .then_inc(*r_act.step(f"g_sig{e}"))
                split_hi(at, 2 + n)
            use("ln, exp")
            squares = [S_f[:, 0:SEQ], S_f[:, SEQ:2 * SEQ], sig[:, 0, 0:SEQ], sig[:, 1, 0:SEQ]]
            for e in range(4):
                act.wait_ge(r_dve.sem, r_dve.at(f"yc{e}", i))
                if e == 0:
                    act.wait_ge(r_pe.sem, r_pe.at("mean", i))
                a(squares[e], RY[:, e, :], ACT.Square).then_inc(*r_act.step(f"y_sq{e}"))
            if has_next:
                turned_hi("q", RQ_hi, SEQ, i + 1)
                split_hi(at, 4)
            act.wait_ge(r_pe.sem, r_pe.at("var", i))
            a(r_std[:, :], psum[:, 5, :], ACT.Ln, scale=1.0 / RET_DV, bias=g_col("gn_eps", 0))\
                .then_inc(*r_act.step("ln"))
            act.wait_ge(r_act.sem, r_act.at("ln", i))
            a(r_std[:, :], r_std[:, :], ACT.Exp, scale=-0.5).then_inc(*r_act.step("std"))
            for e in range(4):
                act.wait_ge(r_dve.sem, r_dve.at(f"z{e}", i))
                a(VZ_hi[:, e, :], RY[:, e, :], ACT.Copy).then_inc(*r_act.step(f"z_hi{e}"))
            if has_next:
                turned_hi("k", RK_hi, FULL, i + 1)
                split_hi(at, 5)
                for n in range(2):
                    strips(at, 12 + 4 * n + 3)
                    split_hi(at, 6 + n)

        at = Place("head0")
        turned_hi("q", RQ_hi, SEQ, 0)
        split_hi(at, 0)
        turned_hi("k", RK_hi, FULL, 0)
        split_hi(at, 1)
        loop(act, RET_HEADS - 1, lambda i: head_body(Place("heads", i, 8, 20), i, True))
        head_body(Place("head_last"), RET_HEADS - 1, False)
        at = Place("head_out")
        for n in range(2):
            strips(at, 4 * n + 3)
            split_hi(at, n)
        gates("gate_a", 1)
        for k in range(DT):
            act.wait_ge(mixed, k + 1)
            a(X_hi[:, k, META:FULL], acc[:, k, :], ACT.Copy).then_inc(m_split_hi, 1)

        def out_product(phase):
            def body(i):
                at = Place(phase, i, 2, 4)
                for j in range(2):
                    strips(at, 2 * j + 1)
                    split_hi(at, j)
            loop(act, 2, body)

        out_product("w_out")
        norm(1, squares(1, lambda k: acc[:, k, :], SEQ, lambda k: act.wait_ge(mix_out, k + 1)), SEQ)
        norm(2, squares(2, lambda k: h[:, k, META:FULL], SEQ, lambda k: act.wait_ge(post_done, k + 1)), SEQ, 1)

        def ffn(tag, n):
            def gate_up(at, j, s, i):
                for c in range(2):
                    strips(at, s + c)
                    if c == 0:
                        act.wait_ge(f_dve.sem, f_dve.at("M_lo", i - 1)) if not (type(i) is int and i == 0) else None
                    a(silu_a[:, c, :], strip_view(at.bank(s + c), SEQ), ACT.Sigmoid)\
                        .then_inc(*f_act.step(f"sig{c}"))
                split_hi(at, j)
                strips(at, s + 3)
                split_hi(at, j + 1)
                act.wait_ge(f_dve.sem, f_dve.at("prod", i))
            def hidden(i, slot):
                a(M_hi[:, slot, :, :], silu_a[:, :, :], ACT.Copy).then_inc(*f_act.step("M_hi"))

            def two(at, i0, final):
                for m in range(2):
                    gate_up(at, 3 * m, 12 * m, i0 + m + 1)
                    hidden(i0 + m + 1, (m + 1) % 2)
                    strips(at, 12 * m + 11)
                    if not (final and m == 1):
                        split_hi(at, 3 * m + 2)
            base = FF_PAIRS * n
            use("sigmoid")
            gate_up(Place("ffn0" + tag, depth=4), 0, 0, base)
            hidden(base, 0)
            rounds = 5 if n == 0 else 4
            loop(act, rounds, lambda i: two(Place("ffn" + tag, i, 6, 24, 4), base + 2 * i, False))
            if n:
                two(Place("ffn_last" + tag, depth=4), base + 2 * rounds, True)
            at = Place("ffn_end" + tag, depth=4)
            if n == 0:
                strips(at, 7)
                split_hi(at, 0)

        ffn("", 0)
        norm(3, squares(3, lambda k: acc[:, k, :], SEQ, lambda k: act.wait_ge(f_added, DT * FF_PAIRS) if k == 0 else None), SEQ)
        norm(4, squares(4, lambda k: h[:, k, :], FULL, lambda k: act.wait_ge(post_done, DT + k + 1)), FULL, 2)

        use("sigmoid")
        at = Place("conv_b")
        count = [0]

        def ca(ins):
            count[0] += 1
            ins.then_inc(c_act, 1)
            return count[0]

        for half in range(2):
            for c in range(2):
                strips(at, 4 * half + c)
                if half:
                    act.wait_ge(c_dve, C2[f"glu{c}"])
                a(wide(conv_sig[:, c, :]), strip_view(at.bank(c), FULL), ACT.Sigmoid).then_inc(strip_free, 1)
            split_hi(at, 2 * half)
            strips(at, 4 * half + 3)
            split_hi(at, 2 * half + 1)
        at = Place("conv_a")
        for j in range(6):
            strips(at, 2 * j + 1)
            split_hi(at, j)
        use("ln, exp")
        for t in range(CT):
            act.wait_ge(c_dve, C2[f"zc{t}"])
            if t >= 2:
                act.wait_ge(c_dve, C2[f"zsq{t - 2}"])
            ca(a(sq[:, t % 2, 0:SEQ], z[:, t, :], ACT.Square))
        act.wait_ge(c_pe, 2)
        n = ca(a(std[:, 0:SEQ], psum[:, 5, :], ACT.Ln, scale=1.0 / WB, bias=g_col("ln_eps", 0)))
        act.wait_ge(c_act, n)
        n = ca(a(std[:, 0:SEQ], std[:, 0:SEQ], ACT.Exp, scale=-0.5))
        assert n == A2["std"]
        use("sigmoid")
        for t in range(CT):
            act.wait_ge(c_dve, C2[f"zn{t}"])
            n = ca(a(z[:, t, :], z[:, t, :], ACT.Identity, scale=g_col("ln_gain", t), bias=g_col("ln_bias", t)))
            act.wait_ge(c_act, n)
            if t >= 2:
                act.wait_ge(c_dve, C2[f"yb{t - 2}"])
            n = ca(a(normed[:, t % 2, 0:SEQ], z[:, t, :], ACT.Sigmoid))
            assert n == A2[f"e{t}"]
        for t in range(CT):
            act.wait_ge(c_dve, C2[f"yb{t}"])
            n = ca(a(y2_hi[:, CT + t, :], z[:, t, :], ACT.Copy))
            assert n == A2[f"yh{t}"]
        out_product("w_out2")
        norm(5, squares(5, lambda k: acc[:, k, :], SEQ, lambda k: act.wait_ge(mix_out, DT + k + 1)), SEQ)
        norm(6, squares(6, lambda k: h[:, k, META:FULL], SEQ, lambda k: act.wait_ge(post_done, 2 * DT + k + 1)), SEQ, 3)
        ffn("_2", 1)
        norm(7, squares(7, lambda k: acc[:, k, :], SEQ, lambda k: act.wait_ge(f_added, 2 * DT * FF_PAIRS) if k == 0 else None), SEQ)

    @block.vector
    def _(dve):
        v = nc.vector

        def split_lo(at, j):
            dve.wait_ge(w_hi_ready, at.unit(j) + 3)
            v.tensor_tensor(w_lo[at.ring(j)][:, :], w_raw[at.ring(j)][:, :], as_f32(w_hi[at.ring(j)][:, :]),
                            ALU.subtract).then_inc(w_lo_ready, 1)

        def strips(at, s, n=1):
            dve.wait_ge(strip_done, at.strip(s) + n)

        def stt(out_, in0, scalar, in1, op0, op1):
            return v.scalar_tensor_tensor(out=out_, in0=in0, scalar=scalar, in1=in1, op0=op0, op1=op1)

        def norm(n, width):
            for k in range(DT):
                dve.wait_ge(sq_done, DT * n + k + 1)
                if k == 0:
                    if n:
                        dve.wait_ge(sum_done, n)
                    ins = v.tensor_copy(sq_sum[:, 0:width], sq[:, 0, 0:width])
                else:
                    dve.wait_ge(sq_added, DT * n + k)
                    ins = v.tensor_tensor(sq_sum[:, 0:width], sq_sum[:, 0:width], sq[:, k % 2, 0:width], ALU.add)
                ins.then_inc(sq_added, 1)

        def norm_split(n, s, width, gain):
            norm(n, width)
            dve.wait_ge(std_ready, 2 * n + 2)
            cols = slice(0, FULL) if width == FULL else slice(META, FULL)

            def lo(k):
                dve.wait_ge(x_hi_ready, DT * s + k + 1)
                v.tensor_tensor(X_lo[:, k, cols], normed[:, k % 2, 0:width], as_f32(X_hi[:, k, cols]),
                                ALU.subtract).then_inc(x_lo_ready, 1)
            for k in range(DT):
                if k >= 2:
                    dve.wait_ge(x_lo_ready, DT * s + k - 1)
                stt(normed[:, k % 2, 0:width], h[:, k, cols], g_col(gain, k), std[:, 0:width],
                    ALU.mult, ALU.mult).then_inc(norm_scaled, 1)
                if k:
                    lo(k - 1)
            lo(DT - 1)

        def norm_add(n, p, gain):
            norm(n, SEQ)
            dve.wait_ge(std_ready, 2 * n + 2)
            for k in range(DT):
                stt(normed[:, k % 2, 0:SEQ], acc[:, k, :], g_col(gain, k), std[:, 0:SEQ],
                    ALU.mult, ALU.mult).then_inc(norm_scaled, 1)
                dve.wait_ge(norm_scaled, DT * n + k + 1)
                v.tensor_tensor(h[:, k, META:FULL], h[:, k, META:FULL], normed[:, k % 2, 0:SEQ], ALU.add)\
                    .then_inc(post_done, 1)

        dve.wait_ge(consts_in, 16 * 6)
        dve.wait_ge(x_loaded, 16)
        norm_split(0, 0, FULL, "pre_mix")
        for u in range(2):
            dve.wait_ge(w_hi_ready, u + 1)
            v.tensor_tensor(w_lo[u][:, :], w_raw[u][:, :], as_f32(w_hi[u][:, :]), ALU.subtract)\
                .then_inc(w_lo_ready, 1)
        dve.wait_ge(x_lo_ready, DT)
        v.memset(acc[:, :, :], 0.0).then_inc(memset_done, 1)
        v.memset(KM[:, :], 0.0).then_inc(memset_done, 1)

        def softplus(g):
            for n in (1, 2, 0):
                bank, off, w = PARTS[n]
                if n != 2:
                    dve.wait_ge(hd_act.sem, hd_act.at(f"ln{n}", g))
                stt(sp[:, off:off + w], psum[:, 4 + bank, 0:w], 0.0, sp[:, off:off + w], ALU.max, ALU.add)\
                    .then_inc(*hd_dve.step(f"sp{n}"))
            for n, cols in ((1, slice(SEQ, PACKED)), (0, slice(0, SEQ))):
                dve.wait_ge(hd_act.sem, hd_act.at(f"hi{n}", g))
                v.tensor_tensor(sp_lo[:, cols], sp[:, cols], as_f32(sp_hi[:, cols]), ALU.subtract)\
                    .then_inc(*hd_dve.step(f"sp_lo{n}"))

        def weights(g):
            dve.wait_ge(hd_act.sem, hd_act.at("a_hi", g))
            v.tensor_tensor(a_lo[:, :], a_f[:, :], as_f32(a_hi[:, :]), ALU.subtract)\
                .then_inc(*hd_dve.step("a_lo"))

        def meta_softplus(p):
            dve.wait_ge(mk_act.sem, mk_act.at("m_ln", p))
            stt(m_f[:, :], psum[:, 7, :], 0.0, m_f[:, :], ALU.max, ALU.add).then_inc(*mk_dve.step("m_sp"))
            dve.wait_ge(mk_act.sem, mk_act.at("m_hi", p))
            v.tensor_tensor(m_lo[:, :], m_f[:, :], as_f32(m_hi[:, :]), ALU.subtract).then_inc(*mk_dve.step("m_lo"))

        def meta_weights(p):
            dve.wait_ge(mk_act.sem, mk_act.at("am_hi", p))
            v.tensor_tensor(m_lo[:, :], m_f[:, :], as_f32(m_hi[:, :]), ALU.subtract).then_inc(*mk_dve.step("am_lo"))

        def y_take(p):
            dve.wait_ge(mk_pe.sem, mk_pe.at("y_meta", p))
            if not (type(p) is int and p == 0):
                dve.wait_ge(y_lo_ready, p)
            v.tensor_copy(Y[:, :], psum[:, 3, :]).then_inc(y_out, 1)

        def y_lo(t, p):
            dve.wait_ge(y_hi_ready, p + 1)
            v.tensor_tensor(Y_lo[:, t, :], Y[:, :], as_f32(Y_hi[:, t, :]), ALU.subtract).then_inc(y_lo_ready, 1)

        def key_lo(t, at, s, p):
            dve.wait_ge(qk_act.sem, qk_act.at("K_hi", p))
            v.tensor_tensor(K_lo[:, t, :], psum[:, at.bank(s), :], as_f32(K_hi[:, t, :]), ALU.subtract)\
                .then_inc(*qk_dve.step("K_lo"))
            v.tensor_tensor(KM[:, 0:64].rearrange("p (r m) -> p r m", r=2)[:, :, 0:META],
                            psum[:, at.bank(s) + 1, 0:META].unsqueeze(1).broadcast_to([P, 2, META]),
                            mask_k[:, 0, 0:2, 0:META], ALU.mult).then_inc(strip_free, 1)
            dve.wait_ge(qk_act.sem, qk_act.at("KM_hi", p))
            v.tensor_tensor(KM_lo[:, :], KM[:, :], as_f32(KM_hi[:, :]), ALU.subtract).then_inc(*qk_dve.step("KM_lo"))

        def query_lo(t, at, s, p):
            dve.wait_ge(qk_act.sem, qk_act.at("Q_hi", p))
            stt(Q_lo[:, t, :], psum[:, at.bank(s), :], SB_DH ** -0.5, as_f32(Q_hi[:, t, :]), ALU.mult, ALU.subtract)\
                .then_inc(strip_free, 1)

        def value_lo(at, half, i):
            dve.wait_ge(v_act.sem, v_act.at(f"V_hi{half}", i))
            blocks = (slice(None), slice(4 * half, 4 * half + 4), slice(0, 3, 2), slice(None))
            ins = v.tensor_tensor(V_lo[blocks],
                                  psum[:, at.bank(half), :].rearrange("p (a r c) -> p a r c", r=2, c=SB_DH),
                                  as_f32(V_hi[blocks]), ALU.subtract)
            if half:
                ins.then_inc(strip_free, 1)
                return
            ins.then_inc(*v_dve.step("V_lo0"))
            v.tensor_tensor(VM[:, :, :], psum[:, at.bank(0) + 1, 0:2 * P].rearrange("p (t c) -> p t c", t=2),
                            mask_v[:, 0, :].unsqueeze(1).broadcast_to([P, 2, P]), ALU.mult).then_inc(strip_free, 1)
            dve.wait_ge(v_act.sem, v_act.at("VM_hi", i))
            v.tensor_tensor(VM_lo[:, :, :], VM[:, :, :], as_f32(VM_hi[:, :, :]), ALU.subtract)\
                .then_inc(*v_dve.step("VM_lo"))

        def add_up(dst, at, s, ms):
            for n, m in enumerate(ms):
                strips(at, s + n)
                v.tensor_tensor(dst[:, m, :], dst[:, m, :], strip_view(at.bank(s + n), SEQ), ALU.add)\
                    .then_inc(strip_free, 1)

        def quad_body(at, i, has_d, has_next):
            g, p = 4 * i, 2 * i
            nj, ns = (3, 12) if has_d else (2, 4)
            softplus(g)
            meta_softplus(p)
            if has_d:
                y_lo(1, p - 1)
            value_lo(at, 0, i)
            weights(g)
            value_lo(at, 1, i)
            split_lo(at, 0)
            softplus(g + 1)
            key_lo(1, at, 2, p + 1)
            weights(g + 1)
            query_lo(1, at, 3, p + 1)
            meta_weights(p)
            y_take(p)
            softplus(g + 2)
            split_lo(at, 1)
            meta_softplus(p + 1)
            if has_d:
                add_up(acc, at, 4, range(4))
            weights(g + 2)
            if has_d:
                add_up(acc, at, 8, range(4, 8))
                split_lo(at, 2)
            y_lo(0, p)
            softplus(g + 3)
            if has_next:
                key_lo(0, at, ns, p + 2)
            weights(g + 3)
            if has_next:
                query_lo(0, at, ns + 1, p + 2)
            meta_weights(p + 1)
            y_take(p + 1)
            if has_next:
                split_lo(at, nj)

        dve.wait_ge(memset_done, 2)
        dve.wait_ge(quad_ready, 2)
        at = Place("quad_start")
        key_lo(0, at, 0, 0)
        query_lo(0, at, 1, 0)
        split_lo(at, 0)
        quad_body(Place("quad_first"), 0, False, True)
        with dve.Fori(1, QUADS - 1) as i:
            quad_body(Place("quads", i, 4, 14, first=1), i, True, True)
        quad_body(Place("quad_last"), QUADS - 1, True, False)
        y_lo(1, 2 * QUADS - 1)
        at = Place("quad_end")
        add_up(acc, at, 0, range(8))
        split_lo(at, 0)

        def gates(phase, use_gate):
            for j in range(4):
                at = Place(phase)
                for c in range(2):
                    m = 2 * j + c
                    dve.wait_ge(strip_free, at.strip(m) + 1)
                    use_gate(m, sig[:, c, 0:SEQ])
                split_lo(at, j)

        gates("gate_b", lambda m, gate: v.tensor_tensor(acc[:, m, :], acc[:, m, :], gate, ALU.mult)
              .then_inc(gate_used, 1))
        v.memset(ret[:, :, :], 0.0).then_inc(ret_zero, 1)
        dve.wait_ge(ret_zero, 1)

        def first_tile(x, s, width, at):
            fold = wide if width == FULL else (lambda ap: ap)
            cos, sin = (fold(rot[:, n, FULL - width:]) for n in range(2))
            strips(at, s)
            v.tensor_tensor(fold(turned[:, 0, 0:width]), strip_view(at.bank(s), width), cos, ALU.mult)\
                .then_inc(*t_dve.step(f"{x}_cos"))
            v.tensor_tensor(fold(turned[:, 1, 0:width]), strip_view(at.bank(s), width), sin, ALU.mult)\
                .then_inc(strip_free, 1)

        def second_tile(x, s, width, at, i, hi, lo):
            fold = wide if width == FULL else (lambda ap: ap)
            cos, sin = (fold(rot[:, n, FULL - width:]) for n in range(2))
            spare = [sig[:, n, 0:width] for n in range(2)]
            strips(at, s)
            v.tensor_tensor(fold(spare[0]), strip_view(at.bank(s), width), sin, ALU.mult)\
                .then_inc(*t_dve.step(f"{x}_sin"))
            v.tensor_tensor(fold(spare[1]), strip_view(at.bank(s), width), cos, ALU.mult).then_inc(strip_free, 1)
            dve.wait_ge(t_dve.sem, t_dve.at(f"{x}_sin", i))
            v.tensor_tensor(turned[:, 0, 0:width], turned[:, 0, 0:width], spare[0], ALU.subtract)\
                .then_inc(*t_dve.step(f"{x}_r1"))
            dve.wait_ge(strip_free, at.strip(s) + 1)
            v.tensor_tensor(turned[:, 1, 0:width], turned[:, 1, 0:width], spare[1], ALU.add)\
                .then_inc(*t_dve.step(f"{x}_r2"))
            dve.wait_ge(t_act.sem, t_act.at(f"R{x.upper()}_hi1", i))
            v.tensor_tensor(lo[:, :, :], turned[:, :, 0:width], as_f32(hi[:, :, :]), ALU.subtract)\
                .then_inc(*t_dve.step(f"{x}_lo"))

        def head_body(at, i, has_next):
            dve.wait_ge(r_pe.sem, r_pe.at("scores", i))
            dve.wait_ge(decay_loaded, 16 * (i + 1))
            for n in range(2):
                for half in range(2):
                    s = 2 * n + half
                    dve.wait_ge(r_act.sem, r_act.at(f"V_hi{s}", i))
                    blocks = (slice(None), slice(2 * half, 2 * half + 2), slice(256 * n, 256 * (n + 1)))
                    ins = v.tensor_tensor(VZ_lo[blocks], psum[:, at.bank(s), :].rearrange("p (b c) -> p b c", b=2),
                                          as_f32(VZ_hi[blocks]), ALU.subtract)
                    if half:
                        ins.then_inc(strip_free, 1)
                    else:
                        ins.then_inc(*r_dve.step(f"V_lo{s}"))
                        dve.wait_ge(r_act.sem, r_act.at(f"VM_hi{n}", i))
                        v.tensor_tensor(RVM_lo[:, 256 * n:256 * (n + 1)], psum[0:META, at.bank(s) + 1, 0:256],
                                        as_f32(RVM_hi[:, 256 * n:256 * (n + 1)]), ALU.subtract)\
                            .then_inc(strip_free, 1)
                split_lo(at, n)
            for b in range(BLOCKS):
                v.tensor_tensor(S_f[:, KEY_OFF[b]:KEY_OFF[b] + KEY_LEN[b]],
                                psum[:, 4 + KEY_BANK[b], KEY_COL[b]:KEY_COL[b] + KEY_LEN[b]],
                                decay[:, 0, 0:KEY_LEN[b]], ALU.mult).then_inc(*r_dve.step(f"S{b}"))
            v.tensor_tensor(SM_f[:, :], psum[0:META, 7, :], decay[0:META, 1, :], ALU.mult)\
                .then_inc(*r_dve.step("SM"))
            dve.wait_ge(r_act.sem, r_act.at("S_hi", i))
            v.tensor_tensor(S_lo[:, :], S_f[:, :], as_f32(S_hi[:, :]), ALU.subtract).then_inc(*r_dve.step("S_lo"))
            dve.wait_ge(r_act.sem, r_act.at("SM_hi", i))
            v.tensor_tensor(SM_lo[:, :], SM_f[:, :], as_f32(SM_hi[:, :]), ALU.subtract)\
                .then_inc(*r_dve.step("SM_lo"))
            for e in range(4):
                dve.wait_ge(r_act.sem, r_act.at(f"g_sig{e}", i))
                v.tensor_tensor(silu_g[:, e, :], silu_g[:, e, :], strip_view(at.bank(4 + e), SEQ), ALU.mult)\
                    .then_inc(strip_free, 1)
                if e % 2:
                    split_lo(at, 2 + e // 2)
            dve.wait_ge(r_pe.sem, r_pe.at("y", i))
            for e in range(4):
                v.tensor_copy(RY[:, e, :], psum[:, 4 + e, :]).then_inc(*r_dve.step(f"y{e}"))
            for e in range(1, 4):
                dve.wait_ge(r_dve.sem, r_dve.at(f"y{e}" if e == 1 else f"ys{e - 1}", i))
                v.tensor_tensor(S_f[:, 0:SEQ], RY[:, 0, :] if e == 1 else S_f[:, 0:SEQ], RY[:, e, :],
                                ALU.add).then_inc(*r_dve.step(f"ys{e}"))
            dve.wait_ge(r_pe.sem, r_pe.at("mean", i))
            for e in range(4):
                stt(RY[:, e, :], psum[:, 4, :], -1.0 / RET_DV, RY[:, e, :], ALU.mult, ALU.add)\
                    .then_inc(*r_dve.step(f"yc{e}"))
            if has_next:
                first_tile("q", 8, SEQ, at)
            squares = [S_f[:, 0:SEQ], S_f[:, SEQ:2 * SEQ], sig[:, 0, 0:SEQ], sig[:, 1, 0:SEQ]]
            for e in range(1, 4):
                dve.wait_ge(r_act.sem, r_act.at(f"y_sq{e}", i))
                if e > 1:
                    dve.wait_ge(r_dve.sem, r_dve.at(f"sqs{e - 1}", i))
                v.tensor_tensor(squares[0], squares[0], squares[e], ALU.add).then_inc(*r_dve.step(f"sqs{e}"))
            v.tensor_tensor(RY[:, :, :], RY[:, :, :], silu_g[:, :, :], ALU.mult).then_inc(*r_dve.step("yg"))
            if has_next:
                dve.wait_ge(r_dve.sem, r_dve.at("sqs3", i))
                second_tile("q", 9, SEQ, at, i + 1, RQ_hi, RQ_lo)
                split_lo(at, 4)
                dve.wait_ge(t_dve.sem, t_dve.at("q_lo", i + 1))
                first_tile("k", 10, FULL, at)
            dve.wait_ge(r_act.sem, r_act.at("std", i))
            dve.wait_ge(r_dve.sem, r_dve.at("yg", i))

            def z_lo(e):
                dve.wait_ge(r_act.sem, r_act.at(f"z_hi{e}", i))
                v.tensor_tensor(VZ_lo[:, e, :], RY[:, e, :], as_f32(VZ_hi[:, e, :]), ALU.subtract)\
                    .then_inc(*r_dve.step(f"z_lo{e}"))
            for e in range(4):
                v.tensor_tensor(RY[:, e, :], RY[:, e, :], r_std[:, :], ALU.mult).then_inc(*r_dve.step(f"z{e}"))
                if e:
                    z_lo(e - 1)
            z_lo(3)
            if has_next:
                second_tile("k", 11, FULL, at, i + 1, RK_hi, RK_lo)
                split_lo(at, 5)
                for n in range(2):
                    add_up(ret, at, 12 + 4 * n, range(4 * n, 4 * n + 4))
                    split_lo(at, 6 + n)
                dve.wait_ge(t_dve.sem, t_dve.at("k_lo", i + 1))

        at = Place("head0")
        first_tile("q", 0, SEQ, at)
        second_tile("q", 1, SEQ, at, 0, RQ_hi, RQ_lo)
        split_lo(at, 0)
        dve.wait_ge(t_dve.sem, t_dve.at("q_lo", 0))
        first_tile("k", 2, FULL, at)
        second_tile("k", 3, FULL, at, 0, RK_hi, RK_lo)
        split_lo(at, 1)
        loop(dve, RET_HEADS - 1, lambda i: head_body(Place("heads", i, 8, 20), i, True))
        head_body(Place("head_last"), RET_HEADS - 1, False)
        at = Place("head_out")
        for n in range(2):
            add_up(ret, at, 4 * n, range(4 * n, 4 * n + 4))
            split_lo(at, n)

        def mix(m, gate):
            v.tensor_tensor(ret[:, m, :], ret[:, m, :], gate, ALU.mult).then_inc(gate_used, 1)
            dve.wait_ge(gate_used, DT + m + 1)
            v.tensor_tensor(acc[:, m, :], acc[:, m, :], ret[:, m, :], ALU.add).then_inc(mixed, 1)

        gates("gate_a", mix)
        for k in range(DT):
            dve.wait_ge(m_split_hi, k + 1)
            v.tensor_tensor(X_lo[:, k, META:FULL], acc[:, k, :], as_f32(X_hi[:, k, META:FULL]), ALU.subtract)\
                .then_inc(m_split_lo, 1)

        def out_product(phase):
            def body(i):
                at = Place(phase, i, 2, 4)
                for j in range(2):
                    for c in range(2):
                        strips(at, 2 * j + c)
                        v.tensor_copy(acc[:, 4 * i + 2 * j + c, :], strip_view(at.bank(2 * j + c), SEQ))\
                            .then_inc(strip_free, 1)
                    split_lo(at, j)
            loop(dve, 2, body)
            dve.wait_ge(strip_free, START[phase][1] + DT)
            for k in range(DT):
                v.tensor_copy(acc[:, k, 0:1], acc[:, k, 0:1]).then_inc(mix_out, 1)

        out_product("w_out")
        dve.wait_ge(x_loaded, 48)
        norm_add(1, 0, "post_mix")
        norm_split(2, 1, SEQ, "pre_ffn")

        def ffn(tag, n):
            def gate_up(at, j, s, i, slot, final=False):
                for c in range(2):
                    dve.wait_ge(f_act.sem, f_act.at(f"sig{c}", i))
                    v.tensor_tensor(silu_a[:, c, :], silu_a[:, c, :], strip_view(at.bank(s + c), SEQ), ALU.mult)\
                        .then_inc(strip_free, 1)
                split_lo(at, j)
                dve.wait_ge(strip_free, at.strip(s + 1) + 1)
                for c in range(2):
                    strips(at, s + 2 + c)
                    v.tensor_tensor(silu_a[:, c, :], silu_a[:, c, :], strip_view(at.bank(s + 2 + c), SEQ), ALU.mult)\
                        .then_inc(strip_free, 1)
                dve.wait_ge(strip_free, at.strip(s + 3) + 1)
                v.tensor_copy(silu_a[:, 0, 0:1], silu_a[:, 0, 0:1]).then_inc(*f_dve.step("prod"))
                split_lo(at, j + 1)
                dve.wait_ge(f_act.sem, f_act.at("M_hi", i))
                v.tensor_tensor(M_lo[:, slot, :, :], silu_a[:, :, :], as_f32(M_hi[:, slot, :, :]), ALU.subtract)\
                    .then_inc(*f_dve.step("M_lo"))

            def add(at, s, i):
                for m in range(DT):
                    strips(at, s + m)
                    v.tensor_tensor(acc[:, m, :], acc[:, m, :], strip_view(at.bank(s + m), SEQ), ALU.add)\
                        .then_inc(strip_free, 1)

            def two(at, i0, final):
                for m in range(2):
                    gate_up(at, 3 * m, 12 * m, i0 + m + 1, (m + 1) % 2)
                    add(at, 12 * m + 4, i0 + m)
                    if not (final and m == 1):
                        split_lo(at, 3 * m + 2)
            base = FF_PAIRS * n
            dve.wait_ge(post_done, (2 * n + 1) * DT)
            v.memset(acc[:, :, :], 0.0).then_inc(acc_zero, 1)
            gate_up(Place("ffn0" + tag, depth=4), 0, 0, base, 0)
            dve.wait_ge(acc_zero, n + 1)
            rounds = 5 if n == 0 else 4
            loop(dve, rounds, lambda i: two(Place("ffn" + tag, i, 6, 24, 4), base + 2 * i, False))
            if n:
                two(Place("ffn_last" + tag, depth=4), base + 2 * rounds, True)
            at = Place("ffn_end" + tag, depth=4)
            add(at, 0, base + FF_PAIRS - 1)
            if n == 0:
                split_lo(at, 0)
            dve.wait_ge(strip_free, at.strip(7) + 1)
            v.tensor_copy(acc[:, 0, 0:1], acc[:, 0, 0:1]).then_inc(f_added, DT * FF_PAIRS)

        ffn("", 0)
        v.tensor_copy(h[:, :, 0:META], meta2_f[:, :, :]).then_inc(memset_done, 1)
        dve.wait_ge(memset_done, 3)
        norm_add(3, 1, "post_ffn")
        norm_split(4, 2, FULL, "pre_mix2")

        count = [0]

        def cd(ins, name=None):
            count[0] += 1
            ins.then_inc(c_dve, 1)
            if name:
                assert C2[name] == count[0], (name, count[0])
            return count[0]

        def last():
            dve.wait_ge(c_dve, count[0])

        LEFT = TAPS_B - 1
        pad = LEFT - META
        cd(v.memset(glu[:, :, 0:pad], 0.0))
        at = Place("conv_b")
        for half in range(2):
            for c in range(2):
                dve.wait_ge(strip_free, at.strip(4 * half + c) + 1)
            split_lo(at, 2 * half)
            for c in range(2):
                strips(at, 4 * half + 2 + c)
                v.tensor_tensor(wide(glu[:, 2 * half + c, pad:]), wide(conv_sig[:, c, :]),
                                strip_view(at.bank(4 * half + 2 + c), FULL), ALU.mult).then_inc(strip_free, 1)
            dve.wait_ge(strip_free, at.strip(4 * half + 3) + 1)
            for c in range(2):
                cd(v.tensor_copy(conv_sig[:, c, 0:1], conv_sig[:, c, 0:1]), f"glu{c}" if half == 0 else None)
            split_lo(at, 2 * half + 1)

        at = Place("conv_a")
        steps = [0]

        def taps(t, n0, n1):
            for k in range(n0, n1):
                shifted = glu[:, t, k:k + SEQ]
                w = g_col("conv_b_w", t * TAPS_B + k)
                if k == 0:
                    ins = v.tensor_scalar(z[:, t, :], shifted, w, g_col("conv_b_bias", t), ALU.mult, ALU.add)
                else:
                    dve.wait_ge(conv_step, steps[0])
                    ins = stt(z[:, t, :], shifted, w, z[:, t, :], ALU.mult, ALU.add)
                ins.then_inc(conv_step, 1)
                steps[0] += 1

        pieces = [(t, n, min(n + 11, TAPS_B)) for t in range(CT) for n in range(0, TAPS_B, 11)]
        per = 2
        for half in range(2):
            o = 6 * half
            for c in range(2):
                strips(at, o + c)
                v.tensor_copy(wide(c_in[:, c, :]), strip_view(at.bank(o + c), FULL)).then_inc(strip_free, 1)
            split_lo(at, 3 * half)
            for x in pieces[:per]:
                taps(*x)
            pieces = pieces[per:]
            dve.wait_ge(strip_free, at.strip(o + 1) + 1)
            for c in range(2):
                strips(at, o + 2 + c)
                v.tensor_tensor(wide(u_in[:, c, :]), wide(c_in[:, c, :]), strip_view(at.bank(o + 2 + c), FULL),
                                ALU.mult).then_inc(strip_free, 1)
            split_lo(at, 3 * half + 1)
            dve.wait_ge(strip_free, at.strip(o + 3) + 1)
            for c in range(2):
                for k in range(TAPS_A):
                    w = g_col("conv_a_w", (2 * half + c) * TAPS_A + k)
                    shifted = u_in[:, c, META - (TAPS_A - 1) + k:META - (TAPS_A - 1) + k + SEQ]
                    if k == 0:
                        cd(v.tensor_scalar(c_in[:, c, 0:SEQ], shifted, w, None, ALU.mult))
                    else:
                        last()
                        cd(stt(c_in[:, c, 0:SEQ], shifted, w, c_in[:, c, 0:SEQ], ALU.mult, ALU.add))
            last()
            for c in range(2):
                strips(at, o + 4 + c)
                v.tensor_tensor(c_in[:, c, 0:SEQ], c_in[:, c, 0:SEQ], strip_view(at.bank(o + 4 + c), SEQ),
                                ALU.mult).then_inc(strip_free, 1)
            dve.wait_ge(strip_free, at.strip(o + 5) + 1)
            for c in range(2):
                cd(v.tensor_copy(y2_hi[:, 2 * half + c, :], c_in[:, c, 0:SEQ]))
                last()
                cd(v.tensor_tensor(y2_lo[:, 2 * half + c, :], c_in[:, c, 0:SEQ],
                                   as_f32(y2_hi[:, 2 * half + c, :]), ALU.subtract))
            split_lo(at, 3 * half + 2)
            for x in pieces[:per]:
                taps(*x)
            pieces = pieces[per:]
        for x in pieces:
            taps(*x)
        dve.wait_ge(conv_step, steps[0])
        cd(v.tensor_tensor(sq_sum[:, 0:SEQ], z[:, 0, :], z[:, 1, :], ALU.add))
        for t in range(2, CT):
            last()
            cd(v.tensor_tensor(sq_sum[:, 0:SEQ], sq_sum[:, 0:SEQ], z[:, t, :], ALU.add),
               "z_sum" if t == CT - 1 else None)
        dve.wait_ge(c_pe, 1)
        for t in range(CT):
            cd(stt(z[:, t, :], psum[:, 4, :], -1.0 / WB, z[:, t, :], ALU.mult, ALU.add), f"zc{t}")
        for t in range(CT):
            dve.wait_ge(c_act, A2["sq"] + t)
            if t:
                last()
            cd(v.tensor_copy(sq_sum[:, 0:SEQ], sq[:, 0, 0:SEQ]) if t == 0 else
               v.tensor_tensor(sq_sum[:, 0:SEQ], sq_sum[:, 0:SEQ], sq[:, t % 2, 0:SEQ], ALU.add),
               f"zsq{t}")
        dve.wait_ge(c_act, A2["std"])
        for t in range(CT):
            cd(v.tensor_tensor(z[:, t, :], z[:, t, :], std[:, 0:SEQ], ALU.mult), f"zn{t}")
        for t in range(CT):
            dve.wait_ge(c_act, A2[f"e{t}"])
            cd(v.tensor_tensor(z[:, t, :], z[:, t, :], normed[:, t % 2, 0:SEQ], ALU.mult), f"yb{t}")
        for t in range(CT):
            dve.wait_ge(c_act, A2[f"yh{t}"])
            cd(v.tensor_tensor(y2_lo[:, CT + t, :], z[:, t, :], as_f32(y2_hi[:, CT + t, :]), ALU.subtract),
               "y_lo" if t == CT - 1 else None)
        out_product("w_out2")
        norm_add(5, 2, "post_mix2")
        norm_split(6, 3, SEQ, "pre_ffn2")
        ffn("_2", 1)
        norm_add(7, 3, "post_ffn2")

    ctx.close()


def second_mixer_steps():
    d, n = {}, 1
    n += 2
    d["glu0"], d["glu1"] = n - 1, n
    n += 2
    n += 2 * (2 * TAPS_A + 4)
    n += CT - 1
    d["z_sum"] = n
    for t in range(CT):
        n += 1
        d[f"zc{t}"] = n
    for t in range(CT):
        n += 1
        d[f"zsq{t}"] = n
    d["z_sq_sum"] = n
    for t in range(CT):
        n += 1
        d[f"zn{t}"] = n
    for t in range(CT):
        n += 1
        d[f"yb{t}"] = n
    d["y_lo"] = n + CT
    a, n = {}, 0
    a["sq"] = n + 1
    n += CT + 2
    a["std"] = n
    for t in range(CT):
        n += 2
        a[f"e{t}"] = n
    for t in range(CT):
        n += 1
        a[f"yh{t}"] = n
    return d, a


C2, A2 = second_mixer_steps()

C_IDENT, C_BLOCKED, C_TRI, C_ALL, C_TRI_META, C_ROWS = 0, 1, 2, 3, 4, 5
N_CMAT = 9

VEC, VEC_COLS = {}, 0
for _name, _n in (("norm_eps", 1), ("gn_eps", 1), ("ln_eps", 1), ("one", 1), ("pre_mix", 8), ("post_mix", 8),
                  ("pre_ffn", 8), ("post_ffn", 8), ("pre_mix2", 8), ("post_mix2", 8), ("pre_ffn2", 8),
                  ("post_ffn2", 8), ("conv_a_w", CT * TAPS_A), ("conv_b_w", CT * TAPS_B), ("conv_b_bias", CT),
                  ("ln_gain", CT), ("ln_bias", CT)):
    VEC[_name] = VEC_COLS
    VEC_COLS += _n


def constants():
    i = np.arange(P)
    ones = np.ones((P, P), np.float32)
    ident = np.eye(P, dtype=np.float32)
    mask_k = np.zeros((P, 2, 4, 32), np.float32)
    mask_v = np.zeros((P, 2, P), np.float32)
    for t in range(2):
        for r in range(2):
            j = 2 * t + r
            mask_k[64 * r:64 * r + 64, t, j, 0:META] = 1
            mask_v[32 * j:32 * j + META, t, 64 * r:64 * r + 64] = 1
    half = RET_DK // 2
    inv = np.float32(10000.0) ** (-np.arange(half, dtype=np.float32) / np.float32(half))
    ang = (np.arange(FULL, dtype=np.float32)[None, :] * inv[:, None]).astype(np.float32)
    cos, sin = np.cos(ang), np.sin(ang)
    cm = np.zeros((P, N_CMAT, P), np.float32)
    cm[:, C_IDENT] = ident
    cm[:, C_BLOCKED] = np.where(i[:, None] < i[None, :], 0.0, BLOCKED)
    cm[:, C_TRI] = np.where(i[:, None] >= i[None, :], -1.0, 0.0)
    cm[:, C_ALL] = -1.0
    same = (i[:, None] // 32 == i[None, :] // 32) & (i[:, None] % 32 < META)
    cm[:, C_TRI_META] = np.where(same & (i[:, None] >= i[None, :]), -1.0, 0.0)
    for j in range(4):
        cm[:, C_ROWS + j] = np.where(i[None, :] // 32 == j, -1.0, 0.0)
    consts = np.concatenate([ones, ident, mask_k.reshape(P, -1), mask_v.reshape(P, -1), cos, sin,
                             cm.reshape(P, -1)], axis=1).astype(np.float32)
    log_g = np.log1p(-(2.0 ** (-5.0 - np.arange(RET_HEADS))))
    scale = RET_DK ** -0.5
    dec = np.zeros((RET_HEADS, P, 2, SEQ))
    u = np.arange(SEQ)
    for n in range(RET_HEADS):
        diff = u[None, :] - i[:, None]
        dec[n, :, 0] = np.where(diff >= 0, np.exp(log_g[n] * np.maximum(diff, 0)), 0.0) * scale
        dec[n, :META, 1] = np.exp(log_g[n] * (u[None, :] + META - i[:META, None])) * scale
    return consts, dec.reshape(RET_HEADS, P, 2 * SEQ).astype(np.float32)


def lay_out(inp):
    def P_unit(w, c):
        return w[:, c:c + 256].reshape(8, P, 256).transpose(1, 0, 2).reshape(P, UNIT)

    def R_unit(w, r, c):
        return w[r:r + 512, c:c + 512].reshape(4, P, 512).transpose(1, 0, 2).reshape(P, UNIT)

    def D_unit(w, r):
        return w[r:r + 256, :].reshape(2, P, 1024).transpose(1, 0, 2).reshape(P, UNIT)

    w_in, w_ret, w_sb, w_out = (inp[n][0] for n in ("w_in", "w_ret_out", "w_sb_out", "w_out"))
    w_fi, w_fo, w_in2, w_out2 = (inp[n][0] for n in ("w_ffn_in", "w_ffn_out", "w_in_2", "w_out_2"))
    w_g, w_u, w_d = (inp[n][0] for n in ("w_gate_2", "w_up_2", "w_down_2"))
    rq, rk, rv, rg, sq, sk, sv, ga, gb = np.cumsum([0, 1024, 1024, 2048, 2048, 1024, 1024, 1024, 1024])
    L = []

    def pair(t):
        return P_unit(np.concatenate([w_in[:, o + P * t:o + P * (t + 1)] for o in (sk, sq)], axis=1), 0)
    L.append(pair(0))
    for q in range(QUADS):
        L += [P_unit(w_in, sv + 256 * q), pair(2 * q + 1)]
        L += [D_unit(w_sb, 256 * (q - 1))] if q else []
        L += [pair(2 * q + 2)] if q < QUADS - 1 else []
    L.append(D_unit(w_sb, 256 * (QUADS - 1)))
    L += [P_unit(w_in, gb + 256 * k) for k in range(4)]
    for n in range(RET_HEADS + 1):
        L += [P_unit(w_in, o + 256 * n) for o in (rq, rk)] if n < RET_HEADS else []
        if n:
            L += [R_unit(w_ret, 512 * (n - 1), c) for c in (0, 512)]
        if n < RET_HEADS:
            L += [P_unit(w_in, o + 512 * n + c) for o in (rv, rg) for c in (0, 256)]
    L += [P_unit(w_in, ga + 256 * k) for k in range(4)]
    L += [P_unit(w_out, 256 * k) for k in range(4)]

    def ffn(g, go, u, uo, d):
        r = []
        for k in range(FF_PAIRS):
            r += [P_unit(g, go + 256 * k), P_unit(u, uo + 256 * k)]
            if k:
                r.append(D_unit(d, 256 * (k - 1)))
        return r + [D_unit(d, 256 * (FF_PAIRS - 1))]
    L += ffn(w_fi, 0, w_fi, D_FF, w_fo)
    for c in range(2):
        L += [P_unit(w_in2, 3 * WA + WB + 256 * c), P_unit(w_in2, 3 * WA + 256 * c)]
    for c in range(2):
        L += [P_unit(w_in2, o + 256 * c) for o in (WA, 2 * WA, 0)]
    L += [P_unit(w_out2, 256 * k) for k in range(4)]
    L += ffn(w_g, 0, w_u, 0, w_d)
    assert len(L) == N_UNITS
    units = np.stack(L)

    def tiles(a):
        n = a.shape[0]
        return a.T.reshape(-1, P, n).transpose(1, 0, 2).reshape(P, -1)
    xfm = tiles(np.concatenate([inp["meta_tokens"], inp["x"][0]], axis=0))
    meta2 = tiles(inp["meta_tokens_2"])
    col = lambda a: a.reshape(-1, P).T
    const = lambda x: np.full((P, 1), x, np.float32)
    taps = lambda w: w.T.reshape(CT, P, -1).transpose(1, 0, 2).reshape(P, -1)
    vecs = np.concatenate(
        [const(NORM_EPS), const(GN_EPS), const(LN_EPS), const(1.0)]
        + [col(inp[n][0]) for n in ("norm_mix_pre", "norm_mix_post", "norm_ffn_pre", "norm_ffn_post",
                                    "pre_mix_norm_2", "post_mix_norm_2", "pre_ffn_norm_2", "post_ffn_norm_2")]
        + [taps(inp["conv_a_w_2"][0]), taps(inp["conv_b_w_2"][0])]
        + [col(inp[n][0]) for n in ("conv_b_bias_2", "ln_b_gain_2", "ln_b_bias_2")], axis=1)
    consts, dec = constants()
    return dict(units=units, xfm=xfm, meta2=meta2, consts=consts, dec=dec, vecs=vecs)


def kernel(**inputs):
    import concourse.bacc as _bacc
    from concourse.bass_utils import run_bass_kernel_spmd as _run

    laid = lay_out({k: np.asarray(x) for k, x in inputs.items()})
    nc = _bacc.Bacc("TRN2", target_bir_lowering=False, num_devices=1)
    arrays, args = {}, []
    for name, a in laid.items():
        a = np.ascontiguousarray(a)
        arrays[f"in_{name}"] = a
        args.append(nc.dram_tensor(f"in_{name}", a.shape, mybir.dt.from_np(a.dtype), kind="ExternalInput").ap())
    args.append(nc.dram_tensor("out_0", (P, DT * SEQ), F32, kind="ExternalOutput").ap())
    build(nc, *args)
    r = _run(nc, [arrays], core_ids=[0])
    o = np.asarray(r.results[0]["out_0"])
    return o.reshape(P, DT, SEQ).transpose(2, 1, 0).reshape(1, SEQ, D)
```

```python
from contextlib import ExitStack

import numpy as np

import concourse.bass as bass
from concourse import mybir

F32 = mybir.dt.float32
F32R = mybir.dt.float32r
ACT = mybir.ActivationFunctionType
ALU = mybir.AluOpType

P = 128
D = 1024
DT = D // P
SEQ = 512
META = 16
FULL = META + SEQ
HALF = FULL // 2
UNIT = 2048
RET_HEADS, RET_DK, RET_DV = 4, 256, 512
QUADS = 4
SB_DH = 64
D_FF = 2816
FF_PAIRS = D_FF // 256
WA = WB = 512
CT = WA // P
TAPS_A, TAPS_B = 3, 31
NORM_EPS, GN_EPS, LN_EPS = 1e-6, 1e-5, 1e-5
BLOCKS = SEQ // P
KEY_OFF = [0, 512, 896, 1152]
KEY_LEN = [SEQ - P * b for b in range(BLOCKS)]
PACKED = sum(KEY_LEN)
KEY_BANK = [0, 1, 2, 2]
KEY_COL = [0, 0, 0, 256]
PARTS = [(0, 0, 512), (1, 512, 384), (2, 896, 384)]
BLOCKED = -(2.0 ** 100)
RQ_W = 4 * (SEQ + FULL)

STRIPS = {"P": 2, "R": 4, "D": 8}


def plan():
    phases = [
        ("quad_start", "P"),
        ("quad_first", "PPP"),
        ("quads", "PPDP" * (QUADS - 2)),
        ("quad_last", "PPD"),
        ("quad_end", "D"),
        ("head0", "PP"),
        ("gate_b", "P" * 4),
        ("heads", "PPPPPPRR" * 3),
        ("head_last", "PPPPPPPP"),
        ("head_out", "RR"),
        ("w_out", "P" * 4),
        ("ffn0", "PP"),
        ("ffn", "PPDPPD" * 5),
        ("ffn_end", "D"),
        ("conv_b", "PPPP"),
        ("conv_a", "PPPPPP"),
        ("w_out2_a", "RR"),
        ("w_out2_b", "RR"),
        ("ffn0_2", "PP"),
        ("ffn_2", "PPDPPD" * 4),
        ("ffn_last_2", "PPDPPD"),
        ("ffn_end_2", "D"),
    ]
    start, u, s = {}, 0, 0
    for name, kinds in phases:
        start[name] = (u, s)
        u += len(kinds)
        s += sum(STRIPS[k] for k in kinds)
    return start, u, s


START, N_UNITS, N_STRIPS = plan()


class Place:

    def __init__(self, phase, i=0, per_u=0, per_s=0, depth=2, first=0):
        assert per_u % 2 == 0 and per_s % depth == 0
        self.depth = depth
        self.first = first
        self.phase = phase
        self.u0, self.s0 = START[phase]
        self.i, self.per_u, self.per_s = i, per_u, per_s

    def unit(self, j):
        return self.u0 + j - self.per_u * self.first + self.per_u * self.i

    def ring(self, j):
        return (self.u0 + j) % 2

    def loads(self, j):
        return (self.u0 + j) // 2 + 1 - (self.per_u // 2) * self.first + (self.per_u // 2) * self.i

    def strip(self, j):
        return self.s0 + j - self.per_s * self.first + self.per_s * self.i

    def four(self):
        assert self.s0 % 4 == 0
        return Place(self.phase, self.i, self.per_u, self.per_s, 4, self.first)

    def bank(self, j):
        return (self.s0 + j) % self.depth * (4 // self.depth)


class Steps:

    def __init__(self, sem, names):
        self.sem, self.names, self.n = sem, list(names), 0
        self.index = {x: k for k, x in enumerate(self.names)}
        assert len(self.index) == len(self.names)

    def at(self, name, i=0):
        return self.index[name] + 1 + len(self.names) * i

    def step(self, name):
        want = self.names[self.n % len(self.names)]
        assert name == want, (name, want)
        self.n += 1
        return self.sem, 1


def build(nc, units, xfm, meta2, consts, dec, vecs, out):
    ctx = ExitStack()

    def sb(name, shape, dt=F32, where=ctx):
        return where.enter_context(nc.sbuf_tensor(name, shape, dt))

    def sem(name):
        return ctx.enter_context(nc.semaphore(name))

    X_hi = sb("X_hi", [P, DT, FULL], F32R)
    X_lo = sb("X_lo", [P, DT, FULL], F32R)
    acc = sb("acc", [P, DT, SEQ])
    w_raw = [sb(f"w_raw{n}", [P, UNIT]) for n in range(2)]
    w_hi = [sb(f"w_hi{n}", [P, UNIT], F32R) for n in range(2)]
    w_lo = [sb(f"w_lo{n}", [P, UNIT], F32R) for n in range(2)]
    ones = sb("ones", [P, P])
    vec = sb("vec", [P, VEC_COLS])
    psum = ctx.enter_context(nc.psum_tensor("psum", [P, 8, 512], F32))

    rot = sb("rot", [P, 2, FULL])
    mixer = ExitStack()
    sig = sb("sig", [P, 2, FULL], where=mixer)

    quad = ExitStack()
    Q_hi = sb("Q_hi", [P, 2, SEQ], F32R, quad)
    Q_lo = sb("Q_lo", [P, 2, SEQ], F32R, quad)
    K_hi = sb("K_hi", [P, 2, SEQ], F32R, quad)
    K_lo = sb("K_lo", [P, 2, SEQ], F32R, quad)
    V_hi = sb("V_hi", [P, 2 * BLOCKS, 3, SB_DH], F32R, quad)
    V_lo = sb("V_lo", [P, 2 * BLOCKS, 3, SB_DH], F32R, quad)
    XM_hi = sb("XM_hi", [P, DT, P], F32R, quad)
    XM_lo = sb("XM_lo", [P, DT, P], F32R, quad)
    XM2 = sb("XM2", [P, DT, 2, META], F32R, quad)
    KM = sb("KM", [P, P], F32, quad)
    KM_x = sb("KM_x", [P, 2, META], F32, quad)
    KM_hi = sb("KM_hi", [P, P], F32R, quad)
    KM_lo = sb("KM_lo", [P, P], F32R, quad)
    VM = sb("VM", [P, 2, P], F32, quad)
    VM_hi = sb("VM_hi", [P, 2, P], F32R, quad)
    VM_lo = sb("VM_lo", [P, 2, P], F32R, quad)
    sp = sb("sp", [P, PACKED], F32, quad)
    sp_hi = sb("sp_hi", [P, PACKED], F32R, quad)
    sp_lo = sb("sp_lo", [P, PACKED], F32R, quad)
    sp_all_hi = sb("sp_all_hi", [P, SEQ], F32R, quad)
    sp_all_lo = sb("sp_all_lo", [P, SEQ], F32R, quad)
    a_f = sb("a_f", [P, PACKED], F32, quad)
    a_hi = sb("a_hi", [P, PACKED], F32R, quad)
    a_lo = sb("a_lo", [P, PACKED], F32R, quad)
    m_f = sb("m_f", [P, SEQ], F32, quad)
    m_hi = sb("m_hi", [P, SEQ], F32R, quad)
    m_lo = sb("m_lo", [P, SEQ], F32R, quad)
    Y = sb("Y", [P, SEQ], F32, quad)
    Y_hi = sb("Y_hi", [P, 2, SEQ], F32R, quad)
    Y_lo = sb("Y_lo", [P, 2, SEQ], F32R, quad)
    cmat = sb("cmat", [P, N_CMAT, P], F32R, quad)
    mask_k = sb("mask_k", [P, 2, META], F32, quad)
    mask_v = sb("mask_v", [P, P], F32, quad)
    quad.close()

    head = ExitStack()
    ret = sb("ret", [P, DT, SEQ], F32, head)
    qk = ExitStack()
    RQ_hi = sb("RQ_hi", [P, 2, SEQ], F32R, qk)
    RQ_lo = sb("RQ_lo", [P, 2, SEQ], F32R, qk)
    RK_hi = sb("RK_hi", [P, 2, FULL], F32R, qk)
    RK_lo = sb("RK_lo", [P, 2, FULL], F32R, qk)
    qk.close()
    gate = sb("gate", [P, DT, (RQ_W + 7) // 8], F32, head)
    turned = sb("turned", [P, 2, FULL], F32, head)
    RY = sb("RY", [P, 4, SEQ], F32, head)
    VZ_hi = sb("VZ_hi", [P, 4, SEQ], F32R, head)
    VZ_lo = sb("VZ_lo", [P, 4, SEQ], F32R, head)
    RVM_hi = sb("RVM_hi", [META, SEQ], F32R, head)
    RVM_lo = sb("RVM_lo", [META, SEQ], F32R, head)
    S_f = sb("S_f", [P, PACKED], F32, head)
    S_hi = sb("S_hi", [P, PACKED], F32R, head)
    S_lo = sb("S_lo", [P, PACKED], F32R, head)
    SM_f = sb("SM_f", [META, SEQ], F32, head)
    SM_hi = sb("SM_hi", [META, SEQ], F32R, head)
    SM_lo = sb("SM_lo", [META, SEQ], F32R, head)
    decay = sb("decay", [P, 2, SEQ], F32, head)
    r_std = sb("r_std", [P, SEQ], F32, head)
    silu_g = sb("silu_g", [P, 4, SEQ], F32, head)
    head.close()
    mixer.close()

    h = sb("h", [P, DT, FULL])
    std = sb("std", [P, FULL])
    sq = sb("sq", [P, 2, FULL])
    normed = sb("normed", [P, 2, FULL])
    meta2_f = sb("meta2_f", [P, DT, META])
    ffns = ExitStack()
    M_hi = sb("M_hi", [P, 2, 2, SEQ], F32R, ffns)
    M_lo = sb("M_lo", [P, 2, 2, SEQ], F32R, ffns)
    silu_a = sb("silu_a", [P, 2, SEQ], F32, ffns)
    ffns.close()
    conv_sig = sb("conv_sig", [P, 2, FULL])
    glu = sb("glu", [P, CT, TAPS_B - 1 - META + FULL])
    glu_val = sb("glu_val", [P, 2, FULL])
    c_in = sb("c_in", [P, 2, FULL])
    u_in = sb("u_in", [P, 2, FULL])
    b_in = sb("b_in", [P, 2, SEQ])
    z = sb("z", [P, CT, SEQ])
    y2_hi = sb("y2_hi", [P, DT, SEQ], F32R)
    y2_lo = sb("y2_lo", [P, DT, SEQ], F32R)

    consts_in = sem("consts_in")
    rot_in = sem("rot_in")
    cmat_ready = sem("cmat_ready")
    w_loaded = [sem("w_loaded0"), sem("w_loaded1")]
    w_hi_ready = sem("w_hi_ready")
    w_lo_ready = sem("w_lo_ready")
    strip_done = sem("strip_done")
    strip_free = sem("strip_free")
    x_in = [sem(f"x_in{n}") for n in range(4)]
    vec_in = sem("vec_in")
    ones_ready = sem("ones_ready")
    x_loaded = sem("x_loaded")
    decay_loaded = sem("decay_loaded")
    memset_done = sem("memset_done")
    stored = sem("stored")

    sq_done = sem("sq_done")
    sq_added = sem("sq_added")
    std_ready = sem("std_ready")
    norm_scaled = sem("norm_scaled")
    x_hi_ready = sem("x_hi_ready")
    x_lo_ready = sem("x_lo_ready")
    post_done = sem("post_done")

    qk_act = Steps(sem("qk_act"), ["K_hi", "KM_hi", "Q_hi"])
    qk_dve = Steps(sem("qk_dve"), ["K_lo", "KM_part", "KM", "KM_lo"])
    mk_act = Steps(sem("mk_act"), ["m_abs", "m_exp", "m_ln", "m_hi", "am_exp", "am_hi"])
    mk_dve = Steps(sem("mk_dve"), ["m_sp", "m_lo", "am_lo"])
    mk_pe = Steps(sem("mk_pe"), ["m_scores", "m_rows", "y_meta"])
    y_out = sem("y_out")
    y_hi_ready = sem("y_hi_ready")
    y_lo_ready = sem("y_lo_ready")
    v_act = Steps(sem("v_act"), ["V_hi0", "VM_hi", "V_hi1"])
    v_dve = Steps(sem("v_dve"), ["V_lo0", "VM_lo"])
    hd_act = Steps(sem("hd_act"), ["abs1", "abs2", "abs0", "exp1", "exp0", "ln1", "ln0", "hi1", "hi0", "all_hi",
                                   "a_part0", "a_part1", "a_part2", "a_hi"])
    hd_dve = Steps(sem("hd_dve"), ["sp1", "sp2", "sp0", "sp_lo1", "sp_lo0", "all1", "all2", "all3", "all_lo", "a_lo"])
    hd_pe = Steps(sem("hd_pe"), ["scores", "logs"])
    t_act = Steps(sem("t_act"), ["RQ_hi0", "RQ_hi1", "RK_hi0", "RK_hi1"])
    t_dve = Steps(sem("t_dve"), ["q_cos", "q_sin", "q_r1", "q_r2", "q_lo",
                                 "k_cos", "k_sin", "k_r1", "k_r2", "k_lo"])
    r_act = Steps(sem("r_act"), ["V_hi0", "VM_hi0", "V_hi1", "V_hi2", "VM_hi1", "V_hi3",
                                 "S_hi", "SM_hi", "g_sig0", "g_sig1", "g_sig2", "g_sig3",
                                 "y_sq0", "y_sq1", "y_sq2", "y_sq3", "ln", "std",
                                 "z_hi0", "z_hi1", "z_hi2", "z_hi3"])
    r_dve = Steps(sem("r_dve"), ["V_lo0", "V_lo2", "S0", "S1", "S2", "S3", "SM", "S_lo", "SM_lo",
                                 "y0", "y1", "y2", "y3", "ys1", "ys2", "ys3",
                                 "yc0", "yc1", "yc2", "yc3", "sqs1", "sqs2", "sqs3", "yg",
                                 "z0", "z1", "z_lo0", "z2", "z_lo1", "z3", "z_lo2", "z_lo3"])
    r_pe = Steps(sem("r_pe"), ["scores", "y", "mean", "var"])
    premixed = sem("premixed")
    mixed = sem("mixed")
    quad_ready = sem("quad_ready")
    gate_used = sem("gate_used")
    m_split_hi = sem("m_split_hi")
    m_split_lo = sem("m_split_lo")
    f_act = Steps(sem("f_act"), ["sig0", "sig1", "M_hi"])
    f_dve = Steps(sem("f_dve"), ["prod", "M_lo"])
    acc_zero = sem("acc_zero")
    ret_zero = sem("ret_zero")
    c_act = Steps(sem("c_act"), ["y_hi0", "y_hi1", "y_hi2", "y_hi3", "zsq0", "zsq1", "zsq2", "zsq3", "ln", "std",
                                 "sig0", "lin0", "sig1", "lin1", "zhi0", "sig2", "lin2", "zhi1",
                                 "sig3", "lin3", "zhi2", "zhi3"])
    short = [f"ca{c}_{k}" for k in range(TAPS_A) for c in range(2)]
    c_dve = Steps(sem("c_dve"), ["pad", "glu0", "glu1", "glu2", "glu3", "u0", "u1"] + short + ["ya0", "ya1", "u2", "u3"]
                  + ["2nd" + x for x in short] + ["ya2", "ya3"]
                  + [f"{x}{t}" for x in ("zc", "zn", "yb") for t in range(CT)])
    c_pe = Steps(sem("c_pe"), [f"{x}{t}" for x in ("mean", "var") for t in range(CT)])
    y2_ready = sem("y2_ready")
    conv_step = sem("conv_step")

    def ring3(u_hi_or_lo, kind):
        k, c = {"P": (8, 256), "R": (4, 512), "D": (2, 1024)}[kind]
        return u_hi_or_lo[:, :].rearrange("p (k c) -> p k c", k=k, c=c)

    def strip_view(bank, width):
        if width == FULL:
            return psum[:, bank:bank + 2, 0:HALF]
        return psum[:, bank, 0:SEQ]

    def wide(ap):
        return ap.rearrange("p (a b) -> p a b", a=2)

    def as_f32(ap):
        return ap.bitcast(F32)

    def g_col(name, k):
        o = VEC[name] + k
        return vec[:, o:o + 1]

    def loop(eng, n, body, peel=0):
        for i in range(peel):
            body(i)
        if peel == n:
            return
        with eng.Fori(peel, n) as i:
            body(i)

    block = ctx.enter_context(nc.Block())

    @block.sync
    def _(sync):
        for n in range(4):
            sync.dma_start(h[:, 2 * n:2 * n + 2, :].rearrange("p a b -> p (a b)"),
                           xfm[:, 2 * FULL * n:2 * FULL * (n + 1)]).then_inc(x_in[n], 16)
            if n == 0:
                sync.dma_start(vec[:, :], vecs).then_inc(vec_in, 16)
        def constant(dst, n):
            sync.dma_start(dst, consts[:, CONST[n]:CONST[n + 1]]).then_inc(rot_in if n == 2 else consts_in, 16)

        sync.dma_start(w_raw[0][:, :], units[0, :, :]).then_inc(w_loaded[0], 16)
        constant(mask_k[:, :, :].rearrange("p a b -> p (a b)"), 0)
        constant(mask_v[:, :], 1)
        constant(acc[:, 0:2, :].rearrange("p a b -> p (a b)")[:, 0:N_CMAT * P], 3)
        sync.dma_start(w_raw[1][:, :], units[1, :, :]).then_inc(w_loaded[1], 16)
        constant(rot[:, :, :].rearrange("p a b -> p (a b)"), 2)

        def load(u, slot):
            sync.wait_ge(w_hi_ready, u - 1)
            sync.wait_ge(w_lo_ready, u - 1)
            sync.dma_start(w_raw[slot][:, :], units[bass.ds(u, 1), :, :].rearrange("a p c -> (a p) c"))\
                .then_inc(w_loaded[slot], 16)

        def load_decay(n):
            if n > 0:
                sync.wait_ge(r_dve.sem, r_dve.at("SM", n - 1))
            sync.dma_start(decay[:, :, :].rearrange("p a b -> p (a b)"), dec[n, :, :]).then_inc(decay_loaded, 16)

        def loads(first, last):
            n = (last - first) // 2
            if last <= first:
                return

            def body(i):
                for slot in range(2):
                    load(first + 2 * i + slot, (first + slot) % 2)
            loop(sync, n, body)
            if (last - first) % 2:
                load(last - 1, (last - 1) % 2)

        loads(2, START["head0"][0] + 2)
        sync.wait_ge(strip_free, START["head0"][1])
        load_decay(0)
        loads(START["head0"][0] + 2, START["heads"][0] + 6)
        for n in range(1, RET_HEADS):
            load_decay(n)
            loads(START["heads"][0] + 8 * (n - 1) + 6, START["heads"][0] + 8 * n + (6 if n < RET_HEADS - 1 else 2))
        loads(START["head_last"][0] + 2, START["ffn0"][0] - 2)
        sync.wait_ge(m_split_lo, DT)
        sync.dma_start(h[:, :, :].rearrange("p a b -> p (a b)"), xfm).then_inc(x_loaded, 16)
        sync.dma_start(meta2_f[:, :, :].rearrange("p a b -> p (a b)"), meta2).then_inc(x_loaded, 16)
        loads(START["ffn0"][0] - 2, N_UNITS)
        for n in range(4):
            sync.wait_ge(post_done, 3 * DT + 2 * n + 2)
            sync.dma_start(out.rearrange("p (a b) -> p a b", a=DT)[:, 2 * n:2 * n + 2, :],
                           h[:, 2 * n:2 * n + 2, META:FULL]).then_inc(stored, 16)
        sync.wait_ge(stored, 16 * 4)

    @block.gpsimd
    def _(pool):
        nc.gpsimd.memset(ones[:, :], 1.0).then_inc(ones_ready, 1)
        pool.wait_ge(x_lo_ready, DT)
        nc.gpsimd.memset(KM[:, :], 0.0).then_inc(memset_done, 1)
        pool.wait_ge(cmat_ready, 1)
        nc.gpsimd.memset(acc[:, :, :], 0.0).then_inc(memset_done, 1)
        pool.wait_ge(strip_free, START["head0"][1])
        nc.gpsimd.memset(ret[:, :, :], 0.0).then_inc(ret_zero, 1)
        for n in range(2):
            pool.wait_ge(post_done, (2 * n + 1) * DT)
            nc.gpsimd.memset(acc[:, :, :], 0.0).then_inc(acc_zero, 1)

    @block.tensor
    def _(pe):
        def mm3(dst, w2, x2, first, last, sig=None):
            nc.tensor.matmul(dst, w2[0], x2[0], start=first, stop=False, skip_group_check=True)
            nc.tensor.matmul(dst, w2[0], x2[1], start=False, stop=False, skip_group_check=True)
            m = nc.tensor.matmul(dst, w2[1], x2[0], start=False, stop=last, skip_group_check=True)
            if sig:
                m.then_inc(*sig)

        def take(at, s, after_wide=None):
            if after_wide is not None and after_wide < 3:
                pe.wait_ge(strip_free, at.strip(s) - (1, 2, 2)[after_wide])
            elif not (type(at.strip(s)) is int and at.strip(s) < at.depth):
                pe.wait_ge(strip_free, at.strip(s) + 1 - at.depth)

        def unit(at, j, s, kind, width, x, cs=None, ready=None, after_wide=False):
            pe.wait_ge(w_lo_ready, at.unit(j) + 1)
            w = [ring3(r[at.ring(j)], kind) for r in (w_hi, w_lo)]
            tiles = {"P": 8, "R": 4, "D": 2}[kind]
            cs = range(STRIPS[kind]) if cs is None else cs
            groups = [cs[:2]] + [[c] for c in cs[2:]] if ready else [[c] for c in cs]
            halves = [(0, HALF), (HALF, FULL)] if width == FULL else [(META, FULL)]
            for group in groups:
                for c in group:
                    take(at, s + c, c if after_wide else None)
                for k in range(tiles):
                    if ready and group is groups[0]:
                        pe.wait_ge(*ready(k))
                    for c in group:
                        for n, (a, b) in enumerate(halves):
                            end = k == tiles - 1 and n == len(halves) - 1
                            mm3(psum[:, at.bank(s + c) + n, 0:b - a], [y[:, k, c * P:(c + 1) * P] for y in w],
                                x(k, a, b), k == 0, k == tiles - 1, (strip_done, 1) if end else None)

        def counted(sem, before):
            return lambda k: (sem, before + k + 1)

        def from_x(k, a, b):
            return X_hi[:, k, a:b], X_lo[:, k, a:b]

        def seq_of(hi, lo):
            return lambda k, a, b: (hi[:, k, a - META:b - META], lo[:, k, a - META:b - META])

        def sums(n, width, ks=range(DT)):
            if n and ks[0] == 0:
                pe.wait_ge(std_ready, 2 * n - 1)
            halves = [(0, HALF), (HALF, FULL)] if width == FULL else [(0, SEQ)]
            for k in ks:
                pe.wait_ge(sq_done, DT * n + k + 1)
                for hf, (a, b) in enumerate(halves):
                    m = nc.tensor.matmul(psum[:, 6 + hf, 0:b - a], ones[:, :], sq[:, k % 2, a:b],
                                         start=k == 0, stop=k == DT - 1, skip_group_check=True)
                m.then_inc(sq_added, 1)

        def keep_warm(n, bank=5):
            for _ in range(n):
                nc.tensor.matmul(psum[:, bank, 0:P], ones[:, :], ones[:, :], start=True, stop=True)

        pe.wait_ge(ones_ready, 1)
        sums(0, FULL)
        keep_warm(36)
        def split(hi, lo, *ix):
            return hi[ix], lo[ix]

        ALL = slice(None)

        def value_strip(at, j, s, half, meta):
            pe.wait_ge(w_lo_ready, at.unit(j) + 1)
            take(at, s)
            w = [ring3(r[at.ring(j)], "P") for r in (w_hi, w_lo)]
            parts = [(0, n * 256, split(X_hi, X_lo, ALL, ALL, slice(META + b * P, META + (b + 1) * P)))
                     for n, b in enumerate((2 * half, 2 * half + 1))]
            if half == 0:
                parts.append((1, 0, meta))
            for nb, col, x in parts:
                for k in range(DT):
                    end = x is parts[-1][2] and k == DT - 1
                    mm3(psum[:, at.bank(s) + nb, col:col + 256], (x[0][:, k], x[1][:, k]),
                        (w[0][:, k, :], w[1][:, k, :]), k == 0 and col == 0, k == DT - 1,
                        (strip_done, 1) if end else None)

        def key_strip(at, j, s, ready=None, first=False):
            pe.wait_ge(w_lo_ready, at.unit(j) + 1)
            take(at, s)
            w = [ring3(r[at.ring(j)], "P") for r in (w_hi, w_lo)]
            for k in range(DT):
                if ready:
                    pe.wait_ge(*ready(k))
                mm3(psum[:, at.bank(s), :], [y[:, k, 0:P] for y in w], from_x(k, META, FULL), k == 0, k == DT - 1)
            if first:
                pe.wait_ge(quad_ready, 2)
            for k in range(DT):
                nc.tensor.matmul(psum[:, at.bank(s) + 1, 0:2 * META], w[0][:, k, 0:P],
                                 XM2[:, k, :, :].rearrange("p a m -> p (a m)"), start=k == 0, stop=False,
                                 skip_group_check=True)
                m = nc.tensor.matmul(psum[:, at.bank(s) + 1, 0:META], w[1][:, k, 0:P], XM2[:, k, 0, :],
                                     start=False, stop=k == DT - 1, skip_group_check=True)
            m.then_inc(strip_done, 1)

        def scores(t, r, at, s, g):
            pe.wait_ge(strip_free, at.strip(s) + 1)
            if not (type(g) is int and g == 0):
                pe.wait_ge(hd_act.sem, hd_act.at("a_part2", g - 1))
            rows = slice(SB_DH * r, SB_DH * (r + 1))
            for b in range(BLOCKS):
                dst = psum[:, 4 + KEY_BANK[b], KEY_COL[b]:KEY_COL[b] + KEY_LEN[b]]
                mm3(dst, split(K_hi, K_lo, rows, t, slice(b * P, (b + 1) * P)),
                    split(Q_hi, Q_lo, rows, t, slice(b * P, SEQ)), b < 3, False)
                m = nc.tensor.matmul(psum[:, 4 + KEY_BANK[b], KEY_COL[b]:KEY_COL[b] + P],
                                     cmat[:, C_IDENT, :], cmat[:, C_BLOCKED, :], start=False, stop=False,
                                     skip_group_check=True)
            m.then_inc(*hd_pe.step("scores"))

        def logs(g):
            pe.wait_ge(hd_dve.sem, hd_dve.at("sp_lo0", g))
            for b in range(BLOCKS):
                for b2 in range(b, BLOCKS):
                    c0 = KEY_COL[b] + P * (b2 - b)
                    for x in (sp_hi, sp_lo):
                        m = nc.tensor.matmul(psum[:, 4 + KEY_BANK[b], c0:c0 + KEY_LEN[b2]],
                                             cmat[:, C_TRI if b2 == b else C_ALL, :],
                                             x[:, KEY_OFF[b2]:KEY_OFF[b2] + KEY_LEN[b2]],
                                             start=False, stop=False, skip_group_check=True)
            m.then_inc(*hd_pe.step("logs"))

        def meta_scores(t, p):
            pe.wait_ge(qk_dve.sem, qk_dve.at("KM_lo", p))
            mm3(psum[:, 7, :], (KM_hi[:, :], KM_lo[:, :]), split(Q_hi, Q_lo, ALL, t, ALL), True, False,
                mk_pe.step("m_scores"))

        def meta_logs(r, p, g):
            if r == 0:
                pe.wait_ge(mk_dve.sem, mk_dve.at("m_lo", p))
                for x in (m_hi, m_lo):
                    nc.tensor.matmul(psum[:, 7, :], cmat[:, C_TRI_META, :], x[:, :], start=False, stop=False,
                                     skip_group_check=True)
            pe.wait_ge(hd_dve.sem, hd_dve.at("all_lo", g))
            for x in (sp_all_hi, sp_all_lo):
                m = nc.tensor.matmul(psum[:, 7, :], cmat[:, C_ROWS + r, :], x[:, :], start=False, stop=False,
                                     skip_group_check=True)
            if r == 1:
                m.then_inc(*mk_pe.step("m_rows"))

        def outputs(t, r, g, p):
            pe.wait_ge(hd_dve.sem, hd_dve.at("a_lo", g))
            if r == 0 and not (type(p) is int and p == 0):
                pe.wait_ge(y_out, p)
            for b in range(BLOCKS):
                vw = [x[:, 2 * b + t, r:r + 2, :].rearrange("p a c -> p (a c)") for x in (V_hi, V_lo)]
                mm3(psum[:, 3, b * P:SEQ], vw,
                    split(a_hi, a_lo, ALL, slice(KEY_OFF[b], KEY_OFF[b] + KEY_LEN[b])),
                    r == 0 and b == 0, False)

        def meta_outputs(t, p):
            pe.wait_ge(mk_dve.sem, mk_dve.at("am_lo", p))
            mm3(psum[:, 3, :], split(VM_hi, VM_lo, ALL, t, ALL), (m_hi[:, :], m_lo[:, :]), False, True,
                mk_pe.step("y_meta"))

        def quad_body(at, i, has_d, has_next):
            g, p = 4 * i, 2 * i
            dj, ds = 2, 4
            nj, ns = (3, 12) if has_d else (2, 4)
            value_strip(at, 0, 0, 0, (XM_hi, XM_lo))
            logs(g)
            value_strip(at, 0, 1, 1, None)
            meta_logs(0, p, g)
            scores(0, 1, at, 1, g + 1)
            pe.wait_ge(v_dve.sem, v_dve.at("VM_lo", i))
            pe.wait_ge(strip_free, at.strip(1) + 1)
            outputs(0, 0, g, p)
            key_strip(at, 1, 2)
            logs(g + 1)
            unit(at, 1, 2, "P", SEQ, from_x, [1])
            meta_logs(1, p, g + 1)
            outputs(0, 1, g + 1, p)
            scores(1, 0, at, 3, g + 2)
            meta_outputs(0, p)
            meta_scores(1, p + 1)
            y = seq_of(Y_hi, Y_lo)
            if has_d:
                pe.wait_ge(y_lo_ready, p)
                unit(at, dj, ds, "D", SEQ, y, range(4))
            else:
                keep_warm(24, 2)
            logs(g + 2)
            if has_d:
                unit(at, dj, ds, "D", SEQ, y, range(4, 8))
            meta_logs(0, p + 1, g + 2)
            scores(1, 1, at, 3, g + 3)
            outputs(1, 0, g + 2, p + 1)
            if has_next:
                key_strip(at, nj, ns)
            else:
                pe.wait_ge(strip_free, at.strip(11) + 1)
                keep_warm(20, 2)
            logs(g + 3)
            if has_next:
                unit(at, nj, ns, "P", SEQ, from_x, [1])
            meta_logs(1, p + 1, g + 3)
            outputs(1, 1, g + 3, p + 1)
            if has_next:
                scores(0, 0, at, ns + 1, g + 4)
            meta_outputs(1, p + 1)
            if has_next:
                meta_scores(0, p + 2)

        at = Place("quad_start")
        key_strip(at, 0, 0, counted(x_lo_ready, 0), True)
        unit(at, 0, 0, "P", SEQ, from_x, [1])
        pe.wait_ge(cmat_ready, 1)
        pe.wait_ge(quad_ready, 6)
        scores(0, 0, at, 1, 0)
        meta_scores(0, 0)
        quad_body(Place("quad_first"), 0, False, True)
        with pe.Fori(1, QUADS - 1) as i:
            quad_body(Place("quads", i, 4, 14, first=1), i, True, True)
        quad_body(Place("quad_last"), QUADS - 1, True, False)
        pe.wait_ge(y_lo_ready, 2 * QUADS)
        unit(Place("quad_end"), 0, 0, "D", SEQ, seq_of(Y_hi, Y_lo))

        def gates(phase):
            def body(i):
                at = Place(phase, i, 2, 4)
                for j in range(2):
                    unit(at, j, 2 * j, "P", SEQ, from_x)
            loop(pe, 2, body)

        def ret_scores(i):
            pe.wait_ge(t_dve.sem, t_dve.at("k_lo", i))
            for b in range(BLOCKS):
                for t in range(2):
                    mm3(psum[:, 4 + KEY_BANK[b], KEY_COL[b]:KEY_COL[b] + KEY_LEN[b]],
                        split(RK_hi, RK_lo, ALL, t, slice(META + b * P, META + (b + 1) * P)),
                        split(RQ_hi, RQ_lo, ALL, t, slice(b * P, SEQ)), t == 0 and b < 3, t == 1)
            for t in range(2):
                mm3(psum[:, 7, :], split(RK_hi, RK_lo, ALL, t, slice(0, P)),
                    split(RQ_hi, RQ_lo, ALL, t, ALL), t == 0, t == 1,
                    r_pe.step("scores") if t else None)

        def mean():
            nc.tensor.matmul(psum[:, 4, :], ones[:, :], S_f[:, 0:SEQ], start=True, stop=True)\
                .then_inc(*r_pe.step("mean"))

        def var():
            nc.tensor.matmul(psum[:, 5, :], ones[:, :], S_f[:, 0:SEQ], start=True, stop=True)\
                .then_inc(*r_pe.step("var"))

        plain_meta = [x[:, :, 0:P] for x in (X_hi, X_lo)]

        def head_body(at, i, has_next):
            for n in range(2):
                for half in range(2):
                    value_strip(at, n, 2 * n + half, half, plain_meta)
            for n in range(2):
                unit(at, 2 + n, 4 + 2 * n, "P", SEQ, from_x)
            pe.wait_ge(r_dve.sem, r_dve.at("SM_lo", i))
            for e in range(4):
                for b in range(BLOCKS):
                    mm3(psum[:, 4 + e, b * P:SEQ],
                        split(VZ_hi, VZ_lo, ALL, b, slice(e * P, (e + 1) * P)),
                        split(S_hi, S_lo, ALL, slice(KEY_OFF[b], KEY_OFF[b] + KEY_LEN[b])),
                        b == 0, False)
                mm3(psum[:, 4 + e, :], split(RVM_hi, RVM_lo, ALL, slice(e * P, (e + 1) * P)),
                    (SM_hi[:, :], SM_lo[:, :]), False, True, r_pe.step("y") if e == 3 else None)
            kw = FULL if has_next else SEQ
            unit(at, 4, 8, "P", SEQ, from_x, [0])
            pe.wait_ge(r_dve.sem, r_dve.at("ys3", i))
            mean()
            unit(at, 4, 8, "P", SEQ, from_x, [1])
            unit(at, 5, 10, "P", kw, from_x, [0])
            pe.wait_ge(r_dve.sem, r_dve.at("sqs3", i))
            var()
            unit(at, 5, 10, "P", kw, from_x, [1])
            if has_next:
                out_units(at.four(), 6, 12, i)
                ret_scores(i + 1)
            else:
                for n in range(2):
                    unit(at, 6 + n, 12 + 2 * n, "P", SEQ, from_x)

        def out_units(at, j, s, i):
            for n in range(2):
                unit(at, j + n, s + 4 * n, "R", SEQ, seq_of(VZ_hi, VZ_lo), None,
                     None if n else lambda k: (r_dve.sem, r_dve.at(f"z_lo{k}", i)), n == 0)

        at = Place("head0")
        unit(at, 0, 0, "P", SEQ, from_x)
        unit(at, 1, 2, "P", FULL, from_x)
        gates("gate_b")
        ret_scores(0)
        loop(pe, RET_HEADS - 1, lambda i: head_body(Place("heads", i, 8, 20), i, True))
        head_body(Place("head_last"), RET_HEADS - 1, False)
        out_units(Place("head_out").four(), 0, 0, RET_HEADS - 1)

        def out_product(phase, x, n, ready=None):
            at = Place(phase).four()
            for j in range(4):
                unit(at, j, 2 * j, "P", SEQ, x, None, ready if j == 0 else None)
                if j:
                    sums(n, SEQ, range(2 * j - 2, 2 * j))
            sums(n, SEQ, range(DT - 2, DT))

        out_product("w_out", from_x, 1, counted(m_split_lo, 0))
        keep_warm(16)
        sums(2, SEQ)
        keep_warm(14)

        def ffn(tag, n):
            def up(at, j, s, ready=None):
                unit(at, j, s, "P", SEQ, from_x, None, ready)
                unit(at, j + 1, s + 2, "P", SEQ, from_x)

            def down(at, j, s, i, slot):
                pe.wait_ge(f_dve.sem, f_dve.at("M_lo", i))
                unit(at, j, s, "D", SEQ, lambda k, a, b: (M_hi[:, slot, k, :], M_lo[:, slot, k, :]))

            def two(at, i0):
                for m in range(2):
                    up(at, 3 * m, 12 * m)
                    down(at, 3 * m + 2, 12 * m + 4, i0 + m, m)
            base = FF_PAIRS * n
            up(Place("ffn0" + tag, depth=4), 0, 0, counted(x_lo_ready, (2 * n + 1) * DT))
            rounds = 5 if n == 0 else 4
            loop(pe, rounds, lambda i: two(Place("ffn" + tag, i, 6, 24, 4), base + 2 * i))
            if n:
                two(Place("ffn_last" + tag, depth=4), base + 2 * rounds)
            down(Place("ffn_end" + tag, depth=4), 0, 0, base + FF_PAIRS - 1, 0)

        ffn("", 0)
        sums(3, SEQ)
        keep_warm(16)
        sums(4, FULL)
        keep_warm(14)
        at = Place("conv_b")
        for j in range(4):
            unit(at, j, 2 * j, "P", FULL, from_x, None, counted(x_lo_ready, 2 * DT) if j == 0 else None)
        at = Place("conv_a")
        for j in range(6):
            unit(at, j, 2 * j, "P", FULL if j % 3 < 2 else SEQ, from_x)
        y2 = seq_of(y2_hi, y2_lo)
        at = Place("w_out2_a")
        for j in range(2):
            unit(at, j, 4 * j, "R", SEQ, y2, None, counted(y2_ready, 0) if j == 0 else None)
        keep_warm(45)
        for t in range(CT):
            pe.wait_ge(conv_step, z_done(t))
            nc.tensor.matmul(psum[:, 4, :], ones[:, :], z[:, t, :], start=t == 0, stop=t == CT - 1,
                             skip_group_check=True).then_inc(*c_pe.step(f"mean{t}"))
        for t in range(CT):
            pe.wait_ge(c_act.sem, c_act.at(f"zsq{t}"))
            nc.tensor.matmul(psum[:, 5, :], ones[:, :], sq[:, t % 2, 0:SEQ], start=t == 0, stop=t == CT - 1,
                             skip_group_check=True).then_inc(*c_pe.step(f"var{t}"))
        keep_warm(30, 4)
        at = Place("w_out2_b").four()
        for j in range(2):
            unit(at, j, 4 * j, "R", SEQ, lambda k, a, b: y2(CT + k, a, b), None,
                 counted(y2_ready, CT) if j == 0 else None, j == 0)
        sums(5, SEQ)
        keep_warm(16)
        sums(6, SEQ)
        keep_warm(14)
        ffn("_2", 1)
        sums(7, SEQ)

    @block.scalar
    def _(act):
        def a(out_, in_, f, **kw):
            return nc.scalar.activation(out_, in_, f, **kw)

        def split_hi(at, j):
            act.wait_ge(w_loaded[at.ring(j)], 16 * (at.loads(j) + 1))
            a(w_hi[at.ring(j)][:, :], w_raw[at.ring(j)][:, :], ACT.Copy).then_inc(w_hi_ready, 1)

        def strips(at, s, n=1):
            act.wait_ge(strip_done, at.strip(s) + n)

        def norm(n, src, width, k_split=None):
            use("ln, exp")
            for k in range(DT):
                if DT * n + k >= 2:
                    act.wait_ge(sq_added, DT * n + k - 1)
                src(k)
            act.wait_ge(sq_added, DT * (n + 1))
            if n == 0:
                act.wait_ge(vec_in, 16)
            if width == FULL:
                dst, ps = wide(std[:, :]), psum[:, 6:8, 0:HALF]
            else:
                dst, ps = std[:, 0:SEQ], psum[:, 6, :]
            if n:
                act.wait_ge(norm_scaled, DT * n)
            a(dst, ps, ACT.Ln, scale=1.0 / D, bias=g_col("norm_eps", 0)).then_inc(std_ready, 1)
            act.wait_ge(std_ready, 2 * n + 1)
            a(dst, dst, ACT.Exp, scale=-0.5).then_inc(std_ready, 1)
            if k_split is not None:
                for k in range(DT):
                    if k == 2 and n == 0:
                        first_hi(0)
                    act.wait_ge(norm_scaled, DT * n + k + 1)
                    a(X_hi[:, k, 0:width] if width == FULL else X_hi[:, k, META:FULL],
                      normed[:, k % 2, 0:width], ACT.Copy).then_inc(x_hi_ready, 1)

        def squares(n, tile, width, ready):
            def src(k):
                ready(k)
                a(sq[:, k % 2, 0:width], tile(k), ACT.Square).then_inc(sq_done, 1)
            return src

        def use(functions):
            act.preload_act_table_set({"ln, exp": "natural_log_exp_and_others",
                                       "sigmoid": "sigmoid_and_others"}[functions])

        def first_hi(u):
            act.wait_ge(w_loaded[u], 16)
            a(w_hi[u][:, :], w_raw[u][:, :], ACT.Copy).then_inc(w_hi_ready, 1)

        norm(0, squares(0, lambda k: h[:, k, :], FULL, lambda k: act.wait_ge(x_in[k // 2], 16)), FULL, 0)
        act.wait_ge(consts_in, 16 * 3)
        a(cmat[:, :, :].rearrange("p a b -> p (a b)"), acc[:, 0:2, :].rearrange("p a b -> p (a b)")[:, 0:N_CMAT * P],
          ACT.Copy).then_inc(cmat_ready, 1)

        H1, H0 = slice(SEQ, PACKED), slice(0, SEQ)

        def softplus(g):
            act.wait_ge(hd_pe.sem, hd_pe.at("scores", g))
            for n in (1, 2, 0):
                bank, off, w = PARTS[n]
                a(sp[:, off:off + w], psum[:, 4 + bank, 0:w], ACT.Abs).then_inc(*hd_act.step(f"abs{n}"))
            for n, cols, ready in ((1, H1, "abs2"), (0, H0, "abs0")):
                act.wait_ge(hd_act.sem, hd_act.at(ready, g))
                a(sp[:, cols], sp[:, cols], ACT.Exp, scale=-1.0).then_inc(*hd_act.step(f"exp{n}"))
            for n, cols in ((1, H1), (0, H0)):
                act.wait_ge(hd_act.sem, hd_act.at(f"exp{n}", g))
                a(sp[:, cols], sp[:, cols], ACT.Ln, bias=g_col("one", 0)).then_inc(*hd_act.step(f"ln{n}"))
            for n, cols, ready in ((1, H1, "sp2"), (0, H0, "sp0")):
                act.wait_ge(hd_dve.sem, hd_dve.at(ready, g))
                a(sp_hi[:, cols], sp[:, cols], ACT.Copy).then_inc(*hd_act.step(f"hi{n}"))

        def weights(g):
            act.wait_ge(hd_dve.sem, hd_dve.at("all3", g))
            a(sp_all_hi[:, :], sp[:, 0:SEQ], ACT.Copy).then_inc(*hd_act.step("all_hi"))
            act.wait_ge(hd_pe.sem, hd_pe.at("logs", g))
            for n, (bank, off, w) in enumerate(PARTS):
                a(a_f[:, off:off + w], psum[:, 4 + bank, 0:w], ACT.Exp).then_inc(*hd_act.step(f"a_part{n}"))
            act.wait_ge(hd_act.sem, hd_act.at("a_part2", g))
            a(a_hi[:, :], a_f[:, :], ACT.Copy).then_inc(*hd_act.step("a_hi"))

        def meta_softplus(p):
            act.wait_ge(mk_pe.sem, mk_pe.at("m_scores", p))
            a(m_f[:, :], psum[:, 7, :], ACT.Abs).then_inc(*mk_act.step("m_abs"))
            act.wait_ge(mk_act.sem, mk_act.at("m_abs", p))
            a(m_f[:, :], m_f[:, :], ACT.Exp, scale=-1.0).then_inc(*mk_act.step("m_exp"))
            act.wait_ge(mk_act.sem, mk_act.at("m_exp", p))
            a(m_f[:, :], m_f[:, :], ACT.Ln, bias=g_col("one", 0)).then_inc(*mk_act.step("m_ln"))
            act.wait_ge(mk_dve.sem, mk_dve.at("m_sp", p))
            a(m_hi[:, :], m_f[:, :], ACT.Copy).then_inc(*mk_act.step("m_hi"))

        def meta_weights(p):
            act.wait_ge(mk_pe.sem, mk_pe.at("m_rows", p))
            a(m_f[:, :], psum[:, 7, :], ACT.Exp).then_inc(*mk_act.step("am_exp"))
            act.wait_ge(mk_act.sem, mk_act.at("am_exp", p))
            a(m_hi[:, :], m_f[:, :], ACT.Copy).then_inc(*mk_act.step("am_hi"))

        def key_hi(t, at, s, p):
            strips(at, s)
            a(K_hi[:, t, :], psum[:, at.bank(s), :], ACT.Copy).then_inc(*qk_act.step("K_hi"))
            act.wait_ge(qk_dve.sem, qk_dve.at("KM", p))
            a(KM_hi[:, :], KM[:, :], ACT.Copy).then_inc(*qk_act.step("KM_hi"))

        def query_hi(t, at, s):
            strips(at, s)
            a(Q_hi[:, t, :], psum[:, at.bank(s), :], ACT.Copy, scale=SB_DH ** -0.5).then_inc(*qk_act.step("Q_hi"))

        def value_hi(at, half):
            strips(at, half)
            a(V_hi[:, 4 * half:4 * half + 4, 0:3:2, :],
              psum[:, at.bank(half), :].rearrange("p (a r c) -> p a r c", r=2, c=SB_DH), ACT.Copy)\
                .then_inc(*v_act.step(f"V_hi{half}"))
            if half == 0:
                act.wait_ge(strip_free, at.strip(0) + 1)
                a(VM_hi[:, :, :], VM[:, :, :], ACT.Copy).then_inc(*v_act.step("VM_hi"))

        def y_hi(t, p):
            act.wait_ge(y_out, p + 1)
            a(Y_hi[:, t, :], Y[:, :], ACT.Copy).then_inc(y_hi_ready, 1)

        def quad_body(at, i, has_d, has_next):
            g, p = 4 * i, 2 * i
            nj, ns = (3, 12) if has_d else (2, 4)
            softplus(g)
            meta_softplus(p)
            if has_d:
                y_hi(1, p - 1)
            value_hi(at, 0)
            weights(g)
            value_hi(at, 1)
            split_hi(at, 0)
            softplus(g + 1)
            key_hi(1, at, 2, p + 1)
            weights(g + 1)
            query_hi(1, at, 3)
            meta_weights(p)
            softplus(g + 2)
            split_hi(at, 1)
            meta_softplus(p + 1)
            weights(g + 2)
            if has_d:
                strips(at, 11)
                split_hi(at, 2)
            y_hi(0, p)
            softplus(g + 3)
            if has_next:
                key_hi(0, at, ns, p + 2)
            weights(g + 3)
            if has_next:
                query_hi(0, at, ns + 1)
            meta_weights(p + 1)
            if has_next:
                split_hi(at, nj)

        at = Place("quad_start")
        act.wait_ge(x_lo_ready, DT)
        for n, x in enumerate((X_hi, X_lo)):
            a(XM2[:, :, n, :], as_f32(x[:, :, 0:META]), ACT.Copy).then_inc(quad_ready, 1)
        act.wait_ge(ones_ready, 1)
        for x in (V_hi, V_lo):
            a(x[:, :, 1, :], ones[:, 0:SB_DH].unsqueeze(1).broadcast_to([P, 2 * BLOCKS, SB_DH]), ACT.Copy,
              scale=0.0).then_inc(quad_ready, 1)
        for x, y in ((XM_hi, X_hi), (XM_lo, X_lo)):
            a(x[:, :, :].rearrange("p k (j m) -> p k j m", j=4),
              as_f32(y[:, :, 0:32]).unsqueeze(2).broadcast_to([P, DT, 4, 32]), ACT.Copy).then_inc(quad_ready, 1)
        first_hi(1)
        key_hi(0, at, 0, 0)
        query_hi(0, at, 1)
        split_hi(at, 0)
        quad_body(Place("quad_first"), 0, False, True)
        with act.Fori(1, QUADS - 1) as i:
            quad_body(Place("quads", i, 4, 14, first=1), i, True, True)
        quad_body(Place("quad_last"), QUADS - 1, True, False)
        y_hi(1, 2 * QUADS - 1)
        at = Place("quad_end")
        strips(at, 7)
        split_hi(at, 0)

        def gates(phase):
            use("sigmoid")
            act.wait_ge(strip_free, START[phase][1])

            def body(i):
                at = Place(phase, i, 2, 4)
                for j in range(2):
                    for c in range(2):
                        strips(at, 2 * j + c)
                        if i or j:
                            act.wait_ge(gate_used, 4 * i + 2 * j + c - 1)
                        a(sig[:, c, 0:SEQ], strip_view(at.bank(2 * j + c), SEQ), ACT.Sigmoid).then_inc(strip_free, 1)
                    split_hi(at, j)
            loop(act, 2, body, 2)

        def turned_hi(x, hi, width, i):
            for t in range(2):
                act.wait_ge(t_dve.sem, t_dve.at(f"{x}_r{t + 1}", i))
                a(hi[:, t, :], turned[:, t, 0:width], ACT.Copy).then_inc(*t_act.step(f"R{x.upper()}_hi{t}"))

        def gate_hi(at, m):
            strips(at, 8 + m)
            a(gate[:, m, 0:SEQ], strip_view(at.bank(8 + m), SEQ), ACT.Sigmoid).then_inc(strip_free, 1)

        def head_body(at, i, has_next):
            for n in range(2):
                for half in range(2):
                    s = 2 * n + half
                    strips(at, s)
                    a(VZ_hi[:, 2 * half:2 * half + 2, 256 * n:256 * (n + 1)],
                      psum[:, at.bank(s), :].rearrange("p (b c) -> p b c", b=2), ACT.Copy)\
                        .then_inc(*r_act.step(f"V_hi{s}"))
                    if half == 0:
                        a(RVM_hi[:, 256 * n:256 * (n + 1)], psum[0:META, at.bank(s) + 1, 0:256], ACT.Copy)\
                            .then_inc(*r_act.step(f"VM_hi{n}"))
                split_hi(at, n)
            act.wait_ge(r_dve.sem, r_dve.at("S3", i))
            a(S_hi[:, :], S_f[:, :], ACT.Copy).then_inc(*r_act.step("S_hi"))
            act.wait_ge(r_dve.sem, r_dve.at("SM", i))
            a(SM_hi[:, :], SM_f[:, :], ACT.Copy).then_inc(*r_act.step("SM_hi"))
            use("sigmoid")
            for n in range(2):
                for c in range(2):
                    e = 2 * n + c
                    strips(at, 4 + e)
                    a(silu_g[:, e, :], strip_view(at.bank(4 + e), SEQ), ACT.Sigmoid)\
                        .then_inc(*r_act.step(f"g_sig{e}"))
                split_hi(at, 2 + n)
            if has_next:
                use("ln, exp")
            else:
                act.wait_ge(strip_free, at.strip(8))
                gate_hi(at, 0)
            squares = [S_f[:, 0:SEQ], S_f[:, SEQ:2 * SEQ], sig[:, 0, 0:SEQ], sig[:, 1, 0:SEQ]]
            for e in range(4):
                act.wait_ge(r_dve.sem, r_dve.at(f"yc{e}", i))
                if e == 0:
                    act.wait_ge(r_pe.sem, r_pe.at("mean", i))
                a(squares[e], RY[:, e, :], ACT.Square).then_inc(*r_act.step(f"y_sq{e}"))
            if has_next:
                turned_hi("q", RQ_hi, SEQ, i + 1)
                split_hi(at, 4)
            else:
                gate_hi(at, 1)
                split_hi(at, 4)
                gate_hi(at, 2)
                use("ln, exp")
            act.wait_ge(r_pe.sem, r_pe.at("var", i))
            a(r_std[:, :], psum[:, 5, :], ACT.Ln, scale=1.0 / RET_DV, bias=g_col("gn_eps", 0))\
                .then_inc(*r_act.step("ln"))
            act.wait_ge(r_act.sem, r_act.at("ln", i))
            a(r_std[:, :], r_std[:, :], ACT.Exp, scale=-0.5).then_inc(*r_act.step("std"))
            for e in range(4):
                act.wait_ge(r_dve.sem, r_dve.at(f"z{e}", i))
                a(VZ_hi[:, e, :], RY[:, e, :], ACT.Copy).then_inc(*r_act.step(f"z_hi{e}"))
            if not has_next:
                use("sigmoid")
                for m in range(3, DT):
                    gate_hi(at, m)
                    if m % 2:
                        split_hi(at, 4 + m // 2)
            if has_next:
                turned_hi("k", RK_hi, FULL, i + 1)
                split_hi(at, 5)
                for n in range(2):
                    strips(at, 12 + 4 * n + 3)
                    split_hi(at, 6 + n)

        at = Place("head0")
        turned_hi("q", RQ_hi, SEQ, 0)
        split_hi(at, 0)
        turned_hi("k", RK_hi, FULL, 0)
        split_hi(at, 1)
        gates("gate_b")
        loop(act, RET_HEADS - 1, lambda i: head_body(Place("heads", i, 8, 20), i, True))
        head_body(Place("head_last"), RET_HEADS - 1, False)
        at = Place("head_out")
        for k in range(DT):
            act.wait_ge(mixed, k + 1)
            a(X_hi[:, k, META:FULL], acc[:, k, :], ACT.Copy).then_inc(m_split_hi, 1)
            if k % 4 == 3:
                split_hi(at, k // 4)

        def product_norm(phase, n):
            at = Place(phase)

            def ready(k):
                if k % 2:
                    strips(at, k)
                    split_hi(at, k // 2)
                act.wait_ge(strip_free, at.strip(k) + 1)

            norm(n, squares(n, lambda k: acc[:, k, :], SEQ, ready), SEQ)

        product_norm("w_out", 1)
        norm(2, squares(2, lambda k: h[:, k, META:FULL], SEQ, lambda k: act.wait_ge(post_done, k + 1)), SEQ, 1)

        def ffn(tag, n):
            def gate_up(at, j, s, i):
                for c in range(2):
                    strips(at, s + c)
                    if c == 0:
                        act.wait_ge(f_dve.sem, f_dve.at("M_lo", i - 1)) if not (type(i) is int and i == 0) else None
                    a(silu_a[:, c, :], strip_view(at.bank(s + c), SEQ), ACT.Sigmoid)\
                        .then_inc(*f_act.step(f"sig{c}"))
                split_hi(at, j)
                strips(at, s + 3)
                split_hi(at, j + 1)
                act.wait_ge(f_dve.sem, f_dve.at("prod", i))
            def hidden(i, slot):
                a(M_hi[:, slot, :, :], silu_a[:, :, :], ACT.Copy).then_inc(*f_act.step("M_hi"))

            def two(at, i0, final):
                for m in range(2):
                    gate_up(at, 3 * m, 12 * m, i0 + m + 1)
                    hidden(i0 + m + 1, (m + 1) % 2)
                    strips(at, 12 * m + 11)
                    if not (final and m == 1):
                        split_hi(at, 3 * m + 2)
            base = FF_PAIRS * n
            use("sigmoid")
            gate_up(Place("ffn0" + tag, depth=4), 0, 0, base)
            hidden(base, 0)
            rounds = 5 if n == 0 else 4
            loop(act, rounds, lambda i: two(Place("ffn" + tag, i, 6, 24, 4), base + 2 * i, False))
            if n:
                two(Place("ffn_last" + tag, depth=4), base + 2 * rounds, True)

            def ready(k):
                at = Place("ffn_end" + tag, depth=4)
                if n == 0 and k == DT - 1:
                    strips(at, k)
                    split_hi(at, 0)
                act.wait_ge(strip_free, at.strip(k) + 1)
            m = 4 * n + 3
            norm(m, squares(m, lambda k: acc[:, k, :], SEQ, ready), SEQ)

        ffn("", 0)
        norm(4, squares(4, lambda k: h[:, k, :], FULL, lambda k: act.wait_ge(post_done, DT + k + 1)), FULL, 2)

        use("sigmoid")
        act.wait_ge(strip_free, START["conv_b"][1])
        at = Place("conv_b")

        def take(at, s, n, f, dst, free=None):
            for c in range(2):
                strips(at, s + c)
                if free:
                    act.wait_ge(*free)
                if n == FULL:
                    a(wide(dst[:, c, :]), strip_view(at.bank(s + c), FULL), f).then_inc(strip_free, 1)
                else:
                    a(dst[:, c, :], strip_view(at.bank(s + c), SEQ), f).then_inc(strip_free, 1)

        for half in range(2):
            take(at, 4 * half, FULL, ACT.Sigmoid, conv_sig, (c_dve.sem, c_dve.at("glu1")) if half else None)
            split_hi(at, 2 * half)
            take(at, 4 * half + 2, FULL, ACT.Copy, glu_val, (c_dve.sem, c_dve.at("glu1")) if half else None)
            split_hi(at, 2 * half + 1)
        at = Place("conv_a")
        for half in range(2):
            for j, (dst, n, free) in enumerate(((c_in, FULL, (y2_ready, 2)), (u_in, FULL, (y2_ready, 2)), (b_in, SEQ, (y2_ready, 2)))):
                take(at, 6 * half + 2 * j, n, ACT.Copy, dst, free if half else None)
                if j < 2:
                    split_hi(at, 3 * half + j)
            for t in (2 * half, 2 * half + 1):
                act.wait_ge(c_dve.sem, c_dve.at(f"ya{t}"))
                a(y2_hi[:, t, :], c_in[:, t % 2, 0:SEQ], ACT.Copy).then_inc(*c_act.step(f"y_hi{t}"))
            split_hi(at, 3 * half + 2)
        at = Place("w_out2_a")
        for j in range(2):
            for m in range(4 * j, 4 * j + 4):
                strips(at, m)
                a(acc[:, m, :], strip_view(at.bank(m), SEQ), ACT.Copy).then_inc(strip_free, 1)
            split_hi(at, j)
        use("ln, exp")
        for t in range(CT):
            act.wait_ge(c_dve.sem, c_dve.at(f"zc{t}"))
            if t >= 2:
                act.wait_ge(c_pe.sem, c_pe.at(f"var{t - 2}"))
            a(sq[:, t % 2, 0:SEQ], z[:, t, :], ACT.Square).then_inc(*c_act.step(f"zsq{t}"))
        act.wait_ge(c_pe.sem, c_pe.at(f"var{CT - 1}"))
        a(std[:, 0:SEQ], psum[:, 5, :], ACT.Ln, scale=1.0 / WB, bias=g_col("ln_eps", 0)).then_inc(*c_act.step("ln"))
        act.wait_ge(c_act.sem, c_act.at("ln"))
        a(std[:, 0:SEQ], std[:, 0:SEQ], ACT.Exp, scale=-0.5).then_inc(*c_act.step("std"))
        use("sigmoid")

        def z_hi(t):
            act.wait_ge(c_dve.sem, c_dve.at(f"yb{t}"))
            a(y2_hi[:, CT + t, :], z[:, t, :], ACT.Copy).then_inc(*c_act.step(f"zhi{t}"))
        for t in range(CT):
            act.wait_ge(c_dve.sem, c_dve.at(f"zn{t}"))
            if t >= 2:
                act.wait_ge(c_dve.sem, c_dve.at(f"yb{t - 2}"))
            for name, f, dst in (("sig", ACT.Sigmoid, normed), ("lin", ACT.Identity, conv_sig)):
                a(dst[:, t % 2, 0:SEQ], z[:, t, :], f, scale=g_col("ln_gain", t), bias=g_col("ln_bias", t))\
                    .then_inc(*c_act.step(f"{name}{t}"))
            if t:
                z_hi(t - 1)
        z_hi(CT - 1)

        def ready(k):
            at = Place("w_out2_b")
            if k % 4 == 0:
                strips(at, k + 3)
                split_hi(at, k // 4)
            act.wait_ge(strip_free, at.strip(k) + 1)
        norm(5, squares(5, lambda k: acc[:, k, :], SEQ, ready), SEQ)
        norm(6, squares(6, lambda k: h[:, k, META:FULL], SEQ, lambda k: act.wait_ge(post_done, 2 * DT + k + 1)), SEQ, 3)
        ffn("_2", 1)

    @block.vector
    def _(dve):
        v = nc.vector

        def split_lo(at, j):
            dve.wait_ge(w_hi_ready, at.unit(j) + 3)
            v.tensor_tensor(w_lo[at.ring(j)][:, :], w_raw[at.ring(j)][:, :], as_f32(w_hi[at.ring(j)][:, :]),
                            ALU.subtract).then_inc(w_lo_ready, 1)

        def strips(at, s, n=1):
            dve.wait_ge(strip_done, at.strip(s) + n)

        def stt(out_, in0, scalar, in1, op0, op1):
            return v.scalar_tensor_tensor(out=out_, in0=in0, scalar=scalar, in1=in1, op0=op0, op1=op1)

        def norm_split(n, s, width, gain):
            dve.wait_ge(std_ready, 2 * n + 2)
            cols = slice(0, FULL) if width == FULL else slice(META, FULL)

            def lo(k):
                dve.wait_ge(x_hi_ready, DT * s + k + 1)
                v.tensor_tensor(X_lo[:, k, cols], normed[:, k % 2, 0:width], as_f32(X_hi[:, k, cols]),
                                ALU.subtract).then_inc(x_lo_ready, 1)
            for k in range(DT):
                if k >= 2:
                    dve.wait_ge(x_lo_ready, DT * s + k - 1)
                stt(normed[:, k % 2, 0:width], h[:, k, cols], g_col(gain, k), std[:, 0:width],
                    ALU.mult, ALU.mult).then_inc(norm_scaled, 1)
                if k == 1 and n == 0:
                    first_lo(0)
                if k:
                    lo(k - 1)
            lo(DT - 1)

        def norm_add(n, p, gain):
            dve.wait_ge(std_ready, 2 * n + 2)
            for k in range(DT):
                stt(normed[:, k % 2, 0:SEQ], acc[:, k, :], g_col(gain, k), std[:, 0:SEQ],
                    ALU.mult, ALU.mult).then_inc(norm_scaled, 1)
                dve.wait_ge(norm_scaled, DT * n + k + 1)
                v.tensor_tensor(h[:, k, META:FULL], h[:, k, META:FULL], normed[:, k % 2, 0:SEQ], ALU.add)\
                    .then_inc(post_done, 1)

        def first_lo(u):
            dve.wait_ge(w_hi_ready, u + 1)
            v.tensor_tensor(w_lo[u][:, :], w_raw[u][:, :], as_f32(w_hi[u][:, :]), ALU.subtract)\
                .then_inc(w_lo_ready, 1)

        dve.wait_ge(vec_in, 16)
        for n in range(4):
            dve.wait_ge(x_in[n], 16)
        norm_split(0, 0, FULL, "pre_mix")
        first_lo(1)
        dve.wait_ge(consts_in, 16 * 3)

        def softplus(g, first=None, then=None):
            if first:
                first()
            for n in (1, 2, 0):
                bank, off, w = PARTS[n]
                if n != 2:
                    dve.wait_ge(hd_act.sem, hd_act.at(f"ln{n}", g))
                stt(sp[:, off:off + w], psum[:, 4 + bank, 0:w], 0.0, sp[:, off:off + w], ALU.max, ALU.add)\
                    .then_inc(*hd_dve.step(f"sp{n}"))
            for n, cols in ((1, slice(SEQ, PACKED)), (0, slice(0, SEQ))):
                dve.wait_ge(hd_act.sem, hd_act.at(f"hi{n}", g))
                v.tensor_tensor(sp_lo[:, cols], sp[:, cols], as_f32(sp_hi[:, cols]), ALU.subtract)\
                    .then_inc(*hd_dve.step(f"sp_lo{n}"))
            if then:
                then()
            for b in range(1, BLOCKS):
                dve.wait_ge(hd_dve.sem, hd_dve.at(f"all{b - 1}" if b > 1 else "sp_lo0", g))
                v.tensor_tensor(sp[:, b * P:SEQ], sp[:, b * P:SEQ], sp[:, KEY_OFF[b]:KEY_OFF[b] + KEY_LEN[b]],
                                ALU.add).then_inc(*hd_dve.step(f"all{b}"))

        def weights(g):
            dve.wait_ge(hd_act.sem, hd_act.at("all_hi", g))
            v.tensor_tensor(sp_all_lo[:, :], sp[:, 0:SEQ], as_f32(sp_all_hi[:, :]), ALU.subtract)\
                .then_inc(*hd_dve.step("all_lo"))
            dve.wait_ge(hd_act.sem, hd_act.at("a_hi", g))
            v.tensor_tensor(a_lo[:, :], a_f[:, :], as_f32(a_hi[:, :]), ALU.subtract)\
                .then_inc(*hd_dve.step("a_lo"))

        def meta_softplus(p):
            dve.wait_ge(mk_act.sem, mk_act.at("m_ln", p))
            stt(m_f[:, :], psum[:, 7, :], 0.0, m_f[:, :], ALU.max, ALU.add).then_inc(*mk_dve.step("m_sp"))
            dve.wait_ge(mk_act.sem, mk_act.at("m_hi", p))
            v.tensor_tensor(m_lo[:, :], m_f[:, :], as_f32(m_hi[:, :]), ALU.subtract).then_inc(*mk_dve.step("m_lo"))

        def meta_weights(p):
            dve.wait_ge(mk_act.sem, mk_act.at("am_hi", p))
            v.tensor_tensor(m_lo[:, :], m_f[:, :], as_f32(m_hi[:, :]), ALU.subtract).then_inc(*mk_dve.step("am_lo"))

        def y_take(p):
            dve.wait_ge(mk_pe.sem, mk_pe.at("y_meta", p))
            if not (type(p) is int and p == 0):
                dve.wait_ge(y_lo_ready, p)
            v.tensor_copy(Y[:, :], psum[:, 3, :]).then_inc(y_out, 1)

        def y_lo(t, p):
            dve.wait_ge(y_hi_ready, p + 1)
            v.tensor_tensor(Y_lo[:, t, :], Y[:, :], as_f32(Y_hi[:, t, :]), ALU.subtract).then_inc(y_lo_ready, 1)

        def key_lo(t, at, s, p):
            dve.wait_ge(qk_act.sem, qk_act.at("K_hi", p))
            v.tensor_tensor(K_lo[:, t, :], psum[:, at.bank(s), :], as_f32(K_hi[:, t, :]), ALU.subtract)\
                .then_inc(*qk_dve.step("K_lo"))
            KM_rows = KM[:, 0:64].rearrange("p (r m) -> p r m", r=2)[:, :, 0:META]
            part = [psum[:, at.bank(s) + 1, n * META:(n + 1) * META].unsqueeze(1).broadcast_to([P, 2, META])
                    for n in range(2)]
            mask = mask_k[:, :, :]
            v.tensor_tensor(KM_rows, part[0], mask, ALU.mult).then_inc(*qk_dve.step("KM_part"))
            dve.wait_ge(qk_dve.sem, qk_dve.at("KM_part", p))
            v.tensor_tensor(KM_x[:, :, :], part[1], mask, ALU.mult).then_inc(strip_free, 1)
            dve.wait_ge(strip_free, at.strip(s) + 1)
            v.tensor_tensor(KM_rows, KM_rows, KM_x[:, :, :], ALU.add).then_inc(*qk_dve.step("KM"))
            dve.wait_ge(qk_act.sem, qk_act.at("KM_hi", p))
            v.tensor_tensor(KM_lo[:, :], KM[:, :], as_f32(KM_hi[:, :]), ALU.subtract).then_inc(*qk_dve.step("KM_lo"))

        def query_lo(t, at, s, p):
            dve.wait_ge(qk_act.sem, qk_act.at("Q_hi", p))
            stt(Q_lo[:, t, :], psum[:, at.bank(s), :], SB_DH ** -0.5, as_f32(Q_hi[:, t, :]), ALU.mult, ALU.subtract)\
                .then_inc(strip_free, 1)

        def value_lo(at, half, i):
            dve.wait_ge(v_act.sem, v_act.at(f"V_hi{half}", i))
            blocks = (slice(None), slice(4 * half, 4 * half + 4), slice(0, 3, 2), slice(None))
            ins = v.tensor_tensor(V_lo[blocks],
                                  psum[:, at.bank(half), :].rearrange("p (a r c) -> p a r c", r=2, c=SB_DH),
                                  as_f32(V_hi[blocks]), ALU.subtract)
            if half:
                ins.then_inc(strip_free, 1)
                return
            ins.then_inc(*v_dve.step("V_lo0"))
            v.tensor_tensor(VM[:, :, :], psum[:, at.bank(0) + 1, 0:2 * P].rearrange("p (t c) -> p t c", t=2),
                            mask_v[:, :].unsqueeze(1).broadcast_to([P, 2, P]), ALU.mult).then_inc(strip_free, 1)
            dve.wait_ge(v_act.sem, v_act.at("VM_hi", i))
            v.tensor_tensor(VM_lo[:, :, :], VM[:, :, :], as_f32(VM_hi[:, :, :]), ALU.subtract)\
                .then_inc(*v_dve.step("VM_lo"))

        def add_up(dst, at, s, ms):
            for n, m in enumerate(ms):
                strips(at, s + n)
                v.tensor_tensor(dst[:, m, :], dst[:, m, :], strip_view(at.bank(s + n), SEQ), ALU.add)\
                    .then_inc(strip_free, 1)

        def quad_body(at, i, has_d, has_next):
            g, p = 4 * i, 2 * i
            nj, ns = (3, 12) if has_d else (2, 4)
            softplus(g)
            meta_softplus(p)
            if has_d:
                y_lo(1, p - 1)
            value_lo(at, 0, i)
            weights(g)
            value_lo(at, 1, i)
            split_lo(at, 0)
            softplus(g + 1)
            key_lo(1, at, 2, p + 1)
            weights(g + 1)
            query_lo(1, at, 3, p + 1)
            meta_weights(p)
            y_take(p)
            softplus(g + 2, has_d and (lambda: add_up(acc, at, 4, range(2))),
                     has_d and (lambda: add_up(acc, at, 6, range(2, 4))))
            meta_softplus(p + 1)
            if has_d:
                add_up(acc, at, 8, range(4, 6))
            split_lo(at, 1)
            weights(g + 2)
            if has_d:
                add_up(acc, at, 10, range(6, 8))
                split_lo(at, 2)
            y_lo(0, p)
            softplus(g + 3)
            if has_next:
                key_lo(0, at, ns, p + 2)
            weights(g + 3)
            if has_next:
                query_lo(0, at, ns + 1, p + 2)
            meta_weights(p + 1)
            y_take(p + 1)
            if has_next:
                split_lo(at, nj)

        dve.wait_ge(memset_done, 1)
        dve.wait_ge(quad_ready, 4)
        at = Place("quad_start")
        key_lo(0, at, 0, 0)
        query_lo(0, at, 1, 0)
        split_lo(at, 0)
        quad_body(Place("quad_first"), 0, False, True)
        dve.wait_ge(memset_done, 2)
        with dve.Fori(1, QUADS - 1) as i:
            quad_body(Place("quads", i, 4, 14, first=1), i, True, True)
        quad_body(Place("quad_last"), QUADS - 1, True, False)
        y_lo(1, 2 * QUADS - 1)
        at = Place("quad_end")
        add_up(acc, at, 0, range(8))
        split_lo(at, 0)

        def gates(phase, use_gate):
            for j in range(4):
                at = Place(phase)
                for c in range(2):
                    m = 2 * j + c
                    dve.wait_ge(strip_free, at.strip(m) + 1)
                    use_gate(m, sig[:, c, 0:SEQ])
                split_lo(at, j)


        def first_tile(x, s, width, at):
            fold = wide if width == FULL else (lambda ap: ap)
            cos, sin = (fold(rot[:, n, FULL - width:]) for n in range(2))
            strips(at, s)
            v.tensor_tensor(fold(turned[:, 0, 0:width]), strip_view(at.bank(s), width), cos, ALU.mult)\
                .then_inc(*t_dve.step(f"{x}_cos"))
            v.tensor_tensor(fold(turned[:, 1, 0:width]), strip_view(at.bank(s), width), sin, ALU.mult)\
                .then_inc(strip_free, 1)

        def second_tile(x, s, width, at, i, hi, lo):
            fold = wide if width == FULL else (lambda ap: ap)
            cos, sin = (fold(rot[:, n, FULL - width:]) for n in range(2))
            spare = [sig[:, n, 0:width] for n in range(2)]
            strips(at, s)
            v.tensor_tensor(fold(spare[0]), strip_view(at.bank(s), width), sin, ALU.mult)\
                .then_inc(*t_dve.step(f"{x}_sin"))
            v.tensor_tensor(fold(spare[1]), strip_view(at.bank(s), width), cos, ALU.mult).then_inc(strip_free, 1)
            dve.wait_ge(t_dve.sem, t_dve.at(f"{x}_sin", i))
            v.tensor_tensor(turned[:, 0, 0:width], turned[:, 0, 0:width], spare[0], ALU.subtract)\
                .then_inc(*t_dve.step(f"{x}_r1"))
            dve.wait_ge(strip_free, at.strip(s) + 1)
            v.tensor_tensor(turned[:, 1, 0:width], turned[:, 1, 0:width], spare[1], ALU.add)\
                .then_inc(*t_dve.step(f"{x}_r2"))
            dve.wait_ge(t_act.sem, t_act.at(f"R{x.upper()}_hi1", i))
            v.tensor_tensor(lo[:, :, :], turned[:, :, 0:width], as_f32(hi[:, :, :]), ALU.subtract)\
                .then_inc(*t_dve.step(f"{x}_lo"))

        def head_body(at, i, has_next):
            dve.wait_ge(r_pe.sem, r_pe.at("scores", i))
            dve.wait_ge(decay_loaded, 16 * (i + 1))
            for n in range(2):
                for half in range(2):
                    s = 2 * n + half
                    dve.wait_ge(r_act.sem, r_act.at(f"V_hi{s}", i))
                    blocks = (slice(None), slice(2 * half, 2 * half + 2), slice(256 * n, 256 * (n + 1)))
                    ins = v.tensor_tensor(VZ_lo[blocks], psum[:, at.bank(s), :].rearrange("p (b c) -> p b c", b=2),
                                          as_f32(VZ_hi[blocks]), ALU.subtract)
                    if half:
                        ins.then_inc(strip_free, 1)
                    else:
                        ins.then_inc(*r_dve.step(f"V_lo{s}"))
                        dve.wait_ge(r_act.sem, r_act.at(f"VM_hi{n}", i))
                        v.tensor_tensor(RVM_lo[:, 256 * n:256 * (n + 1)], psum[0:META, at.bank(s) + 1, 0:256],
                                        as_f32(RVM_hi[:, 256 * n:256 * (n + 1)]), ALU.subtract)\
                            .then_inc(strip_free, 1)
                split_lo(at, n)
            for b in range(BLOCKS):
                v.tensor_tensor(S_f[:, KEY_OFF[b]:KEY_OFF[b] + KEY_LEN[b]],
                                psum[:, 4 + KEY_BANK[b], KEY_COL[b]:KEY_COL[b] + KEY_LEN[b]],
                                decay[:, 0, 0:KEY_LEN[b]], ALU.mult).then_inc(*r_dve.step(f"S{b}"))
            v.tensor_tensor(SM_f[:, :], psum[0:META, 7, :], decay[0:META, 1, :], ALU.mult)\
                .then_inc(*r_dve.step("SM"))
            dve.wait_ge(r_act.sem, r_act.at("S_hi", i))
            v.tensor_tensor(S_lo[:, :], S_f[:, :], as_f32(S_hi[:, :]), ALU.subtract).then_inc(*r_dve.step("S_lo"))
            dve.wait_ge(r_act.sem, r_act.at("SM_hi", i))
            v.tensor_tensor(SM_lo[:, :], SM_f[:, :], as_f32(SM_hi[:, :]), ALU.subtract)\
                .then_inc(*r_dve.step("SM_lo"))
            for e in range(4):
                dve.wait_ge(r_act.sem, r_act.at(f"g_sig{e}", i))
                v.tensor_tensor(silu_g[:, e, :], silu_g[:, e, :], strip_view(at.bank(4 + e), SEQ), ALU.mult)\
                    .then_inc(strip_free, 1)
                if e % 2:
                    split_lo(at, 2 + e // 2)
            dve.wait_ge(r_pe.sem, r_pe.at("y", i))
            for e in range(4):
                v.tensor_copy(RY[:, e, :], psum[:, 4 + e, :]).then_inc(*r_dve.step(f"y{e}"))
            for e in range(1, 4):
                dve.wait_ge(r_dve.sem, r_dve.at(f"y{e}" if e == 1 else f"ys{e - 1}", i))
                v.tensor_tensor(S_f[:, 0:SEQ], RY[:, 0, :] if e == 1 else S_f[:, 0:SEQ], RY[:, e, :],
                                ALU.add).then_inc(*r_dve.step(f"ys{e}"))
            dve.wait_ge(r_pe.sem, r_pe.at("mean", i))
            for e in range(4):
                stt(RY[:, e, :], psum[:, 4, :], -1.0 / RET_DV, RY[:, e, :], ALU.mult, ALU.add)\
                    .then_inc(*r_dve.step(f"yc{e}"))
            if has_next:
                first_tile("q", 8, SEQ, at)
            squares = [S_f[:, 0:SEQ], S_f[:, SEQ:2 * SEQ], sig[:, 0, 0:SEQ], sig[:, 1, 0:SEQ]]
            for e in range(1, 4):
                dve.wait_ge(r_act.sem, r_act.at(f"y_sq{e}", i))
                if e > 1:
                    dve.wait_ge(r_dve.sem, r_dve.at(f"sqs{e - 1}", i))
                v.tensor_tensor(squares[0], squares[0], squares[e], ALU.add).then_inc(*r_dve.step(f"sqs{e}"))
            v.tensor_tensor(RY[:, :, :], RY[:, :, :], silu_g[:, :, :], ALU.mult).then_inc(*r_dve.step("yg"))
            if has_next:
                dve.wait_ge(r_dve.sem, r_dve.at("sqs3", i))
                second_tile("q", 9, SEQ, at, i + 1, RQ_hi, RQ_lo)
                split_lo(at, 4)
                dve.wait_ge(t_dve.sem, t_dve.at("q_lo", i + 1))
                first_tile("k", 10, FULL, at)
            else:
                split_lo(at, 4)
            dve.wait_ge(r_act.sem, r_act.at("std", i))
            dve.wait_ge(r_dve.sem, r_dve.at("yg", i))

            def z_lo(e):
                dve.wait_ge(r_act.sem, r_act.at(f"z_hi{e}", i))
                v.tensor_tensor(VZ_lo[:, e, :], RY[:, e, :], as_f32(VZ_hi[:, e, :]), ALU.subtract)\
                    .then_inc(*r_dve.step(f"z_lo{e}"))
            for e in range(4):
                v.tensor_tensor(RY[:, e, :], RY[:, e, :], r_std[:, :], ALU.mult).then_inc(*r_dve.step(f"z{e}"))
                if e:
                    z_lo(e - 1)
            z_lo(3)
            if has_next:
                second_tile("k", 11, FULL, at, i + 1, RK_hi, RK_lo)
                split_lo(at, 5)
                for n in range(2):
                    add_up(ret, at.four(), 12 + 4 * n, range(4 * n, 4 * n + 4))
                    split_lo(at, 6 + n)
                dve.wait_ge(t_dve.sem, t_dve.at("k_lo", i + 1))
            else:
                for n in range(3):
                    ms = range(3 * n, min(3 * n + 3, DT))
                    for m in ms:
                        dve.wait_ge(strip_free, at.strip(8 + m) + 1)
                        v.tensor_tensor(ret[:, m, :], ret[:, m, :], gate[:, m, 0:SEQ], ALU.mult)\
                            .then_inc(gate_used, 1)
                    for m in ms:
                        dve.wait_ge(gate_used, DT + m + 1)
                        v.tensor_tensor(acc[:, m, :], acc[:, m, :], ret[:, m, :], ALU.add).then_inc(premixed, 1)
                    split_lo(at, 5 + n)

        at = Place("head0")
        dve.wait_ge(rot_in, 16)
        first_tile("q", 0, SEQ, at)
        second_tile("q", 1, SEQ, at, 0, RQ_hi, RQ_lo)
        split_lo(at, 0)
        dve.wait_ge(t_dve.sem, t_dve.at("q_lo", 0))
        first_tile("k", 2, FULL, at)
        second_tile("k", 3, FULL, at, 0, RK_hi, RK_lo)
        split_lo(at, 1)
        gates("gate_b", lambda m, gate: v.tensor_tensor(acc[:, m, :], acc[:, m, :], gate, ALU.mult)
              .then_inc(gate_used, 1))
        dve.wait_ge(ret_zero, 1)
        dve.wait_ge(gate_used, DT)
        loop(dve, RET_HEADS - 1, lambda i: head_body(Place("heads", i, 8, 20), i, True))
        head_body(Place("head_last"), RET_HEADS - 1, False)
        at = Place("head_out").four()

        def mixed_lo(m):
            dve.wait_ge(m_split_hi, m + 1)
            v.tensor_tensor(X_lo[:, m, META:FULL], acc[:, m, :], as_f32(X_hi[:, m, META:FULL]), ALU.subtract)\
                .then_inc(m_split_lo, 1)
        for m in range(DT):
            strips(at, m)
            dve.wait_ge(premixed, m + 1)
            v.tensor_tensor(ret[:, m, :], strip_view(at.bank(m), SEQ), gate[:, m, 0:SEQ], ALU.mult)\
                .then_inc(strip_free, 1)
            if m:
                mixed_lo(m - 1)
            dve.wait_ge(strip_free, at.strip(m) + 1)
            v.tensor_tensor(acc[:, m, :], acc[:, m, :], ret[:, m, :], ALU.add).then_inc(mixed, 1)
            if m % 4 == 3:
                split_lo(at, m // 4)
        mixed_lo(DT - 1)

        def out_product(phase):
            at = Place(phase).four()
            for m in range(DT):
                strips(at, m)
                v.tensor_copy(acc[:, m, :], strip_view(at.bank(m), SEQ)).then_inc(strip_free, 1)
                if m % 2:
                    split_lo(at, m // 2)

        out_product("w_out")
        dve.wait_ge(x_loaded, 32)
        norm_add(1, 0, "post_mix")
        norm_split(2, 1, SEQ, "pre_ffn")

        def ffn(tag, n):
            def gate_up(at, j, s, i):
                for c in range(2):
                    dve.wait_ge(f_act.sem, f_act.at(f"sig{c}", i))
                    v.tensor_tensor(silu_a[:, c, :], silu_a[:, c, :], strip_view(at.bank(s + c), SEQ), ALU.mult)\
                        .then_inc(strip_free, 1)
                split_lo(at, j)
                dve.wait_ge(strip_free, at.strip(s + 1) + 1)
                for c in range(2):
                    strips(at, s + 2 + c)
                    v.tensor_tensor(silu_a[:, c, :], silu_a[:, c, :], strip_view(at.bank(s + 2 + c), SEQ), ALU.mult)\
                        .then_inc(strip_free, 1)
                dve.wait_ge(strip_free, at.strip(s + 3) + 1)
                v.tensor_copy(silu_a[:, 0, 0:1], silu_a[:, 0, 0:1]).then_inc(*f_dve.step("prod"))

            def hidden_lo(i, slot):
                dve.wait_ge(f_act.sem, f_act.at("M_hi", i))
                v.tensor_tensor(M_lo[:, slot, :, :], silu_a[:, :, :], as_f32(M_hi[:, slot, :, :]), ALU.subtract)\
                    .then_inc(*f_dve.step("M_lo"))

            def two(at, i0, final):
                for m in range(2):
                    gate_up(at, 3 * m, 12 * m, i0 + m + 1)
                    add_up(acc, at, 12 * m + 4, range(3))
                    split_lo(at, 3 * m + 1)
                    hidden_lo(i0 + m + 1, (m + 1) % 2)
                    add_up(acc, at, 12 * m + 7, range(3, DT))
                    if not (final and m == 1):
                        split_lo(at, 3 * m + 2)
            base = FF_PAIRS * n
            at = Place("ffn0" + tag, depth=4)
            gate_up(at, 0, 0, base)
            split_lo(at, 1)
            hidden_lo(base, 0)
            dve.wait_ge(acc_zero, n + 1)
            rounds = 5 if n == 0 else 4
            loop(dve, rounds, lambda i: two(Place("ffn" + tag, i, 6, 24, 4), base + 2 * i, False))
            if n:
                two(Place("ffn_last" + tag, depth=4), base + 2 * rounds, True)
            at = Place("ffn_end" + tag, depth=4)
            add_up(acc, at, 0, range(DT))
            if n == 0:
                split_lo(at, 0)

        ffn("", 0)
        v.tensor_copy(h[:, :, 0:META], meta2_f[:, :, :]).then_inc(memset_done, 1)
        dve.wait_ge(memset_done, 3)
        norm_add(3, 1, "post_ffn")
        norm_split(4, 2, FULL, "pre_mix2")

        LEFT = TAPS_B - 1
        pad = LEFT - META
        v.memset(glu[:, :, 0:pad], 0.0).then_inc(*c_dve.step("pad"))
        steps = [0]

        def taps(n):
            for _ in range(n):
                q = steps[0]
                t, k = q // (2 * TAPS_B) * 2 + q % 2, q % (2 * TAPS_B) // 2
                shifted = glu[:, t, k:k + SEQ]
                w = g_col("conv_b_w", t * TAPS_B + k)
                if k == 0:
                    ins = v.tensor_scalar(z[:, t, :], shifted, w, g_col("conv_b_bias", t), ALU.mult, ALU.add)
                else:
                    dve.wait_ge(conv_step, q - 1)
                    ins = stt(z[:, t, :], shifted, w, z[:, t, :], ALU.mult, ALU.add)
                ins.then_inc(conv_step, 1)
                steps[0] += 1

        def gated_linear(half):
            at = Place("conv_b")
            dve.wait_ge(strip_free, at.strip(4 * half + 3) + 1)
            for c in range(2):
                v.tensor_tensor(glu[:, 2 * half + c, pad:], conv_sig[:, c, :], glu_val[:, c, :], ALU.mult)\
                    .then_inc(*c_dve.step(f"glu{2 * half + c}"))

        def short_conv(half):
            at, o = Place("conv_a"), 6 * half
            dve.wait_ge(strip_free, at.strip(o + 3) + 1)
            for c in range(2):
                v.tensor_tensor(u_in[:, c, :], c_in[:, c, :], u_in[:, c, :], ALU.mult)\
                    .then_inc(*c_dve.step(f"u{2 * half + c}"))
            for k in range(TAPS_A):
                for c in range(2):
                    w = g_col("conv_a_w", (2 * half + c) * TAPS_A + k)
                    shifted = u_in[:, c, META - (TAPS_A - 1) + k:META - (TAPS_A - 1) + k + SEQ]
                    name = ("2nd" if half else "") + f"ca{c}_{k}"
                    dve.wait_ge(c_dve.sem, c_dve.at(name) - 2)
                    if k == 0:
                        ins = v.tensor_scalar(c_in[:, c, 0:SEQ], shifted, w, None, ALU.mult)
                    else:
                        ins = stt(c_in[:, c, 0:SEQ], shifted, w, c_in[:, c, 0:SEQ], ALU.mult, ALU.add)
                    ins.then_inc(*c_dve.step(name))

        def y_a(half):
            at, o = Place("conv_a"), 6 * half
            dve.wait_ge(strip_free, at.strip(o + 5) + 1)
            for c in range(2):
                dve.wait_ge(c_dve.sem, c_dve.at(("2nd" if half else "") + f"ca{c}_{TAPS_A - 1}"))
                v.tensor_tensor(c_in[:, c, 0:SEQ], c_in[:, c, 0:SEQ], b_in[:, c, :], ALU.mult)\
                    .then_inc(*c_dve.step(f"ya{2 * half + c}"))

        def y_a_lo(half):
            for c in range(2):
                t = 2 * half + c
                dve.wait_ge(c_act.sem, c_act.at(f"y_hi{t}"))
                v.tensor_tensor(y2_lo[:, t, :], c_in[:, c, 0:SEQ], as_f32(y2_hi[:, t, :]), ALU.subtract)\
                    .then_inc(y2_ready, 1)

        b, ca = Place("conv_b"), Place("conv_a")
        split_lo(b, 0)
        split_lo(b, 1)
        gated_linear(0)
        dve.wait_ge(c_dve.sem, c_dve.at("glu1"))
        taps(11)
        split_lo(b, 2)
        taps(13)
        split_lo(b, 3)
        gated_linear(1)
        taps(11)
        split_lo(ca, 0)
        taps(13)
        split_lo(ca, 1)
        short_conv(0)
        taps(5)
        y_a(0)
        taps(3)
        y_a_lo(0)
        split_lo(ca, 2)
        taps(6)
        dve.wait_ge(c_dve.sem, c_dve.at("glu3"))
        split_lo(ca, 3)
        taps(13)
        split_lo(ca, 4)
        short_conv(1)
        taps(4)
        y_a(1)
        taps(1)
        y_a_lo(1)
        split_lo(ca, 5)
        taps(2 * 2 * TAPS_B - steps[0])
        dve.wait_ge(c_pe.sem, c_pe.at(f"mean{CT - 1}"))
        for t in range(CT):
            stt(z[:, t, :], psum[:, 4, :], -1.0 / WB, z[:, t, :], ALU.mult, ALU.add).then_inc(*c_dve.step(f"zc{t}"))
        for j in range(2):
            split_lo(Place("w_out2_a"), j)
        dve.wait_ge(c_act.sem, c_act.at("std"))
        for t in range(CT):
            v.tensor_tensor(z[:, t, :], z[:, t, :], std[:, 0:SEQ], ALU.mult).then_inc(*c_dve.step(f"zn{t}"))

        def z_lo(t):
            dve.wait_ge(c_act.sem, c_act.at(f"zhi{t}"))
            v.tensor_tensor(y2_lo[:, CT + t, :], z[:, t, :], as_f32(y2_hi[:, CT + t, :]), ALU.subtract)\
                .then_inc(y2_ready, 1)
        for t in range(CT):
            dve.wait_ge(c_act.sem, c_act.at(f"lin{t}"))
            v.tensor_tensor(z[:, t, :], conv_sig[:, t % 2, 0:SEQ], normed[:, t % 2, 0:SEQ], ALU.mult)\
                .then_inc(*c_dve.step(f"yb{t}"))
            if t:
                z_lo(t - 1)
        z_lo(CT - 1)
        at = Place("w_out2_b").four()
        dve.wait_ge(strip_free, at.strip(0))
        add_up(acc, at, 0, range(DT))
        for j in range(2):
            split_lo(at, j)
        norm_add(5, 2, "post_mix2")
        norm_split(6, 3, SEQ, "pre_ffn2")
        ffn("_2", 1)
        norm_add(7, 3, "post_ffn2")

    ctx.close()


def z_done(t):
    return 2 * TAPS_B * (t // 2) + 2 * TAPS_B - 1 + t % 2


C_IDENT, C_BLOCKED, C_TRI, C_ALL, C_TRI_META, C_ROWS = 0, 1, 2, 3, 4, 5
N_CMAT = 7
CONST = np.cumsum([0, 2 * META, P, 2 * FULL, N_CMAT * P]).tolist()

VEC, VEC_COLS = {}, 0
for _name, _n in (("norm_eps", 1), ("gn_eps", 1), ("ln_eps", 1), ("one", 1), ("pre_mix", 8), ("post_mix", 8),
                  ("pre_ffn", 8), ("post_ffn", 8), ("pre_mix2", 8), ("post_mix2", 8), ("pre_ffn2", 8),
                  ("post_ffn2", 8), ("conv_a_w", CT * TAPS_A), ("conv_b_w", CT * TAPS_B), ("conv_b_bias", CT),
                  ("ln_gain", CT), ("ln_bias", CT)):
    VEC[_name] = VEC_COLS
    VEC_COLS += _n


def constants():
    i = np.arange(P)
    ident = np.eye(P, dtype=np.float32)
    mask_k = np.zeros((P, 2, META), np.float32)
    mask_v = np.zeros((P, P), np.float32)
    for r in range(2):
        mask_k[SB_DH * r:SB_DH * (r + 1), r] = 1
        mask_v[32 * r:32 * r + META, SB_DH * r:SB_DH * (r + 1)] = 1
    half = RET_DK // 2
    inv = np.float32(10000.0) ** (-np.arange(half, dtype=np.float32) / np.float32(half))
    ang = (np.arange(FULL, dtype=np.float32)[None, :] * inv[:, None]).astype(np.float32)
    cos, sin = np.cos(ang), np.sin(ang)
    cm = np.zeros((P, N_CMAT, P), np.float32)
    cm[:, C_IDENT] = ident
    cm[:, C_BLOCKED] = np.where(i[:, None] < i[None, :], 0.0, BLOCKED)
    cm[:, C_TRI] = np.where(i[:, None] >= i[None, :], -1.0, 0.0)
    cm[:, C_ALL] = -1.0
    same = (i[:, None] // 32 == i[None, :] // 32) & (i[:, None] % 32 < META)
    cm[:, C_TRI_META] = np.where(same & (i[:, None] >= i[None, :]), -1.0, 0.0)
    for j in range(2):
        cm[:, C_ROWS + j] = np.where(i[None, :] // 32 == j, -1.0, 0.0)
    consts = np.concatenate([mask_k.reshape(P, -1), mask_v, cos, sin, cm.reshape(P, -1)], axis=1).astype(np.float32)
    log_g = np.log1p(-(2.0 ** (-5.0 - np.arange(RET_HEADS))))
    scale = RET_DK ** -0.5
    dec = np.zeros((RET_HEADS, P, 2, SEQ))
    u = np.arange(SEQ)
    for n in range(RET_HEADS):
        diff = u[None, :] - i[:, None]
        dec[n, :, 0] = np.where(diff >= 0, np.exp(log_g[n] * np.maximum(diff, 0)), 0.0) * scale
        dec[n, :META, 1] = np.exp(log_g[n] * (u[None, :] + META - i[:META, None])) * scale
    return consts, dec.reshape(RET_HEADS, P, 2 * SEQ).astype(np.float32)


def lay_out(inp):
    def P_unit(w, c):
        return w[:, c:c + 256].reshape(8, P, 256).transpose(1, 0, 2).reshape(P, UNIT)

    def R_unit(w, r, c):
        return w[r:r + 512, c:c + 512].reshape(4, P, 512).transpose(1, 0, 2).reshape(P, UNIT)

    def D_unit(w, r):
        return w[r:r + 256, :].reshape(2, P, 1024).transpose(1, 0, 2).reshape(P, UNIT)

    w_in, w_ret, w_sb, w_out = (inp[n][0] for n in ("w_in", "w_ret_out", "w_sb_out", "w_out"))
    w_fi, w_fo, w_in2, w_out2 = (inp[n][0] for n in ("w_ffn_in", "w_ffn_out", "w_in_2", "w_out_2"))
    w_g, w_u, w_d = (inp[n][0] for n in ("w_gate_2", "w_up_2", "w_down_2"))
    rq, rk, rv, rg, sq, sk, sv, ga, gb = np.cumsum([0, 1024, 1024, 2048, 2048, 1024, 1024, 1024, 1024])
    L = []

    def pair(t):
        return P_unit(np.concatenate([w_in[:, o + P * t:o + P * (t + 1)] for o in (sk, sq)], axis=1), 0)
    L.append(pair(0))
    for q in range(QUADS):
        L += [P_unit(w_in, sv + 256 * q), pair(2 * q + 1)]
        L += [D_unit(w_sb, 256 * (q - 1))] if q else []
        L += [pair(2 * q + 2)] if q < QUADS - 1 else []
    L.append(D_unit(w_sb, 256 * (QUADS - 1)))
    for n in range(RET_HEADS + 1):
        L += [P_unit(w_in, o + 256 * n) for o in (rq, rk)] if n < RET_HEADS else []
        if n in (0, RET_HEADS):
            L += [P_unit(w_in, (ga if n else gb) + 256 * k) for k in range(4)]
        if n:
            L += [R_unit(w_ret, 512 * (n - 1), c) for c in (0, 512)]
        if n < RET_HEADS:
            L += [P_unit(w_in, o + 512 * n + c) for o in (rv, rg) for c in (0, 256)]
    L += [P_unit(w_out, 256 * k) for k in range(4)]

    def ffn(g, go, u, uo, d):
        r = []
        for k in range(FF_PAIRS):
            r += [P_unit(g, go + 256 * k), P_unit(u, uo + 256 * k)]
            if k:
                r.append(D_unit(d, 256 * (k - 1)))
        return r + [D_unit(d, 256 * (FF_PAIRS - 1))]
    L += ffn(w_fi, 0, w_fi, D_FF, w_fo)
    for c in range(2):
        L += [P_unit(w_in2, 3 * WA + WB + 256 * c), P_unit(w_in2, 3 * WA + 256 * c)]
    for c in range(2):
        L += [P_unit(w_in2, o + 256 * c) for o in (WA, 2 * WA, 0)]
    L += [R_unit(w_out2, r, c) for r in (0, WA) for c in (0, 512)]
    L += ffn(w_g, 0, w_u, 0, w_d)
    assert len(L) == N_UNITS
    units = np.stack(L)

    def tiles(a):
        n = a.shape[0]
        return a.T.reshape(-1, P, n).transpose(1, 0, 2).reshape(P, -1)
    xfm = tiles(np.concatenate([inp["meta_tokens"], inp["x"][0]], axis=0))
    meta2 = tiles(inp["meta_tokens_2"])
    col = lambda a: a.reshape(-1, P).T
    const = lambda x: np.full((P, 1), x, np.float32)
    taps = lambda w: w.T.reshape(CT, P, -1).transpose(1, 0, 2).reshape(P, -1)
    vecs = np.concatenate(
        [const(NORM_EPS), const(GN_EPS), const(LN_EPS), const(1.0)]
        + [col(inp[n][0]) for n in ("norm_mix_pre", "norm_mix_post", "norm_ffn_pre", "norm_ffn_post",
                                    "pre_mix_norm_2", "post_mix_norm_2", "pre_ffn_norm_2", "post_ffn_norm_2")]
        + [taps(inp["conv_a_w_2"][0]), taps(inp["conv_b_w_2"][0])]
        + [col(inp[n][0]) for n in ("conv_b_bias_2", "ln_b_gain_2", "ln_b_bias_2")], axis=1)
    consts, dec = constants()
    return dict(units=units, xfm=xfm, meta2=meta2, consts=consts, dec=dec, vecs=vecs)


def kernel(**inputs):
    import concourse.bacc as _bacc
    from concourse.bass_utils import run_bass_kernel_spmd as _run

    laid = lay_out({k: np.asarray(x) for k, x in inputs.items()})
    nc = _bacc.Bacc("TRN2", target_bir_lowering=False, num_devices=1)
    arrays, args = {}, []
    for name, a in laid.items():
        a = np.ascontiguousarray(a)
        arrays[f"in_{name}"] = a
        args.append(nc.dram_tensor(f"in_{name}", a.shape, mybir.dt.from_np(a.dtype), kind="ExternalInput").ap())
    args.append(nc.dram_tensor("out_0", (P, DT * SEQ), F32, kind="ExternalOutput").ap())
    build(nc, *args)
    r = _run(nc, [arrays], core_ids=[0])
    o = np.asarray(r.results[0]["out_0"])
    return o.reshape(P, DT, SEQ).transpose(2, 1, 0).reshape(1, SEQ, D)
```
